# Optimizing a Trainium2 kernel written in Bass

```python
import math
import jax, jax.numpy as jnp
from jax import lax
import numpy as np

D_MODEL = 1024
BATCH = 1
SEQ = 512
DEPTH = 2

MIX_WIDTH = D_MODEL
MLA_WIDTH = D_MODEL // 2
SGU_WIDTH = D_MODEL // 4
POOL_WIDTH = D_MODEL // 4

MLA_HEADS = 4
V_HEAD = MLA_WIDTH // MLA_HEADS
QK_NOPE = 64
QK_ROPE = 32
QK_HEAD = QK_NOPE + QK_ROPE
Q_LORA = D_MODEL // 4
KV_LORA = D_MODEL // 8
ROPE_THETA = 10000.0
Q_BLOCK = 128

SGU_HEADS = 4
SGU_HEAD_DIM = SGU_WIDTH // SGU_HEADS
CHUNK = 128

POOL_WINDOWS = (2, 4, 8, 16)
POOL_GROUPS = len(POOL_WINDOWS)
POOL_GROUP_DIM = POOL_WIDTH // POOL_GROUPS

IN_WIDTH = Q_LORA + KV_LORA + QK_ROPE + 2 * SGU_WIDTH + POOL_WIDTH
FFN_HIDDEN = -(-8 * D_MODEL // (3 * 256)) * 256
EPS = 1e-6


def rms_norm(x, g):
    xf = x.astype(jnp.float32)
    y = xf * lax.rsqrt(jnp.mean(xf * xf, axis=-1, keepdims=True) + EPS)
    return (y * g.astype(jnp.float32)).astype(x.dtype)

def apply_rope(x, positions):
    half = x.shape[-1] // 2
    inv_freq = 1.0 / (ROPE_THETA ** (jnp.arange(half, dtype=jnp.float32) / half))
    ang = positions.astype(jnp.float32)[:, :, None, None] * inv_freq
    cos, sin = jnp.cos(ang), jnp.sin(ang)
    xf = x.astype(jnp.float32)
    x1, x2 = xf[..., :half], xf[..., half:]
    return jnp.concatenate([x1 * cos - x2 * sin, x2 * cos + x1 * sin], axis=-1).astype(x.dtype)

def mla_mixer(q_lat, kv_lat, k_rope, positions, g_q_lat, w_q_up, g_kv_lat, w_kv_up, g_q_head, g_k_head):
    B, S, _ = q_lat.shape
    q = (rms_norm(q_lat, g_q_lat) @ w_q_up).reshape(B, S, MLA_HEADS, QK_HEAD)
    kv = (rms_norm(kv_lat, g_kv_lat) @ w_kv_up).reshape(B, S, MLA_HEADS, QK_NOPE + V_HEAD)
    k_nope, v = kv[..., :QK_NOPE], kv[..., QK_NOPE:]
    k_pe = jnp.broadcast_to(k_rope[:, :, None, :], (B, S, MLA_HEADS, QK_ROPE))
    k = jnp.concatenate([k_nope, k_pe], axis=-1)
    q = rms_norm(q, g_q_head)
    k = rms_norm(k, g_k_head)
    q = jnp.concatenate([q[..., :QK_NOPE], apply_rope(q[..., QK_NOPE:], positions)], axis=-1)
    k = jnp.concatenate([k[..., :QK_NOPE], apply_rope(k[..., QK_NOPE:], positions)], axis=-1)

    n_blocks = S // Q_BLOCK
    scale = 1.0 / math.sqrt(QK_HEAD)
    qb = q.reshape(B, n_blocks, Q_BLOCK, MLA_HEADS, QK_HEAD).transpose(1, 0, 2, 3, 4)
    kpos = jnp.arange(S)

    def attend_block(args):
        qi, bi = args
        s = jnp.einsum('bqhd,bkhd->bhqk', qi, k).astype(jnp.float32) * scale
        qpos = bi * Q_BLOCK + jnp.arange(Q_BLOCK)
        causal = kpos[None, :] <= qpos[:, None]
        s = jnp.where(causal[None, None], s, jnp.finfo(jnp.float32).min)
        p = jax.nn.softmax(s, axis=-1)
        return jnp.einsum('bhqk,bkhd->bqhd', p.astype(v.dtype), v)

    o = lax.map(attend_block, (qb, jnp.arange(n_blocks)))
    return o.transpose(1, 0, 2, 3, 4).reshape(B, S, MLA_WIDTH)

def sgu_mixer(uv, g_v, w_spatial, b_spatial):
    B, S, _ = uv.shape
    u, v = uv[..., :SGU_WIDTH], uv[..., SGU_WIDTH:]
    v = rms_norm(v, g_v)
    vc = v.reshape(B, S // CHUNK, CHUNK, SGU_HEADS, SGU_HEAD_DIM)
    w = w_spatial * jnp.tril(jnp.ones((CHUNK, CHUNK), dtype=w_spatial.dtype))
    zc = jnp.einsum('hts,bcshd->bcthd', w, vc) + b_spatial.T[None, None, :, :, None]
    return u * zc.reshape(B, S, SGU_WIDTH)

def pool_mixer(p, w_pool, pool_scale):
    B, S, _ = p.shape
    pf = p.astype(jnp.float32).reshape(B, S, POOL_GROUPS, POOL_GROUP_DIM)
    t1 = jnp.arange(1, S + 1, dtype=jnp.float32)
    outs = []
    for g, win in enumerate(POOL_WINDOWS):
        xg = pf[:, :, g]
        cs = jnp.cumsum(xg, axis=1)
        cs_shift = jnp.pad(cs, ((0, 0), (win, 0), (0, 0)))[:, :S]
        count = jnp.minimum(t1, float(win))[None, :, None]
        outs.append((cs - cs_shift) / count - xg)
    m = jnp.stack(outs, axis=2).astype(p.dtype)
    y = jnp.einsum('bsgc,gcd->bsgd', m, w_pool).reshape(B, S, POOL_WIDTH)
    return y * pool_scale

def first_inputs(seed: int = 0) -> dict:
    key = jax.random.key(seed)
    ks = jax.random.split(key, 24)
    f32 = jnp.float32

    def dense(k, shape, fan_in):
        return jax.random.normal(k, shape, f32) * fan_in ** -0.5

    def gain(k, shape):
        return 1.0 + 0.01 * jax.random.normal(k, shape, f32)

    x = jax.random.normal(ks[0], (BATCH, SEQ, D_MODEL), f32)
    start = jax.random.randint(ks[1], (BATCH, 1), 0, 4096, dtype=jnp.int32)
    positions = start + jnp.arange(SEQ, dtype=jnp.int32)[None, :]
    return {
        "x": x,
        "positions": positions,
        "g_mix_norm": gain(ks[2], (DEPTH, D_MODEL)),
        "w_in": dense(ks[3], (DEPTH, D_MODEL, IN_WIDTH), D_MODEL),
        "g_q_lat": gain(ks[4], (DEPTH, Q_LORA)),
        "w_q_up": dense(ks[5], (DEPTH, Q_LORA, MLA_HEADS * QK_HEAD), Q_LORA),
        "g_kv_lat": gain(ks[6], (DEPTH, KV_LORA)),
        "w_kv_up": dense(ks[7], (DEPTH, KV_LORA, MLA_HEADS * (QK_NOPE + V_HEAD)), KV_LORA),
        "g_q_head": gain(ks[8], (DEPTH, QK_HEAD)),
        "g_k_head": gain(ks[9], (DEPTH, QK_HEAD)),
        "g_sgu_v": gain(ks[10], (DEPTH, SGU_WIDTH)),
        "w_spatial": dense(ks[11], (DEPTH, SGU_HEADS, CHUNK, CHUNK), CHUNK),
        "b_spatial": 1.0 + 0.01 * jax.random.normal(ks[12], (DEPTH, SGU_HEADS, CHUNK), f32),
        "w_pool": dense(ks[13], (DEPTH, POOL_GROUPS, POOL_GROUP_DIM, POOL_GROUP_DIM), POOL_GROUP_DIM),
        "pool_scale": 1.0 + 0.1 * jax.random.normal(ks[14], (DEPTH, POOL_WIDTH), f32),
        "g_out_mla": gain(ks[15], (DEPTH, MLA_WIDTH)),
        "g_out_sgu": gain(ks[16], (DEPTH, SGU_WIDTH)),
        "g_out_pool": gain(ks[17], (DEPTH, POOL_WIDTH)),
        "w_out": dense(ks[18], (DEPTH, MIX_WIDTH, D_MODEL), MIX_WIDTH),
        "g_ffn_norm": gain(ks[19], (DEPTH, D_MODEL)),
        "w_gate": dense(ks[20], (DEPTH, D_MODEL, FFN_HIDDEN), D_MODEL),
        "w_up": dense(ks[21], (DEPTH, D_MODEL, FFN_HIDDEN), D_MODEL),
        "w_down": dense(ks[22], (DEPTH, FFN_HIDDEN, D_MODEL), FFN_HIDDEN),
    }

def first_block(x, positions, g_mix_norm, w_in, g_q_lat, w_q_up, g_kv_lat, w_kv_up, g_q_head, g_k_head,
              g_sgu_v, w_spatial, b_spatial, w_pool, pool_scale, g_out_mla, g_out_sgu, g_out_pool,
              w_out, g_ffn_norm, w_gate, w_up, w_down):
    o1 = Q_LORA
    o2 = o1 + KV_LORA
    o3 = o2 + QK_ROPE
    o4 = o3 + 2 * SGU_WIDTH
    for l in range(DEPTH):
        h = rms_norm(x, g_mix_norm[l])
        z = h @ w_in[l]
        q_lat, kv_lat, k_rope = z[..., :o1], z[..., o1:o2], z[..., o2:o3]
        uv, pin = z[..., o3:o4], z[..., o4:]
        a = mla_mixer(q_lat, kv_lat, k_rope, positions, g_q_lat[l], w_q_up[l], g_kv_lat[l],
                      w_kv_up[l], g_q_head[l], g_k_head[l])
        gm = sgu_mixer(uv, g_sgu_v[l], w_spatial[l], b_spatial[l])
        po = pool_mixer(pin, w_pool[l], pool_scale[l])
        mix = jnp.concatenate([rms_norm(a, g_out_mla[l]), rms_norm(gm, g_out_sgu[l]),
                               rms_norm(po, g_out_pool[l])], axis=-1)
        x = x + mix @ w_out[l]
        h = rms_norm(x, g_ffn_norm[l])
        x = x + (jax.nn.silu(h @ w_gate[l]) * (h @ w_up[l])) @ w_down[l]
    return x


HG_HEADS = 4
HG_HEAD_DIM = 128
HG_DIM = HG_HEADS * HG_HEAD_DIM
GLA_HEADS = 4
GLA_DK = 64
GLA_DV = 128
GLA_KDIM = GLA_HEADS * GLA_DK
GLA_VDIM = GLA_HEADS * GLA_DV
GLA_RANK = 16
GLA_TAU = 16.0
LA_CHUNK = 64
NSA_HEADS = 8
NSA_KV_GROUPS = 2
NSA_REP = NSA_HEADS // NSA_KV_GROUPS
NSA_DH = 64
NSA_DIM = NSA_HEADS * NSA_DH
NSA_KV_DIM = NSA_KV_GROUPS * NSA_DH
CMP_STRIDE = 16
CMP_BLK = 2 * CMP_STRIDE
CMP_HID = 128
SLC_BLK = 64
N_SEL = 16
WIN = 512
ROPE_THETA_2 = 500000.0
ROT_DIM = NSA_DH // 4
N_BRANCH = 3
FF_DIM = ((8 * D_MODEL // 3 + 255) // 256) * 256

IN_SPLITS = (HG_DIM, HG_DIM, HG_DIM, HG_DIM,
             GLA_KDIM, GLA_KDIM, GLA_VDIM, GLA_RANK, GLA_VDIM,
             NSA_DIM, NSA_KV_DIM, NSA_KV_DIM, NSA_KV_DIM, NSA_KV_DIM, NSA_KV_DIM, NSA_KV_DIM,
             3 * NSA_HEADS,
             N_BRANCH * D_MODEL)
IN_COLS = sum(IN_SPLITS)


def rmsnorm(x, g):
    x32 = x.astype(jnp.float32)
    y = x32 * lax.rsqrt(jnp.mean(x32 * x32, axis=-1, keepdims=True) + EPS)
    return y.astype(x.dtype) * g

def split_cols(z):
    outs = []
    start = 0
    for n in IN_SPLITS:
        outs.append(z[..., start:start + n])
        start += n
    return outs

def heads(z, n):
    B, T, _ = z.shape
    return z.reshape(B, T, n, -1).transpose(0, 2, 1, 3)

def head_rmsnorm(o, g, dtype):
    B, H, T, dv = o.shape
    o = o.astype(jnp.float32).transpose(0, 2, 1, 3)
    o = o * lax.rsqrt(jnp.mean(o * o, axis=-1, keepdims=True) + EPS)
    return o.reshape(B, T, H * dv).astype(dtype) * g

def chunked_gated_linear_attention(q, k, v, log_g):
    B, H, T, dk = q.shape
    dv = v.shape[-1]
    n = T // LA_CHUNK

    def to_chunks(a):
        return jnp.moveaxis(a.astype(jnp.float32).reshape(B, H, n, LA_CHUNK, a.shape[-1]), 2, 0)

    causal = jnp.tril(jnp.ones((LA_CHUNK, LA_CHUNK), dtype=bool))[:, :, None]

    def step(state, inp):
        qc, kc, vc, gc = inp
        b = jnp.cumsum(gc, axis=2)
        o_inter = jnp.einsum('bhtd,bhdv->bhtv', qc * jnp.exp(b), state)
        decay = jnp.exp(jnp.where(causal, b[:, :, :, None, :] - b[:, :, None, :, :], -jnp.inf))
        scores = jnp.einsum('bhtd,bhtsd,bhsd->bhts', qc, decay, kc)
        o = o_inter + jnp.einsum('bhts,bhsv->bhtv', scores, vc)
        b_last = b[:, :, -1:, :]
        state = (jnp.exp(b_last[:, :, 0, :, None]) * state
                 + jnp.einsum('bhsd,bhsv->bhdv', kc * jnp.exp(b_last - b), vc))
        return state, o

    s0 = jnp.zeros((B, H, dk, dv), jnp.float32)
    _, o = lax.scan(step, s0, (to_chunks(q), to_chunks(k), to_chunks(v), to_chunks(log_g)))
    return jnp.moveaxis(o, 0, 2).reshape(B, H, T, dv)

def partial_rope(x, cos, sin):
    half = ROT_DIM // 2
    c = cos[None, :, None, :].astype(x.dtype)
    s = sin[None, :, None, :].astype(x.dtype)
    x1 = x[..., :half]
    x2 = x[..., half:ROT_DIM]
    return jnp.concatenate([x1 * c - x2 * s, x2 * c + x1 * s, x[..., ROT_DIM:]], axis=-1)

def masked_softmax(s, mask):
    s = jnp.where(mask, s.astype(jnp.float32), -1e30)
    return jnp.where(mask, jax.nn.softmax(s, axis=-1), 0.0)

def compress(k, pos, w1, w2):
    B, G, T, dh = k.shape
    c = k.reshape(B, G, T // CMP_STRIDE, CMP_STRIDE, dh)
    blocks = jnp.concatenate([c[:, :, :-1], c[:, :, 1:]], axis=3) + pos
    flat = blocks.reshape(B, G, blocks.shape[2], CMP_BLK * dh)
    return jax.nn.gelu(flat @ w1) @ w2

def nsa_attention(q, kc, vc, ks, vs, kw, vw, gates):
    B, T, H, dh = q.shape
    G, R = NSA_KV_GROUPS, NSA_REP
    ncmp = kc.shape[2]
    nslc = T // SLC_BLK
    n_sel = min(N_SEL, nslc)
    nq = T // Q_BLOCK
    cmp_start = jnp.arange(ncmp) * CMP_STRIDE
    cmp_end = cmp_start + CMP_BLK - 1
    blk = jnp.arange(nslc)
    overlap = ((cmp_start[:, None] < (blk[None, :] + 1) * SLC_BLK)
               & (cmp_end[:, None] >= blk[None, :] * SLC_BLK)).astype(jnp.float32)
    ks_b = ks.reshape(B, G, nslc, SLC_BLK, dh)
    vs_b = vs.reshape(B, G, nslc, SLC_BLK, dh)
    kw_pad = jnp.pad(kw, ((0, 0), (0, 0), (WIN, 0), (0, 0)))
    vw_pad = jnp.pad(vw, ((0, 0), (0, 0), (WIN, 0), (0, 0)))
    b_idx = jnp.arange(B)[:, None, None, None]
    g_idx = jnp.arange(G)[None, :, None, None]
    q_blocks = jnp.moveaxis(q.reshape(B, nq, Q_BLOCK, G, R, dh), 1, 0).transpose(0, 1, 3, 4, 2, 5)

    def block_fn(args):
        c, qb = args
        t = c * Q_BLOCK + jnp.arange(Q_BLOCK)
        mask_c = cmp_end[None, :] <= t[:, None]
        p_c = masked_softmax(jnp.einsum('bgrqd,bgnd->bgrqn', qb, kc), mask_c)
        o_c = jnp.einsum('bgrqn,bgnd->bgrqd', p_c.astype(vc.dtype), vc)
        imp = jnp.einsum('bgrqn,nj->bgqj', p_c, overlap)
        cur = t // SLC_BLK
        valid = blk[None, :] <= cur[:, None]
        forced = (blk[None, :] == 0) | (blk[None, :] == cur[:, None]) | (blk[None, :] == cur[:, None] - 1)
        score = jnp.where(valid & forced, 1e9, jnp.where(valid, imp, -1e9))
        top_s, top_i = lax.top_k(score, n_sel)
        k_sel = ks_b[b_idx, g_idx, top_i].reshape(B, G, Q_BLOCK, n_sel * SLC_BLK, dh)
        v_sel = vs_b[b_idx, g_idx, top_i].reshape(B, G, Q_BLOCK, n_sel * SLC_BLK, dh)
        tok = (top_i[..., None] * SLC_BLK + jnp.arange(SLC_BLK)).reshape(B, G, Q_BLOCK, n_sel * SLC_BLK)
        mask_s = (tok <= t[None, None, :, None]) & jnp.repeat(top_s > -1e8, SLC_BLK, axis=-1)
        p_s = masked_softmax(jnp.einsum('bgrqd,bgqmd->bgrqm', qb, k_sel), mask_s[:, :, None])
        o_s = jnp.einsum('bgrqm,bgqmd->bgrqd', p_s.astype(v_sel.dtype), v_sel)
        k_win = lax.dynamic_slice_in_dim(kw_pad, c * Q_BLOCK, WIN + Q_BLOCK, axis=2)
        v_win = lax.dynamic_slice_in_dim(vw_pad, c * Q_BLOCK, WIN + Q_BLOCK, axis=2)
        kp = c * Q_BLOCK - WIN + jnp.arange(WIN + Q_BLOCK)
        mask_w = (kp[None, :] <= t[:, None]) & (kp[None, :] > t[:, None] - WIN) & (kp[None, :] >= 0)
        p_w = masked_softmax(jnp.einsum('bgrqd,bgkd->bgrqk', qb, k_win), mask_w)
        o_w = jnp.einsum('bgrqk,bgkd->bgrqd', p_w.astype(v_win.dtype), v_win)
        return jnp.stack([o_c, o_s, o_w], axis=-1)

    out = lax.map(block_fn, (jnp.arange(nq), q_blocks))
    out = out.transpose(1, 0, 4, 2, 3, 5, 6).reshape(B, T, H, dh, 3)
    return jnp.einsum('bthdk,bthk->bthd', out, gates).reshape(B, T, H * dh)

def hybrid_mixer(h, lb, w_in, hg_norm_g, gla_w2, gla_b, gla_norm_g, cmp_pos_k, cmp_pos_v,
                 cmp_w1_k, cmp_w2_k, cmp_w1_v, cmp_w2_v, w_br_hg, w_br_gla, w_br_nsa, w_out, cos, sin):
    B, T, _ = h.shape
    (hq, hf, hi, hog, gq, gk, gv, glr, gog,
     nq_, nkc, nvc, nks, nvs, nkw, nvw, ngate, mgate) = split_cols(h @ w_in)
    lbh = lb.reshape(1, HG_HEADS, 1, HG_HEAD_DIM)
    log_f = jnp.logaddexp(jnp.log(lbh), jnp.log1p(-lbh)
                          + jax.nn.log_sigmoid(heads(hf, HG_HEADS).astype(jnp.float32)))
    o_hg = chunked_gated_linear_attention(jax.nn.silu(heads(hq, HG_HEADS)), -jnp.expm1(log_f),
                                          heads(hi, HG_HEADS), log_f)
    y_hg = head_rmsnorm(o_hg, hg_norm_g, h.dtype) * jax.nn.silu(hog)
    log_a = jax.nn.log_sigmoid((glr @ gla_w2 + gla_b).astype(jnp.float32)) / GLA_TAU
    o_gla = chunked_gated_linear_attention(heads(gq, GLA_HEADS) * GLA_DK ** -0.5, heads(gk, GLA_HEADS),
                                           heads(gv, GLA_HEADS), heads(log_a, GLA_HEADS))
    y_gla = head_rmsnorm(o_gla, gla_norm_g, h.dtype) * jax.nn.silu(gog)
    q = partial_rope(nq_.reshape(B, T, NSA_HEADS, NSA_DH), cos, sin) * NSA_DH ** -0.5

    def kv(z):
        return z.reshape(B, T, NSA_KV_GROUPS, NSA_DH)

    def to_g(z):
        return z.transpose(0, 2, 1, 3)

    kc = compress(to_g(partial_rope(kv(nkc), cos, sin)), cmp_pos_k, cmp_w1_k, cmp_w2_k)
    vc = compress(to_g(kv(nvc)), cmp_pos_v, cmp_w1_v, cmp_w2_v)
    ks = to_g(partial_rope(kv(nks), cos, sin))
    vs = to_g(kv(nvs))
    kw = to_g(partial_rope(kv(nkw), cos, sin))
    vw = to_g(kv(nvw))
    gates = jax.nn.sigmoid(ngate).reshape(B, T, NSA_HEADS, 3)
    y_nsa = nsa_attention(q, kc, vc, ks, vs, kw, vw, gates)
    g = jax.nn.sigmoid(mgate).reshape(B, T, N_BRANCH, D_MODEL)
    m = (g[:, :, 0] * (y_hg @ w_br_hg) + g[:, :, 1] * (y_gla @ w_br_gla)
         + g[:, :, 2] * (y_nsa @ w_br_nsa))
    return m @ w_out

def swiglu(h, w_gate, w_up, w_down):
    return (jax.nn.silu(h @ w_gate) * (h @ w_up)) @ w_down

def second_inputs(seed: int = 0) -> dict:
    key = jax.random.key(seed)
    k = jax.random.split(key, 24)
    L, D = DEPTH, D_MODEL

    def nrm(kk, shape, scale):
        return jax.random.normal(kk, shape, jnp.float32) * scale

    def gain(kk, shape):
        return 1.0 + 0.02 * jax.random.normal(kk, shape, jnp.float32)

    return {
        'x': nrm(k[0], (BATCH, SEQ, D), 1.0),
        'norm1_g': gain(k[1], (L, D)),
        'w_in': nrm(k[2], (L, D, IN_COLS), D ** -0.5),
        'hg_lb': nrm(k[3], (L, HG_DIM), 0.5),
        'hg_norm_g': gain(k[4], (L, HG_DIM)),
        'gla_w2': nrm(k[5], (L, GLA_RANK, GLA_KDIM), GLA_RANK ** -0.5),
        'gla_b': nrm(k[6], (L, GLA_KDIM), 0.1),
        'gla_norm_g': gain(k[7], (L, GLA_VDIM)),
        'cmp_pos_k': nrm(k[8], (L, CMP_BLK, NSA_DH), 0.1),
        'cmp_pos_v': nrm(k[9], (L, CMP_BLK, NSA_DH), 0.1),
        'cmp_w1_k': nrm(k[10], (L, CMP_BLK * NSA_DH, CMP_HID), (CMP_BLK * NSA_DH) ** -0.5),
        'cmp_w2_k': nrm(k[11], (L, CMP_HID, NSA_DH), CMP_HID ** -0.5),
        'cmp_w1_v': nrm(k[12], (L, CMP_BLK * NSA_DH, CMP_HID), (CMP_BLK * NSA_DH) ** -0.5),
        'cmp_w2_v': nrm(k[13], (L, CMP_HID, NSA_DH), CMP_HID ** -0.5),
        'w_br_hg': nrm(k[14], (L, HG_DIM, D), HG_DIM ** -0.5),
        'w_br_gla': nrm(k[15], (L, GLA_VDIM, D), GLA_VDIM ** -0.5),
        'w_br_nsa': nrm(k[16], (L, NSA_DIM, D), NSA_DIM ** -0.5),
        'w_out': nrm(k[17], (L, D, D), D ** -0.5),
        'norm2_g': gain(k[18], (L, D)),
        'w_ffn_gate': nrm(k[19], (L, D, FF_DIM), D ** -0.5),
        'w_ffn_up': nrm(k[20], (L, D, FF_DIM), D ** -0.5),
        'w_ffn_down': nrm(k[21], (L, FF_DIM, D), FF_DIM ** -0.5),
        'final_norm_g': gain(k[22], (D,)),
    }

def second_block(x, norm1_g, w_in, hg_lb, hg_norm_g, gla_w2, gla_b, gla_norm_g, cmp_pos_k, cmp_pos_v,
              cmp_w1_k, cmp_w2_k, cmp_w1_v, cmp_w2_v, w_br_hg, w_br_gla, w_br_nsa, w_out,
              norm2_g, w_ffn_gate, w_ffn_up, w_ffn_down, final_norm_g):
    T = x.shape[1]
    pos = jnp.arange(T, dtype=jnp.float32)
    inv_freq = ROPE_THETA_2 ** (-jnp.arange(0, ROT_DIM, 2, dtype=jnp.float32) / ROT_DIM)
    ang = pos[:, None] * inv_freq[None, :]
    cos, sin = jnp.cos(ang), jnp.sin(ang)
    lbs = jnp.cumsum(jax.nn.softmax(hg_lb.astype(jnp.float32), axis=0), axis=0)
    lbs = lbs - lbs[0]
    for l in range(DEPTH):
        h = rmsnorm(x, norm1_g[l])
        x = x + hybrid_mixer(h, lbs[l], w_in[l], hg_norm_g[l], gla_w2[l], gla_b[l], gla_norm_g[l],
                             cmp_pos_k[l], cmp_pos_v[l], cmp_w1_k[l], cmp_w2_k[l], cmp_w1_v[l], cmp_w2_v[l],
                             w_br_hg[l], w_br_gla[l], w_br_nsa[l], w_out[l], cos, sin)
        h = rmsnorm(x, norm2_g[l])
        x = x + swiglu(h, w_ffn_gate[l], w_ffn_up[l], w_ffn_down[l])
    return rmsnorm(x, final_norm_g)


def setup_inputs(seed=0):
    out = dict(first_inputs(seed))
    for name, value in second_inputs(seed + 1).items():
        if name != "x":
            out[name + "_2"] = value
    return out


def reference(
    x, positions, g_mix_norm, w_in, g_q_lat, w_q_up, g_kv_lat, w_kv_up, g_q_head, g_k_head,
    g_sgu_v, w_spatial, b_spatial, w_pool, pool_scale, g_out_mla, g_out_sgu, g_out_pool, w_out,
    g_ffn_norm, w_gate, w_up, w_down, norm1_g_2, w_in_2, hg_lb_2, hg_norm_g_2, gla_w2_2,
    gla_b_2, gla_norm_g_2, cmp_pos_k_2, cmp_pos_v_2, cmp_w1_k_2, cmp_w2_k_2, cmp_w1_v_2,
    cmp_w2_v_2, w_br_hg_2, w_br_gla_2, w_br_nsa_2, w_out_2, norm2_g_2, w_ffn_gate_2, w_ffn_up_2,
    w_ffn_down_2, final_norm_g_2,
):
    x = first_block(
        x, positions, g_mix_norm, w_in, g_q_lat, w_q_up, g_kv_lat, w_kv_up, g_q_head, g_k_head,
        g_sgu_v, w_spatial, b_spatial, w_pool, pool_scale, g_out_mla, g_out_sgu, g_out_pool,
        w_out, g_ffn_norm, w_gate, w_up, w_down,
    )
    return second_block(
        x, norm1_g_2, w_in_2, hg_lb_2, hg_norm_g_2, gla_w2_2, gla_b_2, gla_norm_g_2,
        cmp_pos_k_2, cmp_pos_v_2, cmp_w1_k_2, cmp_w2_k_2, cmp_w1_v_2, cmp_w2_v_2, w_br_hg_2,
        w_br_gla_2, w_br_nsa_2, w_out_2, norm2_g_2, w_ffn_gate_2, w_ffn_up_2, w_ffn_down_2,
        final_norm_g_2,
    )


_drawn_inputs = setup_inputs


def setup_inputs(seed=0):
    import zlib

    import numpy as np

    out = dict(_drawn_inputs(seed))
    spreads = {}
    factors = {'g_mix_norm': 3.57,
     'g_q_lat': 8.0,
     'g_kv_lat': 4.229,
     'g_q_head': 7.56,
     'g_k_head': 8.0,
     'g_sgu_v': 26.944,
     'b_spatial': 8.0,
     'g_out_mla': 6.026,
     'g_out_sgu': 8.0,
     'g_out_pool': 8.0,
     'g_ffn_norm': 6.457,
     'norm1_g_2': 4.216,
     'hg_lb_2': 8.0,
     'hg_norm_g_2': 44.994,
     'gla_b_2': 4.319,
     'gla_norm_g_2': 43.733,
     'cmp_pos_k_2': 157.688,
     'cmp_pos_v_2': 123.098,
     'cmp_w1_k_2': 10.016,
     'cmp_w2_k_2': 9.751,
     'norm2_g_2': 19.251,
     'final_norm_g_2': 25.788,
     'cmp_w1_v_2': 2.724}
    for name, (base, spread) in spreads.items():
        noise = np.random.default_rng([zlib.crc32(name.encode()), seed]).standard_normal(out[name].shape)
        drawn = base * np.exp(spread * noise) if base else spread * noise
        out[name] = __import__('jax').numpy.asarray(drawn.astype(out[name].dtype))
    for name, factor in factors.items():
        out[name] = (out[name] * factor).astype(out[name].dtype)
    return out
```

```python
import math
from contextlib import ExitStack

import numpy as np
import concourse.bass as bass
from concourse import mybir

F32 = mybir.dt.float32
I32 = mybir.dt.int32
U32 = mybir.dt.uint32
ACT = mybir.ActivationFunctionType
ALU = mybir.AluOpType
AX_X = mybir.AxisListType.X

P = 128
T = 512
NT = T // P
D = 1024
ND = D // P
LAYERS = 2
EPS = 1e-6
NEG = -1e30
TILE = 1024
RING = 3
FB = 22

MIX1_TILES = 21
MIX2_TILES = 87
FFN_TILES = 3 * FB
PER1 = MIX1_TILES + FFN_TILES
PER2 = MIX2_TILES + FFN_TILES
BASE2 = LAYERS * PER1
ALL_TILES = LAYERS * (PER1 + PER2)

NCMP = T // 16 - 1
LEVELS = [1, 2, 4, 8, 16, 32, 64]

HEADS1, QK1, NOPE1 = 4, 96, 64

def columns(spec):
    out, at = {}, 0
    for name, n in spec:
        out[name] = slice(at, at + n)
        at += n
    return out, at

CONST, NCONST = columns([
    ("ident", P), ("ones", P), ("negdiag", P), ("rot2", P), ("rot1", QK1), ("causalT", P),
    ("levels", 8 * P), ("cos2", T), ("sin2", T), ("negcmp", NT * NCMP), ("invcount", 32), ("invwin", 2),
    ("invfreq", 1), ("eps", 1), ("eps96", 1), ("validcmp", NT), ("lb", 8), ("gfinal", ND)])
PAR1, NPAR1 = columns([
    ("g_in", ND), ("g_q", 2), ("g_kv", 1), ("g_qh", 1), ("g_kh", 1), ("pool_scale", 2), ("g_out", ND),
    ("g_ffn", ND), ("g_sgu", 256), ("w_sp", 4 * P), ("b_sp", 2 * T), ("w_pool", 256)])
PAR2, NPAR2 = columns([
    ("g_in", ND), ("g_hg", 4), ("gla_b", 2), ("g_gla", 4), ("g_ffn", ND), ("w_gla", 256),
    ("pos_k", 16), ("pos_v", 16), ("w2_k", P), ("w2_v", 64)])
NPAR = max(NPAR1, NPAR2)


class Signal:

    def __init__(self, sem, per, start=0):
        self.sem, self.per, self.start = sem, per, start

    def __call__(self, n, k):
        return self.sem, n * self.per + (self.start + k)


def build(nc, xT, pos, wstream, params, const, outT):
    ctx = ExitStack()
    with ctx:
        def sb(name, shape, dt=F32):
            return ctx.enter_context(nc.sbuf_tensor(name, shape, dt))

        def signal(name, per, start=0):
            return Signal(ctx.enter_context(nc.semaphore(name)), per, start)

        x = sb("x", [P, ND, T])
        h = sb("h", [P, ND, T])
        ring = sb("ring", [P, RING, TILE])
        cst = sb("cst", [P, NCONST])
        par = sb("par", [P, NPAR])
        lnv = sb("lnv", [P, 2, T])
        rstd = sb("rstd", [P, 2, T])
        small = sb("small", [P, 64])
        ARENA = 33200
        arena = sb("arena", [P, ARENA])
        bank = [ctx.enter_context(nc.psum_tensor(f"bank{i}", [P, T], F32)) for i in range(8)]

        def C(name, rows=slice(0, P)):
            return cst[rows, CONST[name]]

        def view(off, *dims):
            n = int(np.prod(dims))
            assert off + n <= ARENA, (off, dims)
            a = arena[:, off:off + n]
            if len(dims) == 1:
                return a
            if len(dims) == 2:
                return a.rearrange("p (a b) -> p a b", a=dims[0])
            return a.rearrange("p (a b c) -> p a b c", a=dims[0], b=dims[1])

        act = view(0, FB, T)
        sil = view(FB * T, 3, T)
        W0 = 25000
        prob = view(W0, 2, 1280)
        probT = view(W0 + 2560, 2, 1280)
        ST = [view(W0 + 2048 * i, 4, T) for i in range(2)]
        PS0 = [0, P, 3 * P, 6 * P]
        PT0 = [0, 4 * P, 7 * P, 9 * P]
        sq = view(W0 + 5120, 2, T)
        m1, m1_at = {}, {}
        at = 0
        for name, dims in [("qlat", (2, T)), ("kvlat", (T,)), ("krope", (T,)), ("u", (2, T)), ("v", (NT, 256)),
                           ("pin", (2, T + 16)), ("win_a", (T + 16,)), ("win_b", (T + 16,)), ("qh", (4, T)),
                           ("kh", (4, T)), ("V", (NT, T)), ("mix", (ND, T)), ("sqlat", (3, T)),
                           ("cos", (T,)), ("sin", (T,)), ("ta", (T,)), ("tb", (T,)), ("sqkr", (T,)), ("win_m", (2, T))]:
            m1[name] = view(at, *dims)
            m1_at[name] = at
            at += int(np.prod(dims))
        assert at <= W0, at
        m2 = {}
        at = 0
        for name, dims in [("hq", (4, T)), ("hk", (4, T)), ("hlf", (4, T)), ("hv", (NT, T)), ("hy", (4, T)),
                           ("gq", (2, T)), ("gk", (2, T)), ("glf", (2, T)), ("gv", (NT, T)), ("gy", (4, T)),
                           ("nq", (4, T)), ("ck", (2, T)), ("cv", (2, T)), ("ks", (2, T)), ("kw", (2, T)),
                           ("nv", (NT, 256)), ("gate", (NT, 24)), ("hid", (124,)), ("kc", (62,)), ("vc", (128,)),
                           ]:
            m2[name] = view(at, *dims)
            at += int(np.prod(dims))
        assert at <= W0, at
        at = W0 + 6144
        for name, dims in [("X", (T,)), ("Eq", (256,)), ("Ek", (256,)), ("ob", (2, T))]:
            m2[name] = view(at, *dims)
            at += int(np.prod(dims))
        rope2 = sb("rope2", [P, 2, T])
        ropec, ropes = rope2[:, 0, :], rope2[:, 1, :]
        ksl = rope2
        qsl = view(W0 + 4096, 2, T)
        cm = sb("cm", [P, 2, NT * NCMP])
        m2["cmpT"] = view(0, 8, T)
        m2["m"] = view(0, ND, T)
        m2["sig"] = view(4096, 6, T)

        sgt = view(m1_at["ta"], NT, 256)
        lbt = sb("lbt", [P, 40])

        slot = [ctx.enter_context(nc.semaphore(f"weights_in_slot{r}")) for r in range(RING)]
        s_const = ctx.enter_context(nc.semaphore("constants_loaded"))
        s_x0 = ctx.enter_context(nc.semaphore("x_loaded"))
        s_pos = ctx.enter_context(nc.semaphore("positions_loaded"))
        s_par = signal("params_loaded", 16)
        s_init = ctx.enter_context(nc.semaphore("vector_setup"))
        s_rope = ctx.enter_context(nc.semaphore("rope_angles"))
        s_ropea = ctx.enter_context(nc.semaphore("rope_sines"))
        s_out = ctx.enter_context(nc.semaphore("output_stored"))
        x_ready = signal("residual_block_ready", ND)
        n_sq = signal("norm_squares", ND)
        n_ss = signal("norm_sum", 1)
        n_ln = signal("norm_log", 1)
        n_rs = signal("norm_rstd", 1)
        h_ready = signal("h_block_ready", ND, 1)
        gu_mm = signal("gate_up_product", 2 * FB)
        silu = signal("gate_silu", FB, 3)
        act_ready = signal("ffn_hidden_ready", FB, 3)
        down_mm = signal("down_tile_done", FB, RING)
        z_mm = signal("z1_product", 22)
        z_out = signal("z1_copied", 22)
        z_sq = signal("z1_squares", 3)
        lat_ss = signal("latent_sum", 2)
        lat_ln = signal("latent_log", 2)
        lat_rs = signal("latent_rstd", 2)
        lat_n = signal("latent_normed", 3)
        hd_sq = signal("head_squares", 9)
        hd_raw = signal("head_raw", 8)
        hd_ss = signal("head_sum", 8)
        hd_ln = signal("head_log", 8)
        hd_rs = signal("head_rstd", 8)
        hd_n = signal("head_normed", 8)
        hd_rot = signal("head_rotated", 8)
        hd_t = signal("head_rope_parts", 16)
        hd_r = signal("head_roped", 8)
        sg_q = signal("sgu_squares", 1)
        sg_ss = signal("sgu_sumsq", 1)
        sg_ln = signal("sgu_log", 1)
        sg_rs = signal("sgu_rstd", 1)
        sg_w = signal("sgu_weights_masked", 4)
        sg_v = signal("sgu_values_normed", NT)
        sg_mm = signal("sgu_mixed", 2)
        sg_z = signal("sgu_biased", 2)
        sg_g = signal("sgu_gated", 2)
        pw = signal("pool_step", 13)
        pl_m = signal("pool_means", 2)
        pl_mm = signal("pool_product", 2)
        pl_o = signal("pool_out", 2)
        mx_sq = signal("mix_squares", ND)
        mx_ss = signal("mix_sum", 3)
        mx_ln = signal("mix_log", 3)
        mx_rs = signal("mix_rstd", 3)
        mx_n = signal("mix_normed", ND)
        wo_mm = signal("w_out_product", ND)
        def attention_signals(tag, units):
            return {k: signal(f"{tag}_{k}", n * units) for k, n in
                    [("scores", 4), ("maxed", 4), ("exped", 4), ("recip", 1), ("gated", 1), ("scaled", 4),
                     ("turned", 4), ("turned_out", 4), ("pv", 1)]}
        at1 = attention_signals("mla", HEADS1)
        at2 = attention_signals("nsa", 16)
        o1_out = signal("mla_out_copied", HEADS1)
        y_mm = signal("z2_product", 42)
        y_out = signal("z2_copied", 42)
        lb_s = ctx.enter_context(nc.semaphore("lower_bounds"))
        lb_e = ctx.enter_context(nc.semaphore("lower_bound_exps"))
        lb_l = signal("lower_bound_of_layer", 2)
        hf_s = signal("forget_sigmoid", 4)
        hf_k = signal("forget_key", 4)
        hf_m = signal("forget_mixed", 4)
        hf_f = signal("forget_gate", 4)
        hf_l = signal("forget_log", 4)
        gl_a = signal("gla_abs", 2)
        gl_e = signal("gla_exp", 2)
        gl_l = signal("gla_ln", 2)
        gl_d = signal("gla_logsig", 2)
        gl_f = signal("gla_log_decay", 2)
        ln_x0 = signal("lin_suffix_zeroed", 6)
        ln_e = signal("lin_prefix_exp", 54)
        ln_f = signal("lin_suffix_exp", 48)
        ln_q = signal("lin_scaled_q", 54)
        ln_k = signal("lin_scaled_k", 48)
        ln_x = signal("lin_suffix", 48)
        ln_p = signal("lin_prefix", 48)
        ln_mm = signal("lin_scores", 80)
        ln_st = signal("lin_scores_placed", 80)
        ln_pv = signal("lin_pv", 8)
        lo_sq = signal("lin_out_squares", 8)
        lo_o = signal("lin_out_copied", 8)
        lo_ss = signal("lin_out_sum", 8)
        lo_ln = signal("lin_out_log", 8)
        lo_rs = signal("lin_out_rstd", 8)
        lo_n = signal("lin_out_normed", 8)
        lo_y = signal("lin_out_gated", 8)
        rp_mm = signal("nsa_rotated", 7)
        rp_u = signal("nsa_rope_sin", 7)
        rp_t = signal("nsa_rope_cos", 7)
        rp_o = signal("nsa_roped", 16)
        cv_o = signal("cmp_values_laid", 3)
        ch_mm = signal("cmp_hidden", 4)
        ch_b = signal("cmp_bias", 2)
        ch_g = signal("cmp_gelu", 2)
        cc_mm = signal("cmp_projected", 2)
        cc_o = signal("cmp_kv_copied", 2)
        cs_mm = signal("cmp_scores", 8)
        cs_m = signal("cmp_masked", 8)
        cs_x = signal("cmp_max", 8)
        cs_d = signal("cmp_shifted", 8)
        cs_e = signal("cmp_exp", 8)
        cs_s = signal("cmp_sum", 8)
        cs_r = signal("cmp_recip", 8)
        cs_v = signal("cmp_valid", 8)
        cs_g = signal("cmp_gate", 8)
        cs_p = signal("cmp_probs", 8)
        cs_t = signal("cmp_turned", 8)
        cs_o = signal("cmp_turned_out", 8)
        no_y = signal("nsa_out_copied", 4)
        mg_mm = signal("merge_gate_product", 24)
        mg_s = signal("merge_gate_sigmoid", 24, 3)
        br_mm = signal("branch_product", 24)
        br_m = signal("branch_merged", 24, 6)
        br_a = signal("branch_added", 16)

        block = ctx.enter_context(nc.Block())

        LIN = [(u, m2["hq"][:, u, :], m2["hk"][:, u, :], m2["hlf"][:, u, :], [(u, 0, P)]) for u in range(4)] + \
              [(4 + b, m2["gq"][:, b, :], m2["gk"][:, b, :], m2["glf"][:, b, :],
                [(4 + 2 * b, 0, 64), (5 + 2 * b, 64, P)]) for b in range(2)]

        LIN_PLACED = {hd: 10 * (hd + 1) for hd in range(4)} | {4: 59, 5: 60, 6: 79, 7: 80}

        def raw_block(i):
            return m2["nq"][:, i, :] if i < 4 else (m2["ck"], m2["ks"], m2["kw"])[i - 4][:, 0, :]

        def lin_value(head, s):
            v = m2["hv"] if head < 4 else m2["gv"]
            return v[:, s, (head % 4) * P:(head % 4 + 1) * P]

        def lin_gate(head):
            return (m2["hy"] if head < 4 else m2["gy"])[:, head % 4, :]

        def halves(a, m, which):
            return a.rearrange("p (g two m) -> p g two m", two=2, m=m)[:, :, which, :]

        def ends(a, m, which):
            v = a.rearrange("p (g two m) -> p g two m", two=2, m=m)[:, :, which, m - 1:m]
            return v.broadcast_to([P, T // (2 * m), m])

        def compact(a, m):
            return a.rearrange("p (g m) -> p g m", m=m)

        def diagonal(s):
            flat = ST[s].rearrange("p a b -> p (a b)")
            return [flat[:, 640 * i:640 * i + P] for i in range(NT)]

        def diag4(s):
            off = W0 + 2048 * s
            return arena[:, off:off + 2560].rearrange("p (a b) -> p a b", b=640)[:, :, 0:P]

        Y = {}
        order = [("hf", 4, 0), ("glr", 1, 4), ("ngate", 1, 4), ("hq", 4, 5), ("hog", 4, 9), ("gog", 4, 13),
                 ("hi", 4, 17), ("gdec", 2, None), ("gk", 2, 21), ("gq", 2, 23), ("gv", 4, 25), ("nq", 4, 29),
                 ("nkc", 1, 33), ("nks", 1, 34), ("nkw", 1, 35), ("nvc", 1, 36), ("nv", 2, 37)]
        for name, n, tile in order:
            for i in range(n):
                Y[name, i] = (len(Y), tile)
        YKEYS = list(Y)
        YN = 42
        FILL = {(u, 2 * k + 1): YKEYS[24 + 5 * u + k] for u in range(4) for k in range(5)
                if 24 + 5 * u + k < len(YKEYS)}

        def y_bank(g):
            return bank[g % 3]

        def tile_in(l, base, per, t):
            return slot[t % RING], l * (16 * per // RING) + 16 * ((base + t) // RING + 1)

        FREE1 = [(z_mm, k) for k in (1, 2, 3, 4, 5, 6, 7, 8, 9, 10, 14, 22)] + \
                [(wo_mm, j + 1) for j in range(ND)] + ["pad"]
        FREE2 = [(y_mm, k) for k in (1, 2, 3, 4, *range(6, 23), *range(25, 43))] + \
                [(ch_mm, 1), (ch_mm, 2), (ch_mm, 3), (ch_mm, 4)]
        for i in range(4):
            FREE2 += [(mg_mm, 6 * i + k) for k in range(1, 7)] + \
                     [(br_mm, 6 * i + k) for k in (2, 4, 6)]
        FREE2 += [(wo_mm, j + 1) for j in range(ND)]
        assert len(FREE1) == MIX1_TILES and len(FREE2) == MIX2_TILES, (len(FREE1), len(FREE2))

        @block.sync
        def _(sp):
            def load(t, r):
                sp.dma_start(ring[:, r, :],
                             wstream[bass.ds(t, 1)].rearrange("a p n -> p (a n)")).then_inc(slot[r], 16)

            def layer(l, nf, base, per, free):
                mix = len(free)
                sp.wait_ge(*h_ready(2 * nf, 0))
                sp.dma_start(par[:, :], params[bass.ds(nf, 1)].rearrange("a p n -> p (a n)")).then_inc(s_par.sem, 16)

                def wait_product(t):
                    if t < 0:
                        sp.wait_ge(*down_mm(nf, t + 1))
                    elif t < mix:
                        if free[t] == "pad":
                            sp.wait_ge(*tile_in(l, base, per, t))
                        else:
                            sem, k = free[t]
                            sp.wait_ge(*sem(nf if sem is wo_mm else l, k))
                    elif t < mix + 2 * FB:
                        sp.wait_ge(*gu_mm(nf, t - mix + 1))
                    else:
                        sp.wait_ge(*down_mm(nf, t - mix - 2 * FB + 1))

                for t in range(mix + 2 * RING):
                    wait_product(t - RING)
                    load(l * per + (base + t), t % RING)
                with sp.Fori(1, 7) as it:
                    for r in range(6):
                        sp.wait_ge(gu_mm.sem, nf * gu_mm.per + it * 6 + (r - RING + 1))
                        load(l * per + it * 6 + (base + mix + r), r % RING)
                for t in range(mix + 42, mix + 48):
                    wait_product(t - RING)
                    load(l * per + (base + t), t % RING)
                with sp.Fori(0, 6) as it:
                    for r in range(RING):
                        sp.wait_ge(down_mm.sem, nf * down_mm.per + it * RING + (down_mm.start + 2 + r))
                        load(l * per + it * RING + (base + mix + 48 + r), r)

            sp.dma_start(cst[:, :], const).then_inc(s_const, 16)
            sp.dma_start(arena[:, 0:ND * T], xT).then_inc(s_x0, 16)
            sp.dma_start(m1["ta"].bitcast(I32), pos).then_inc(s_pos, 16)
            with sp.Fori(0, LAYERS) as l:
                layer(l, l, 0, PER1, FREE1)
            with sp.Fori(0, LAYERS) as l:
                layer(l, l + LAYERS, BASE2, PER2, FREE2)
            sp.wait_ge(*h_ready(8, ND))
            sp.dma_start(outT, h[:, :, :].rearrange("p a t -> p (a t)")).then_inc(s_out, 16)
            sp.wait_ge(s_out, 16)

        @block.tensor
        def _(pe):
            def product(out, lhsT, rhs, start=True, stop=True):
                return pe.matmul(out, lhsT, rhs, start=start, stop=stop)

            def norm(n):
                for j in range(ND):
                    pe.wait_ge(*n_sq(n, j + 1))
                    last = product(bank[0][:, :], C("ones"), h[:, j, :], j == 0, j == ND - 1)
                last.then_inc(n_ss.sem, 1)

            def wide(out, r, rhs, n=ND, cols=P):
                for k in range(n):
                    last = product(out, ring[:, r, k * P:k * P + cols], rhs[:, k, :], k == 0, k == n - 1)
                return last

            def token_major(out, r, first=0, cols=P):
                for m in range(NT):
                    for k in range(ND):
                        last = product(out[:, m * cols:(m + 1) * cols], h[:, k, m * P:m * P + P],
                                       ring[:, r, k * P + first:k * P + first + cols], k == 0, k == ND - 1)
                return last

            def w_out(nf, rhs, l, base, per, tile):
                for j in range(ND):
                    pe.wait_ge(*tile_in(l, base, per, tile + j))
                    wide(bank[j][:, :], (tile + j) % RING, rhs).then_inc(wo_mm.sem, 1)

            def ffn(nf, norm_pass, l, base, per, mix):
                def gate_up(g, r, it):
                    for w, (banks, used) in enumerate(((bank[0:3], silu), (bank[3:6], act_ready))):
                        t = 2 * r + w
                        sem, v = tile_in(l, base, per, mix + 2 * g + w)
                        pe.wait_ge(sem, v + it * 32)
                        pe.wait_ge(used.sem, nf * FB + it * RING + (used.start + g - 2))
                        wide(banks[r][:, :], t % RING, h).then_inc(gu_mm.sem, 1)

                with pe.Fori(0, 7) as it:
                    for r in range(3):
                        if r == 0:
                            pe.wait_ge(*h_ready(norm_pass, ND))
                        gate_up(r, r, it)
                gate_up(FB - 1, 0, 0)

                def down(d, it, first=False, last=False):
                    sem, v = tile_in(l, base, per, mix + 2 * FB + d)
                    pe.wait_ge(sem, v + it * 16)
                    r = (mix + 2 * FB + d) % RING
                    hid = act[:, d, :] if isinstance(it, int) else \
                        act[:, bass.ds(it * 3 + d, 1), :].rearrange("p a t -> p (a t)")
                    for j in range(ND):
                        i = product(bank[j][:, :], ring[:, r, j * P:j * P + P], hid, first, last)
                    i.then_inc(down_mm.sem, 1)

                pe.wait_ge(*act_ready(nf, FB))
                down(0, 0, first=True)
                with pe.Fori(0, 6) as it:
                    for d in range(1, 4):
                        down(d, it)
                for d in range(19, FB):
                    down(d, 0, last=d == FB - 1)

            def scores(s, l, u, q, k):
                for t in range(NT):
                    if u > 0:
                        pe.wait_ge(*s["exped"](l, NT * (u - 1) + t + 1))
                    b = bank[3 + t]
                    product(b[:, 0:(t + 1) * P], q[:, t * P:t * P + P], k[:, 0:(t + 1) * P], True, False)
                    product(b[:, t * P:(t + 1) * P], C("ident"), C("negdiag"), False, True)\
                        .then_inc(s["scores"].sem, 1)

            def turn_and_pv(s, l, u, v, out, bank_free, first, more):
                pe.wait_ge(*s["scaled"](l, NT * (u + 1)))
                for st in range(NT):
                    c = NT * u + st
                    if c >= 2:
                        pe.wait_ge(*s["turned_out"](l, c - 1))
                    b = bank[(7, 2)[c % 2]]
                    for t in range(st, NT):
                        off = PS0[t] + st * P
                        last = pe.transpose(b[:, (t - st) * P:(t - st + 1) * P],
                                            prob[:, u % 2, off:off + P], C("ident"))
                    last.then_inc(s["turned"].sem, 1)
                if bank_free is not None:
                    pe.wait_ge(*bank_free)
                for st in range(NT):
                    pe.wait_ge(*s["turned_out"](l, NT * u + st + 1))
                    last = product(out[:, st * P:T], v(st), probT[:, u % 2, PT0[st]:PT0[st] + (NT - st) * P],
                                   first and st == 0, (not more) and st == NT - 1)
                return last

            def mixer1(l):
                def z_wait(g, tile=None):
                    if tile is not None:
                        pe.wait_ge(*tile_in(l, 0, PER1, tile))
                    if g >= 3:
                        pe.wait_ge(*z_out(l, g - 2))

                def lat_sum(i):
                    blocks = ((0, 1), (2,))[i]
                    for c in blocks:
                        pe.wait_ge(*z_sq(l, c + 1))
                        last = product(bank[3 + i][:, :], C("ones"), m1["sqlat"][:, c, :],
                                       c == blocks[0], c == blocks[-1])
                    last.then_inc(lat_ss.sem, 1)

                pe.wait_ge(*h_ready(2 * l, ND))
                for g in range(4):
                    z_wait(g, g)
                    wide(bank[g % 3][:, :], g % RING, h).then_inc(z_mm.sem, 1)
                for c in range(2):
                    z_wait(4 + c, 4 + c)
                    token_major(bank[(4 + c) % 3], (4 + c) % RING).then_inc(z_mm.sem, 1)
                    lat_sum(c)
                for g in range(6, 10):
                    z_wait(g, g)
                    wide(bank[g % 3][:, :], g % RING, h).then_inc(z_mm.sem, 1)

                def head(i):
                    g = 10 + i
                    z_wait(g, 10 if i < 4 else 11)
                    b = bank[g % 3]
                    if i < 4:
                        pe.wait_ge(*lat_n(l, 2))
                        for c in range(2):
                            at = c * 384 + i * QK1
                            last = product(b[0:QK1, :], ring[:, 10 % RING, at:at + QK1], m1["qlat"][:, c, :],
                                           c == 0, c == 1)
                    else:
                        pe.wait_ge(*lat_n(l, 3))
                        at = (i - 4) * NOPE1
                        last = product(b[0:NOPE1, :], ring[:, 11 % RING, at:at + NOPE1], m1["kvlat"])
                    last.then_inc(z_mm.sem, 1)

                def head_sum(i):
                    pe.wait_ge(*hd_sq(l, i + 2))
                    if i >= 2:
                        pe.wait_ge(*hd_ln(l, i - 1))
                    else:
                        pe.wait_ge(*lat_ln(l, i + 1))
                    b = bank[3 + i % 2]
                    if i < 4:
                        last = product(b[0:QK1, :], C("ones", slice(0, QK1))[:, 0:QK1], sq[0:QK1, i % 2, :])
                    else:
                        product(b[0:QK1, :], C("ones", slice(0, 64))[:, 0:QK1], sq[0:64, i % 2, :], True, False)
                        last = product(b[0:QK1, :], C("ones", slice(64, 96))[:, 0:QK1], m1["sqkr"][64:96, :],
                                       False, True)
                    last.then_inc(hd_ss.sem, 1)

                def rotate(i):
                    pe.wait_ge(*hd_n(l, i + 1))
                    if i >= 2:
                        pe.wait_ge(*hd_t(l, 2 * (i - 2) + 1))
                    hv = (m1["qh"] if i < 4 else m1["kh"])[0:QK1, i % 4, :]
                    product(bank[5 + i % 2][0:QK1, :], C("rot1", slice(0, QK1)), hv).then_inc(hd_rot.sem, 1)

                for i in range(8):
                    head(i)
                    if i >= 1:
                        head_sum(i - 1)
                    if i >= 2:
                        rotate(i - 2)
                head_sum(7)
                rotate(6)
                for m in range(NT):
                    z_wait(18 + m)
                    product(bank[(18 + m) % 3][:, :], m1["kvlat"][:, m * P:m * P + P],
                            ring[:, 11 % RING, 256:768]).then_inc(z_mm.sem, 1)
                rotate(7)

                pe.wait_ge(*sg_v(l, NT))
                pe.wait_ge(*sg_w(l, 4))
                pe.wait_ge(*hd_ln(l, 8))
                for b in range(2):
                    for hh in range(2):
                        hd = 2 * b + hh
                        for m in range(NT):
                            last = product(bank[3 + b][64 * hh:64 * hh + 64, m * P:m * P + P],
                                           m1["v"][:, m, hd * 64:hd * 64 + 64],
                                           par[:, PAR1["w_sp"]][:, hd * P:hd * P + P])
                    last.then_inc(sg_mm.sem, 1)
                pe.wait_ge(*hd_t(l, 16))
                for b in range(2):
                    pe.wait_ge(*pl_m(l, b + 1))
                    product(bank[5 + b][:, :], par[:, PAR1["w_pool"]][:, b * P:b * P + P],
                            m1["win_m"][:, b, :]).then_inc(pl_mm.sem, 1)

                def mix_sum(i):
                    pe.wait_ge(*mx_sq(l, (2, 4, 8)[i]))
                    blocks = ((4, 5), (6, 7), (0, 1, 2, 3))[i]
                    for c in blocks:
                        last = product(bank[(3, 4, 3)[i]][:, :], C("ones"), h[:, c, :],
                                       c == blocks[0], c == blocks[-1])
                    last.then_inc(mx_ss.sem, 1)

                pe.wait_ge(*sg_z(l, 2))
                mix_sum(0)
                mix_sum(1)
                pe.wait_ge(*hd_r(l, 8))
                pe.wait_ge(*z_out(l, 22))
                pe.wait_ge(*mx_ln(l, 2))
                pe.wait_ge(*pl_o(l, 2))
                for u in range(HEADS1 + 1):
                    if u < HEADS1:
                        scores(at1, l, u, m1["qh"][0:QK1, u, :], m1["kh"][0:QK1, u, :])
                    if u >= 1:
                        w = u - 1
                        turn_and_pv(at1, l, w, lambda st, w=w: m1["V"][:, st, w * P:w * P + P], bank[w % 2][:, :],
                                    o1_out(l, w - 1) if w >= 2 else None, True, False)\
                            .then_inc(at1["pv"].sem, 1)
                mix_sum(2)
                pe.wait_ge(*mx_n(l, ND))
                w_out(l, m1["mix"], l, 0, PER1, 12)

            def mixer2(l):
                def project(key):
                    name, i = key
                    g, tile = Y[key]
                    b = y_bank(g)
                    if g >= 3:
                        pe.wait_ge(*y_out(l, g - 2))
                    if name == "gdec":
                        pe.wait_ge(*y_out(l, Y["glr", 0][0] + 1))
                        last = product(b[:, :], par[0:16, PAR2["w_gla"]][:, i * P:i * P + P], ropec[0:16, :])
                    elif name == "glr":
                        pe.wait_ge(*tile_in(l, BASE2, PER2, tile))
                        last = wide(b[0:16, :], tile % RING, h, cols=16)
                    elif name == "ngate":
                        last = token_major(b, tile % RING, 16, 24)
                    elif name in ("hi", "gv", "nv"):
                        pe.wait_ge(*tile_in(l, BASE2, PER2, tile + i))
                        last = token_major(b, (tile + i) % RING)
                    else:
                        pe.wait_ge(*tile_in(l, BASE2, PER2, tile + i))
                        last = wide(b[:, :], (tile + i) % RING, h)
                    last.then_inc(y_mm.sem, 1)

                pe.wait_ge(*h_ready(4 + 2 * l, ND))
                for key in YKEYS[:24]:
                    project(key)

                group = 0
                for u, q, k, lf, heads in LIN:
                    if u >= 4:
                        for head, _, _ in LIN[u - 1][4]:
                            lin_pv(l, head)
                            lin_sum(l, head)
                    for v in range(10):
                        for head, lo, hi in heads:
                            rows = slice(lo, hi)
                            if v == 0:
                                pe.wait_ge(*(y_out(l, Y["hq", u][0] + 1) if u < 4 else
                                             y_out(l, Y["gq", u - 4][0] + 1)))
                                if u < 4:
                                    pe.wait_ge(*hf_k(l, u + 1))
                            else:
                                pe.wait_ge(*ln_q(l, 9 * u + v))
                                if v >= 2:
                                    pe.wait_ge(*ln_k(l, 8 * u + v - 1))
                            if group >= 4:
                                pe.wait_ge(*ln_st(l, group - 3))
                            b = bank[3 + group % 4]
                            qv = q if v == 0 else qsl[:, v % 2, :]
                            kv = k if v < 2 else ksl[:, v % 2, :]
                            if v < 8:
                                for t in range(NT):
                                    c = slice(t * P, t * P + P)
                                    last = product(b[:, c], kv[rows, c], qv[rows, c])
                            else:
                                for n, (ks_, q0, q1) in enumerate((((0, 1, 2), (2, 3, 4)) if v == 8 else
                                                                   ((0, 2, 4), (1, 2, 4)))):
                                    w = (q1 - q0) * P
                                    last = product(b[:, n * w:(n + 1) * w], kv[rows, ks_ * P:ks_ * P + P],
                                                   qv[rows, q0 * P:q1 * P])
                            last.then_inc(ln_mm.sem, 1)
                            group += 1
                        if (u, v) in FILL:
                            project(FILL[u, v])
                        if 0 < u < 4 and v == 2:
                            lin_pv(l, u - 1)
                        if 0 < u < 4 and v == 4:
                            lin_sum(l, u - 1)
                for head, _, _ in LIN[-1][4]:
                    lin_pv(l, head)
                    lin_sum(l, head)

                pe.wait_ge(*y_out(l, YN))
                for i in range(7):
                    if i >= 2:
                        pe.wait_ge(*rp_u(l, i - 1))
                    product(bank[i % 2][:, :], C("rot2"), raw_block(i)).then_inc(rp_mm.sem, 1)
                pe.wait_ge(*ln_st(l, 80))
                for kv, (data, done, posn, b1, b2) in enumerate(((m2["ck"], rp_o(l, 8), "pos_k", 4, 5),
                                                                 (m2["cv"], cv_o(l, 3), "pos_v", 6, 3))):
                    pe.wait_ge(*done)
                    for half in range(2):
                        t = 39 + 2 * kv + half
                        pe.wait_ge(*tile_in(l, BASE2, PER2, t))
                        for p in range(8 * half, 8 * half + 8):
                            w = ring[:, t % RING, (p % 8) * P:(p % 8) * P + P]
                            product(bank[b1][:, 0:2 * NCMP], w, data[:, :, 2 * p:2 * p + 16 * (NCMP - 1) + 1:16],
                                    p == 0, p == 15)
                            last = product(bank[b2][:, 0:1], w, par[:, PAR2[posn]][:, p:p + 1], p == 0, p == 15)
                        last.then_inc(ch_mm.sem, 1)
                pe.wait_ge(*ch_g(l, 1))
                pe.wait_ge(*rp_u(l, 7))
                product(bank[0][:, 0:62], par[:, PAR2["w2_k"]], m2["hid"][:, 0:62]).then_inc(cc_mm.sem, 1)
                pe.wait_ge(*ch_g(l, 2))
                for g in range(2):
                    last = product(bank[1][0:NCMP, g * 64:g * 64 + 64], m2["hid"][:, 62 + g * 31:93 + g * 31],
                                   par[:, PAR2["w2_v"]])
                last.then_inc(cc_mm.sem, 1)

                def cmp_scores(hd):
                    if hd >= 2:
                        pe.wait_ge(*cs_m(l, hd - 1))
                    rows, g = slice(64 * (hd % 2), 64 * (hd % 2) + 64), hd // 4
                    for t in range(NT):
                        last = product(bank[2 + hd % 2][:, t * NCMP:(t + 1) * NCMP],
                                       m2["nq"][rows, hd // 2, t * P:t * P + P],
                                       m2["kc"][rows, g * NCMP:(g + 1) * NCMP])
                    last.then_inc(cs_mm.sem, 1)

                pe.wait_ge(*cc_o(l, 2))
                pe.wait_ge(*rp_o(l, 16))
                cmp_scores(0)
                cmp_scores(1)
                for hd in range(8):
                    pe.wait_ge(*cs_p(l, hd + 1))
                    if hd >= 2:
                        pe.wait_ge(*cs_o(l, hd - 1))
                    for t in range(NT):
                        last = pe.transpose(bank[4 + hd % 2][0:NCMP, t * P:t * P + P],
                                            cm[:, hd % 2, t * NCMP:(t + 1) * NCMP], C("ident"))
                    last.then_inc(cs_t.sem, 1)
                    if hd + 2 < 8:
                        cmp_scores(hd + 2)
                pe.wait_ge(*cs_o(l, 8))
                for u in range(17):
                    if u < 16:
                        hd = u // 2
                        rows = slice(64 * (hd % 2), 64 * (hd % 2) + 64)
                        keys = (m2["ks"], m2["kw"])[u % 2][rows, hd // 4, :]
                        scores(at2, l, u, m2["nq"][rows, hd // 2, :], keys)
                    if u >= 1:
                        w = u - 1
                        hd, win = w // 2, w % 2
                        out = bank[(hd // 2) % 2][64 * (hd % 2):64 * (hd % 2) + 64, :]
                        at = 128 * win + 64 * (hd // 4)
                        last = turn_and_pv(at2, l, w, lambda st, at=at: m2["nv"][:, st, at:at + 64], out,
                                           no_y(l, hd // 2 - 1) if hd % 2 == 0 and win == 0 and hd >= 4 else None,
                                           win == 0, True)
                        if win:
                            last = product(out, m2["vc"][0:NCMP, (hd // 4) * 64:(hd // 4) * 64 + 64],
                                           m2["cmpT"][0:NCMP, hd, :], False, True)
                        last.then_inc(at2["pv"].sem, 1)

                with pe.Fori(0, 4) as it:
                    for r in range(6):
                        if r == 0:
                            pe.wait_ge(*lo_y(l, 8))
                            pe.wait_ge(*no_y(l, 4))
                        sem, v = tile_in(l, BASE2, PER2, 43 + r)
                        pe.wait_ge(sem, v + it * 48)
                        pe.wait_ge(mg_s.sem, l * 24 + it * 6 + (mg_s.start + r - 2))
                        wide(bank[r % 3][:, :], (43 + r) % RING, h).then_inc(mg_mm.sem, 1)
                    for r in range(6):
                        sem, v = tile_in(l, BASE2, PER2, 49 + r // 2)
                        pe.wait_ge(sem, v + it * 48)
                        pe.wait_ge(br_m.sem, l * 24 + it * 6 + (br_m.start + r - 2))
                        y = (m2["hy"], m2["gy"], m2["nq"])[r % 3]
                        for c in range(4):
                            at = (r % 2) * 512 + c * P
                            last = product(bank[3 + r % 3][:, :], ring[:, (49 + r // 2) % RING, at:at + P],
                                           y[:, c, :], c == 0, c == 3)
                        last.then_inc(br_mm.sem, 1)
                pe.wait_ge(*br_a(l, 16))
                w_out(l + LAYERS, m2["m"], l, BASE2, PER2, 79)

            def lin_pv(l, head):
                pe.wait_ge(*ln_st(l, LIN_PLACED[head]))
                if head > 0:
                    pe.wait_ge(*lo_ln(l, head))
                else:
                    pe.wait_ge(*y_out(l, Y["hi", 3][0] + 1))
                if head >= 4:
                    pe.wait_ge(*y_out(l, Y["gv", 3][0] + 1))
                for st in range(NT):
                    last = product(bank[7][:, st * P:T], lin_value(head, st), ST[head % 2][:, st, st * P:T],
                                   st == 0, st == NT - 1)
                last.then_inc(ln_pv.sem, 1)

            def lin_sum(l, head):
                pe.wait_ge(*lo_o(l, head + 1))
                product(bank[7][:, :], C("ones"), sq[:, head % 2, :]).then_inc(lo_ss.sem, 1)

            pe.wait_ge(s_const, 16)
            pe.sem_inc(down_mm.sem, down_mm.start)
            with pe.Fori(0, LAYERS) as l:
                norm(2 * l)
                mixer1(l)
                norm(2 * l + 1)
                ffn(l, 2 * l + 1, l, 0, PER1, MIX1_TILES)
            with pe.Fori(0, LAYERS) as l:
                norm(2 * l + 4)
                mixer2(l)
                norm(2 * l + 5)
                ffn(l + LAYERS, 2 * l + 5, l, BASE2, PER2, MIX2_TILES)
            norm(8)

        @block.scalar
        def _(sc):
            def eps(rows, name="eps"):
                return C(name, rows)

            def rsqrt(out_i, psum, rows, scale, eps_name, ln_sig, ln_at, rs_sig, rs_free):
                sc.activation(lnv[rows, out_i, :], psum[rows, :], ACT.Ln, bias=eps(rows, eps_name), scale=scale)\
                    .then_inc(ln_sig.sem, 1)
                sc.wait_ge(*ln_sig(*ln_at))
                if rs_free is not None:
                    sc.wait_ge(*rs_free)
                sc.activation(rstd[rows, out_i, :], lnv[rows, out_i, :], ACT.Exp, scale=-0.5)\
                    .then_inc(rs_sig.sem, 1)

            ALL = slice(0, P)

            def norm(n):
                for j in range(ND):
                    sc.wait_ge(*x_ready(n, j + 1))
                    sc.activation(h[:, j, :], x[:, j, :], ACT.Square).then_inc(n_sq.sem, 1)
                sc.wait_ge(*n_ss(n, 1))
                rsqrt(0, bank[0], ALL, 1.0 / D, "eps", n_ln, (n, 1), n_rs, None)

            def ffn(nf):
                def gate(g, r, it):
                    sc.wait_ge(gu_mm.sem, nf * gu_mm.per + it * 6 + (2 * g + 1))
                    sc.wait_ge(act_ready.sem, nf * FB + it * RING + (act_ready.start + g - 2))
                    sc.activation(sil[:, r, :], bank[r][:, :], ACT.Silu).then_inc(silu.sem, 1)

                with sc.Fori(0, 7) as it:
                    for r in range(3):
                        gate(r, r, it)
                gate(FB - 1, 0, 0)

            def exps(s, l, u):
                for t in range(NT):
                    sc.wait_ge(*s["maxed"](l, NT * u + t + 1))
                    if u >= 2 and t == 0:
                        sc.wait_ge(*s["turned"](l, NT * (u - 1)))
                    c = 4 * (u % 2) + t
                    sc.activation(prob[:, u % 2, PS0[t]:PS0[t] + (t + 1) * P], bank[3 + t][:, 0:(t + 1) * P], ACT.Exp,
                                  bias=small[:, 16 + c:17 + c], accum_out=small[:, 24 + c:25 + c])\
                        .then_inc(s["exped"].sem, 1)

            def turned_copies(s, l, u):
                if u >= 2:
                    sc.wait_ge(*s["pv"](l, u - 1))
                for st in range(NT):
                    c = NT * u + st
                    sc.wait_ge(*s["turned"](l, c + 1))
                    sc.activation(probT[:, u % 2, PT0[st]:PT0[st] + (NT - st) * P],
                                  bank[(7, 2)[c % 2]][:, 0:(NT - st) * P], ACT.Copy).then_inc(s["turned_out"].sem, 1)

            def mixer1(l):
                def lat_rstd(i):
                    sc.wait_ge(*lat_ss(l, i + 1))
                    rsqrt(i, bank[3 + i], ALL, (1 / 256, 1 / 128)[i], "eps", lat_ln, (l, i + 1), lat_rs, None)

                for g in range(3):
                    sc.wait_ge(*z_mm(l, g + 1))
                    dst = m1["qlat"][:, g, :] if g < 2 else m1["kvlat"]
                    sc.activation(m1["sqlat"][:, g, :], bank[g][:, :], ACT.Square).then_inc(z_sq.sem, 1)
                    sc.activation(dst, bank[g][:, :], ACT.Copy).then_inc(z_out.sem, 1)
                sc.wait_ge(*z_mm(l, 4))
                sc.activation(m1["sqkr"][64:96, :], bank[0][64:96, :], ACT.Square).then_inc(hd_sq.sem, 1)
                sc.activation(m1["krope"][64:96, :], bank[0][64:96, :], ACT.Copy).then_inc(z_out.sem, 1)
                for c in range(2):
                    sc.wait_ge(*z_mm(l, 5 + c))
                    sc.activation(m1["v"][:, :, c * P:c * P + P],
                                  bank[(4 + c) % 3][:, :].rearrange("p (m n) -> p m n", m=NT), ACT.Copy)\
                        .then_inc(z_out.sem, 1)
                    lat_rstd(c)
                for g in range(6, 10):
                    sc.wait_ge(*z_mm(l, g + 1))
                    dst = m1["u"][:, g - 6, :] if g < 8 else m1["pin"][:, g - 8, 16:16 + T]
                    sc.activation(dst, bank[g % 3][:, :], ACT.Copy).then_inc(z_out.sem, 1)
                sc.wait_ge(*sg_ss(l, 1))
                sc.activation(small[:, 4:8], small[:, 0:4], ACT.Ln, bias=eps(ALL), scale=1 / 256).then_inc(sg_ln.sem, 1)
                sc.wait_ge(*sg_ln(l, 1))
                sc.activation(small[:, 8:12], small[:, 4:8], ACT.Exp, scale=-0.5).then_inc(sg_rs.sem, 1)

                def head_rstd(i):
                    sc.wait_ge(*hd_ss(l, i + 1))
                    rsqrt(i % 2, bank[3 + i % 2], slice(0, QK1), 1.0 if i < 4 else 1 / QK1,
                          "eps96" if i < 4 else "eps", hd_ln, (l, i + 1), hd_rs,
                          hd_n(l, i - 1) if i >= 2 else lat_n(l, 3))

                for i in range(8):
                    g = 10 + i
                    rows = slice(0, QK1) if i < 4 else slice(0, NOPE1)
                    sc.wait_ge(*z_mm(l, g + 1))
                    if i >= 2:
                        sc.wait_ge(*hd_ss(l, i - 1))
                    sc.activation(sq[rows, i % 2, :], bank[g % 3][rows, :], ACT.Square).then_inc(hd_sq.sem, 1)
                    sc.activation((m1["qh"] if i < 4 else m1["kh"])[rows, i % 4, :], bank[g % 3][rows, :], ACT.Copy)\
                        .then_inc(z_out.sem, 1)
                    if i >= 1:
                        head_rstd(i - 1)
                head_rstd(7)
                for m in range(NT):
                    sc.wait_ge(*z_mm(l, 19 + m))
                    sc.activation(m1["V"][:, m, :], bank[(18 + m) % 3][:, :], ACT.Copy).then_inc(z_out.sem, 1)
                for b in range(2):
                    sc.wait_ge(*sg_g(l, b + 1))
                    sc.activation(h[:, 4 + b, :], m1["mix"][:, 4 + b, :], ACT.Square).then_inc(mx_sq.sem, 1)
                for b in range(2):
                    col = par[:, PAR1["pool_scale"]][:, b:b + 1]
                    sc.wait_ge(*pl_mm(l, b + 1))
                    sc.activation(h[:, 6 + b, :], bank[5 + b][:, :], ACT.Square, scale=col).then_inc(mx_sq.sem, 1)
                    sc.activation(m1["mix"][:, 6 + b, :], bank[5 + b][:, :], ACT.Copy, scale=col)\
                        .then_inc(pl_o.sem, 1)

                def mix_rstd(i):
                    sc.wait_ge(*mx_ss(l, i + 1))
                    rsqrt(i % 2, bank[(3, 4, 3)[i]], ALL, (1 / 256, 1 / 256, 1 / 512)[i], "eps", mx_ln, (l, i + 1),
                          mx_rs, hd_n(l, 8) if i < 2 else mx_n(l, 2))

                mix_rstd(0)
                mix_rstd(1)
                for u in range(HEADS1 + 1):
                    if u < HEADS1:
                        exps(at1, l, u)
                    if u >= 1:
                        w = u - 1
                        turned_copies(at1, l, w)
                        sc.wait_ge(*at1["pv"](l, w + 1))
                        sc.activation(h[:, w, :], bank[w % 2][:, :], ACT.Square).then_inc(mx_sq.sem, 1)
                        sc.activation(m1["mix"][:, w, :], bank[w % 2][:, :], ACT.Copy).then_inc(o1_out.sem, 1)
                mix_rstd(2)

            def mixer2(l):
                def copy_out(key):
                    name, i = key
                    g = Y[key][0]
                    b = y_bank(g)
                    sc.wait_ge(*y_mm(l, g + 1))
                    tok = b[:, :].rearrange("p (m n) -> p m n", m=NT)
                    cols = slice(i * P, i * P + P)
                    if name == "hf":
                        sc.activation(m2["hk"][:, i, :], b[:, :], ACT.Sigmoid, scale=-1.0).then_inc(hf_s.sem, 1)
                        last = sc.activation(m2["hlf"][:, i, :], b[:, :], ACT.Sigmoid)
                    elif name == "glr":
                        last = sc.activation(ropec[0:16, :], b[0:16, :], ACT.Copy)
                    elif name == "ngate":
                        last = sc.activation(m2["gate"].rearrange("p m n -> p (m n)"), b[:, 0:NT * 24], ACT.Sigmoid)
                    elif name == "gdec":
                        col = par[:, PAR2["gla_b"]][:, i:i + 1]
                        sc.activation(m2["gk"][:, i, :], b[:, :], ACT.Abs, bias=col).then_inc(gl_a.sem, 1)
                        last = sc.activation(m2["glf"][:, i, :], b[:, :], ACT.Identity, bias=col)
                    elif name in ("hq", "hog", "gog"):
                        last = sc.activation(m2[{"hq": "hq", "hog": "hy", "gog": "gy"}[name]][:, i, :], b[:, :],
                                             ACT.Silu)
                    elif name in ("hi", "gv", "nv"):
                        last = sc.activation(m2[{"hi": "hv"}.get(name, name)][:, :, cols], tok, ACT.Copy)
                    elif name in ("gq", "nq"):
                        last = sc.activation(m2[name][:, i, :], b[:, :], ACT.Copy, scale=0.125)
                    else:
                        if name == "gk":
                            sc.wait_ge(*gl_d(l, i + 1))
                        dst = {"gk": "gk", "nkc": "ck", "nks": "ks", "nkw": "kw", "nvc": "cv"}[name]
                        last = sc.activation(m2[dst][:, i, :], b[:, :], ACT.Copy)
                    last.then_inc(y_out.sem, 1)

                for key in YKEYS[:24]:
                    copy_out(key)
                for i in range(2):
                    sc.wait_ge(*gl_a(l, i + 1))
                    sc.activation(m2["gk"][:, i, :], m2["gk"][:, i, :], ACT.Exp, scale=-1.0).then_inc(gl_e.sem, 1)
                for i in range(4):
                    sc.wait_ge(*hf_f(l, i + 1))
                    sc.activation(m2["hlf"][:, i, :], m2["hlf"][:, i, :], ACT.Ln).then_inc(hf_l.sem, 1)
                for i in range(2):
                    sc.wait_ge(*gl_e(l, i + 1))
                    sc.activation(m2["gk"][:, i, :], m2["gk"][:, i, :], ACT.Ln, bias=1.0).then_inc(gl_l.sem, 1)

                def out_copy(hd):
                    if hd >= 2:
                        sc.wait_ge(*lo_ss(l, hd - 1))
                        sc.wait_ge(*lo_y(l, hd - 1))
                    sc.wait_ge(*ln_pv(l, hd + 1))
                    sc.activation(sq[:, hd % 2, :], bank[7][:, :], ACT.Square).then_inc(lo_sq.sem, 1)
                    sc.activation(m2["ob"][:, hd % 2, :], bank[7][:, :], ACT.Copy).then_inc(lo_o.sem, 1)

                def out_rstd(hd):
                    sc.wait_ge(*lo_ss(l, hd + 1))
                    rsqrt(hd % 2, bank[7], ALL, 1 / P, "eps", lo_ln, (l, hd + 1), lo_rs,
                          lo_n(l, hd - 1) if hd >= 2 else None)

                for u, q, k, lf, heads in LIN:
                    if u >= 4:
                        for head, _, _ in LIN[u - 1][4]:
                            out_copy(head)
                            out_rstd(head)
                    for v in range(10):
                        m = (1 << v) >> 1
                        if v >= 1:
                            if v == 1:
                                sc.wait_ge(*(hf_l(l, u + 1) if u < 4 else gl_f(l, u - 3)))
                                if u > 0:
                                    sc.wait_ge(*ln_q(l, 9 * u))
                            else:
                                sc.wait_ge(*ln_p(l, 8 * u + v - 1))
                                sc.wait_ge(*ln_q(l, 9 * u + v - 1))
                            sc.activation(compact(m2["Eq"], m), halves(lf, m, 1), ACT.Exp).then_inc(ln_e.sem, 1)
                        if v >= 2:
                            sc.wait_ge(*ln_x(l, 8 * u + v - 1))
                            if 8 * u + v - 2 > 0:
                                sc.wait_ge(*ln_k(l, 8 * u + v - 2))
                            sc.activation(compact(m2["Ek"], m), halves(m2["X"], m, 0), ACT.Exp).then_inc(ln_f.sem, 1)
                        if (u, v) in FILL:
                            copy_out(FILL[u, v])
                        if 0 < u < 4 and v == 3:
                            out_copy(u - 1)
                        if 0 < u < 4 and v == 5:
                            out_rstd(u - 1)
                for head, _, _ in LIN[-1][4]:
                    out_copy(head)
                    out_rstd(head)

                for kv, (b1, b2) in enumerate(((4, 5), (6, 3))):
                    sc.wait_ge(*ch_mm(l, 2 * kv + 2))
                    sc.activation(small[:, 40 + kv:41 + kv], bank[b2][:, 0:1], ACT.Copy).then_inc(ch_b.sem, 1)
                    sc.wait_ge(*ch_b(l, kv + 1))
                    sc.activation(m2["hid"][:, 62 * kv:62 * kv + 62], bank[b1][:, 0:62], ACT.Gelu_apprx_tanh,
                                  bias=small[:, 40 + kv:41 + kv]).then_inc(ch_g.sem, 1)
                sc.wait_ge(*cc_mm(l, 1))
                sc.activation(m2["kc"], bank[0][:, 0:62], ACT.Copy).then_inc(cc_o.sem, 1)
                sc.wait_ge(*cc_mm(l, 2))
                sc.activation(m2["vc"][0:NCMP, :], bank[1][0:NCMP, 0:P], ACT.Copy).then_inc(cc_o.sem, 1)
                for hd in range(9):
                    if hd < 8:
                        sc.wait_ge(*cs_d(l, hd + 1))
                        sc.activation(cm[:, hd % 2, :], cm[:, hd % 2, :], ACT.Exp).then_inc(cs_e.sem, 1)
                    if hd >= 1:
                        sc.wait_ge(*cs_t(l, hd))
                        sc.activation(m2["cmpT"][0:NCMP, hd - 1, :], bank[4 + (hd - 1) % 2][0:NCMP, :], ACT.Copy)\
                            .then_inc(cs_o.sem, 1)
                for u in range(17):
                    if u < 16:
                        exps(at2, l, u)
                    if u >= 1:
                        w = u - 1
                        turned_copies(at2, l, w)
                        if w % 4 == 3:
                            sc.wait_ge(*at2["pv"](l, w + 1))
                            sc.activation(m2["nq"][:, w // 4, :], bank[(w // 4) % 2][:, :], ACT.Copy)\
                                .then_inc(no_y.sem, 1)
                with sc.Fori(0, 4) as it:
                    for r in range(6):
                        sc.wait_ge(mg_mm.sem, l * 24 + it * 6 + (r + 1))
                        sc.wait_ge(br_m.sem, l * 24 + it * 6 + (br_m.start + r - 5))
                        sc.activation(m2["sig"][:, r, :], bank[r % 3][:, :], ACT.Sigmoid).then_inc(mg_s.sem, 1)

            sc.wait_ge(s_const, 16)
            sc.sem_inc(silu.sem, silu.start)
            sc.sem_inc(mg_s.sem, mg_s.start)
            R1 = slice(64, 96)
            sc.wait_ge(s_rope, 9)
            sc.activation(m1["cos"][R1, :], m1["sin"][R1, :], ACT.Sin, scale=0.5).then_inc(s_ropea, 1)
            sc.wait_ge(s_ropea, 1)
            sc.activation(m1["sin"][R1, :], m1["sin"][R1, :], ACT.Sin).then_inc(s_ropea, 1)
            sc.wait_ge(lb_s, 3)
            sc.activation(lbt[:, 0:8], lbt[:, 0:8], ACT.Exp).then_inc(lb_e, 1)
            with sc.Fori(0, LAYERS) as l:
                norm(2 * l)
                mixer1(l)
                norm(2 * l + 1)
                ffn(l)
            with sc.Fori(0, LAYERS) as l:
                norm(2 * l + 4)
                mixer2(l)
                norm(2 * l + 5)
                ffn(l + LAYERS)
            norm(8)

        @block.vector
        def _(ve):
            def mul(out, a, b):
                return ve.tensor_tensor(out, a, b, ALU.mult)

            def add(out, a, b):
                return ve.tensor_tensor(out, a, b, ALU.add)

            def norm(n, nf, gains):
                ve.wait_ge(*n_rs(n, 1))
                if nf is not None:
                    ve.wait_ge(*s_par(nf, 16))
                for j in range(ND):
                    ve.scalar_tensor_tensor(h[:, j, :], x[:, j, :], gains[:, j:j + 1], rstd[:, 0, :],
                                            ALU.mult, ALU.mult).then_inc(h_ready.sem, 1)

            def ffn(nf):
                def hidden(g, r, it):
                    ve.wait_ge(silu.sem, nf * FB + it * RING + (silu.start + g + 1))
                    ve.wait_ge(gu_mm.sem, nf * gu_mm.per + it * 6 + (2 * g + 2))
                    out = act[:, g, :] if isinstance(it, int) else \
                        act[:, bass.ds(it * 3 + g, 1), :].rearrange("p a t -> p (a t)")
                    mul(out, sil[:, r, :], bank[3 + r][:, :]).then_inc(act_ready.sem, 1)

                with ve.Fori(0, 7) as it:
                    for r in range(3):
                        hidden(r, r, it)
                hidden(FB - 1, 0, 0)
                ve.wait_ge(*down_mm(nf, FB))
                for j in range(ND):
                    add(x[:, j, :], x[:, j, :], bank[j][:, :]).then_inc(x_ready.sem, 1)

            def w_out(nf):
                for j in range(ND):
                    ve.wait_ge(*wo_mm(nf, j + 1))
                    add(x[:, j, :], x[:, j, :], bank[j][:, :]).then_inc(x_ready.sem, 1)

            def maxima(s, l, u):
                for t in range(NT):
                    ve.wait_ge(*s["scores"](l, NT * u + t + 1))
                    c = 4 * (u % 2) + t
                    ve.reduce_max(small[:, 16 + c:17 + c], bank[3 + t][:, 0:(t + 1) * P], AX_X, negate=True)\
                        .then_inc(s["maxed"].sem, 1)

            def scale(s, l, u, gates):
                ve.wait_ge(*s["exped"](l, NT * (u + 1)))
                c = 4 * (u % 2)
                inv = small[:, 32 + c:36 + c]
                ve.reciprocal(inv, small[:, 24 + c:28 + c]).then_inc(s["recip"].sem, 1)
                ve.wait_ge(*s["recip"](l, u + 1))
                if gates is not None:
                    mul(inv, inv, gates).then_inc(s["gated"].sem, 1)
                    ve.wait_ge(*s["gated"](l, u + 1))
                for t in range(NT):
                    v = prob[:, u % 2, PS0[t]:PS0[t] + (t + 1) * P]
                    ve.tensor_scalar(v, v, small[:, 32 + c + t:33 + c + t], None, ALU.mult)\
                        .then_inc(s["scaled"].sem, 1)

            def mixer1(l):
                def gain(name, j, rows=slice(0, P)):
                    return par[rows, PAR1[name]][:, j:j + 1]

                def normed(out, src, g, rs, sig=None):
                    i = ve.scalar_tensor_tensor(out, src, g, rs, ALU.mult, ALU.mult)
                    if sig is not None:
                        i.then_inc(sig.sem, 1)
                    return i

                ve.wait_ge(*lat_rs(l, 1))
                for c in range(2):
                    if c == 0:
                        ve.wait_ge(*z_out(l, 2))
                    normed(m1["qlat"][:, c, :], m1["qlat"][:, c, :], gain("g_q", c), rstd[:, 0, :], lat_n)
                ve.wait_ge(*lat_rs(l, 2))
                normed(m1["kvlat"], m1["kvlat"], gain("g_kv", 0), rstd[:, 1, :], lat_n)
                ve.wait_ge(*z_out(l, 6))
                mul(sgt, m1["v"], m1["v"]).then_inc(sg_q.sem, 1)
                ve.wait_ge(*sg_q(l, 1))
                ve.tensor_reduce(small[:, 0:4], sgt, AX_X, ALU.add).then_inc(sg_ss.sem, 1)
                for hd in range(4):
                    w = par[:, PAR1["w_sp"]][:, hd * P:hd * P + P]
                    mul(w, w, C("causalT")).then_inc(sg_w.sem, 1)

                def head_norm(i):
                    ve.wait_ge(*hd_rs(l, i + 1))
                    ve.wait_ge(*z_out(l, 11 + i))
                    if i < 4:
                        v = m1["qh"][0:QK1, i, :]
                        normed(v, v, gain("g_qh", 0, slice(0, QK1)), rstd[0:QK1, i % 2, :], hd_n)
                    else:
                        v = m1["kh"][0:64, i - 4, :]
                        normed(v, v, gain("g_kh", 0, slice(0, 64)), rstd[0:64, i % 2, :])
                        normed(m1["kh"][64:96, i - 4, :], m1["krope"][64:96, :], gain("g_kh", 0, slice(64, 96)),
                               rstd[64:96, i % 2, :], hd_n)

                def head_rope(i):
                    ve.wait_ge(*hd_rot(l, i + 1))
                    r1 = slice(64, 96)
                    if i > 0:
                        ve.wait_ge(*hd_r(l, i))
                    v = (m1["qh"] if i < 4 else m1["kh"])[r1, i % 4, :]
                    mul(m1["tb"][r1, :], bank[5 + i % 2][r1, :], m1["sin"][r1, :]).then_inc(hd_t.sem, 1)
                    mul(v, v, m1["cos"][r1, :]).then_inc(hd_t.sem, 1)
                    ve.wait_ge(*hd_t(l, 2 * i + 2))
                    add(v, v, m1["tb"][r1, :]).then_inc(hd_r.sem, 1)

                for i in range(8):
                    head_norm(i)
                    if i >= 1:
                        head_rope(i - 1)
                head_rope(7)

                ve.wait_ge(*sg_rs(l, 1))
                for m in range(NT):
                    ve.scalar_tensor_tensor(m1["v"][:, m, :], m1["v"][:, m, :], small[:, 8 + m:9 + m],
                                            par[:, PAR1["g_sgu"]], ALU.mult, ALU.mult).then_inc(sg_v.sem, 1)

                steps = [0]

                def step(i):
                    steps[0] += 1
                    i.then_inc(pw.sem, 1)
                    ve.wait_ge(*pw(l, steps[0]))

                A, B = m1["win_a"], m1["win_b"]
                W = T + 16
                low, high = slice(0, 64), slice(64, P)
                step(ve.memset(m1["pin"][:, :, 0:16], 0.0))
                ve.wait_ge(*z_out(l, 10))
                for b in range(2):
                    p_ = m1["pin"][:, b, :]
                    if b > 0:
                        ve.wait_ge(*pl_m(l, b))
                    step(add(A[:, 1:W], p_[:, 1:W], p_[:, 0:W - 1]))
                    if b == 0:
                        step(add(B[high, 3:W], A[high, 3:W], A[high, 1:W - 2]))
                    else:
                        step(add(B[:, 3:W], A[:, 3:W], A[:, 1:W - 2]))
                        step(add(A[:, 7:W], B[:, 7:W], B[:, 3:W - 4]))
                        step(add(B[high, 15:W], A[high, 15:W], A[high, 7:W - 8]))
                    step(ve.tensor_copy(B[low, 16:W], A[low, 16:W]))
                    step(ve.scalar_tensor_tensor(m1["win_m"][:, b, :], B[:, 16:W], C("invwin")[:, b:b + 1],
                                                 p_[:, 16:W], ALU.mult, ALU.subtract))
                    step(mul(A[:, 0:16], B[:, 16:32], C("invcount")[:, 16 * b:16 * b + 16]))
                    ve.tensor_tensor(m1["win_m"][:, b, 0:16], A[:, 0:16], p_[:, 16:32], ALU.subtract)\
                        .then_inc(pl_m.sem, 1)
                assert steps[0] == pw.per, steps[0]

                for b in range(2):
                    ve.wait_ge(*sg_mm(l, b + 1))
                    v = m1["mix"][:, 4 + b, :]
                    add(v, bank[3 + b][:, :], par[:, PAR1["b_sp"]][:, b * T:b * T + T]).then_inc(sg_z.sem, 1)
                    ve.wait_ge(*sg_z(l, b + 1))
                    mul(v, v, m1["u"][:, b, :]).then_inc(sg_g.sem, 1)

                def mix_norm(i):
                    ve.wait_ge(*mx_rs(l, i + 1))
                    if i == 1:
                        ve.wait_ge(*pl_o(l, 2))
                    for c in ((4, 5), (6, 7), (0, 1, 2, 3))[i]:
                        v = m1["mix"][:, c, :]
                        normed(v, v, gain("g_out", c), rstd[:, i % 2, :], mx_n)

                mix_norm(0)
                mix_norm(1)
                for u in range(HEADS1 + 1):
                    if u >= 1:
                        scale(at1, l, u - 1, None)
                    if u < HEADS1:
                        maxima(at1, l, u)
                ve.wait_ge(*o1_out(l, HEADS1))
                mix_norm(2)
                w_out(l)

            def mixer2(l):
                for n in range(2):
                    ve.tensor_copy(lbt[:, 32 + 4 * n:36 + 4 * n], lbt[:, bass.ds(l * 4 + (16 + 8 * n), 4)])\
                        .then_inc(lb_l.sem, 1)
                ve.wait_ge(*lb_l(l, 2))
                for i in range(4):
                    lb, om = lbt[:, 32 + i:33 + i], lbt[:, 36 + i:37 + i]
                    kk, f = m2["hk"][:, i, :], m2["hlf"][:, i, :]
                    ve.wait_ge(*y_out(l, i + 1))
                    ve.tensor_scalar(kk, kk, om, None, ALU.mult).then_inc(hf_k.sem, 1)
                    ve.tensor_scalar(f, f, om, lb, ALU.mult, ALU.add).then_inc(hf_m.sem, 1)
                    ve.wait_ge(*hf_m(l, i + 1))
                    ve.tensor_scalar(f, f, 1e-19, None, ALU.max).then_inc(hf_f.sem, 1)
                for i in range(2):
                    f = m2["glf"][:, i, :]
                    ve.wait_ge(*gl_l(l, i + 1))
                    ve.scalar_tensor_tensor(f, f, 0.0, m2["gk"][:, i, :], ALU.min, ALU.subtract)\
                        .then_inc(gl_d.sem, 1)
                    ve.wait_ge(*gl_d(l, i + 1))
                    ve.tensor_scalar(f, f, 1 / 16, None, ALU.mult).then_inc(gl_f.sem, 1)

                def place(v, group0, heads):
                    for n, (hd, _, _) in enumerate(heads):
                        g = group0 + v * len(heads) + n
                        b = bank[3 + g % 4]
                        s = ST[hd % 2]
                        if v == 0 and hd >= 2:
                            ve.wait_ge(*ln_pv(l, hd - 1))
                        ve.wait_ge(*ln_mm(l, g + 1))
                        if g > 0:
                            ve.wait_ge(*ln_st(l, g))
                        if v < 8:
                            mask = C("levels")[:, v * P:v * P + P].unsqueeze(1).broadcast_to([P, NT, P])
                            src = b[:, :].rearrange("p (a b) -> p a b", a=NT)
                            if v == 0:
                                last = mul(diag4(hd % 2), src, mask)
                            else:
                                ve.memset(small[:, 60:61], 0.0)
                                last = ve.copy_predicated(diag4(hd % 2), mask.bitcast(U32), src)
                        elif v == 8:
                            ve.tensor_copy(s[:, 0, P:2 * P], b[:, 0:P])
                            last = ve.tensor_copy(s[:, 2, 3 * P:T], b[:, P:2 * P])
                        else:
                            last = ve.tensor_copy(s[:, 0:2, 2 * P:T],
                                                  b[:, :].rearrange("p (a b) -> p a b", a=2))
                        last.then_inc(ln_st.sem, 1)

                def lin_out(hd):
                    ve.wait_ge(*lo_rs(l, hd + 1))
                    ve.wait_ge(*lo_o(l, hd + 1))
                    o = m2["ob"][:, hd % 2, :]
                    g = par[:, PAR2["g_hg" if hd < 4 else "g_gla"]][:, hd % 4:hd % 4 + 1]
                    ve.scalar_tensor_tensor(o, o, g, rstd[:, hd % 2, :], ALU.mult, ALU.mult).then_inc(lo_n.sem, 1)
                    ve.wait_ge(*lo_n(l, hd + 1))
                    y = lin_gate(hd)
                    mul(y, y, o).then_inc(lo_y.sem, 1)

                group0 = 0
                for u, q, k, lf, heads in LIN:
                    X = m2["X"]
                    if u >= 4:
                        for hd, _, _ in LIN[u - 1][4]:
                            lin_out(hd)
                    ve.memset(X, 0.0).then_inc(ln_x0.sem, 1)
                    for v in range(1, 10):
                        m = 1 << (v - 1)
                        qo, ko = qsl[:, v % 2, :], ksl[:, v % 2, :]
                        ve.wait_ge(*ln_e(l, 9 * u + v))
                        if v == 1 and u >= 4:
                            ve.wait_ge(*y_out(l, Y["gq", u - 4][0] + 1))
                        elif v == 1:
                            ve.wait_ge(*y_out(l, Y["hq", u][0] + 1))
                        mul(halves(qo, m, 1), halves(q, m, 1), compact(m2["Eq"], m)).then_inc(ln_q.sem, 1)
                        if v >= 2:
                            ve.wait_ge(*ln_f(l, 8 * u + v - 1))
                            mul(halves(ko, m, 0), halves(k, m, 0), compact(m2["Ek"], m)).then_inc(ln_k.sem, 1)
                        if v <= 8:
                            if v == 1:
                                ve.wait_ge(*ln_x0(l, u + 1))
                            else:
                                ve.wait_ge(*ln_p(l, 8 * u + v - 1))
                            add(halves(X, m, 0), halves(X, m, 0), ends(lf, m, 1)).then_inc(ln_x.sem, 1)
                            ve.wait_ge(*ln_x(l, 8 * u + v))
                            add(halves(lf, m, 1), halves(lf, m, 1), ends(lf, m, 0)).then_inc(ln_p.sem, 1)
                        place(v - 1, group0, heads)
                        if 0 < u < 4 and v == 6:
                            lin_out(u - 1)
                    place(9, group0, heads)
                    group0 += 10 * len(heads)
                for hd, _, _ in LIN[-1][4]:
                    lin_out(hd)

                for i in range(7):
                    ve.wait_ge(*rp_mm(l, i + 1))
                    if i > 0:
                        ve.wait_ge(*rp_o(l, (1, 2, 3, 4, 8, 12)[i - 1]))
                    mul(ropes, bank[i % 2][:, :], C("sin2")).then_inc(rp_u.sem, 1)
                    mul(ropec, raw_block(i), C("cos2")).then_inc(rp_t.sem, 1)
                    ve.wait_ge(*rp_u(l, i + 1))
                    ve.wait_ge(*rp_t(l, i + 1))
                    if i < 4:
                        add(m2["nq"][:, i, :], ropec, ropes).then_inc(rp_o.sem, 1)
                        continue
                    dst = (m2["ck"], m2["ks"], m2["kw"])[i - 4]
                    for g in range(2):
                        src = slice(64 * g, 64 * g + 64)
                        add(dst[0:64, g, :], ropec[src, :], ropes[src, :]).then_inc(rp_o.sem, 1)
                        d = 1 if i == 4 else 0
                        add(dst[64:P, g, 0:T - d], ropec[src, d:T], ropes[src, d:T]).then_inc(rp_o.sem, 1)
                cv = m2["cv"]
                ve.tensor_copy(cv[0:64, 1, :], cv[64:P, 0, :]).then_inc(cv_o.sem, 1)
                ve.wait_ge(*cv_o(l, 1))
                ve.tensor_copy(cv[64:P, 0, 0:T - 1], cv[0:64, 0, 1:T]).then_inc(cv_o.sem, 1)
                ve.tensor_copy(cv[64:P, 1, 0:T - 1], cv[0:64, 1, 1:T]).then_inc(cv_o.sem, 1)

                def per_tile(a):
                    return a.unsqueeze(2).broadcast_to([P, NT, NCMP])

                for hd in range(8):
                    c = cm[:, hd % 2, :].rearrange("p (a b) -> p a b", a=NT)
                    if hd >= 2:
                        ve.wait_ge(*cs_t(l, hd - 1))
                    ve.wait_ge(*cs_mm(l, hd + 1))
                    add(cm[:, hd % 2, :], bank[2 + hd % 2][:, 0:NT * NCMP], C("negcmp")).then_inc(cs_m.sem, 1)
                    ve.wait_ge(*cs_m(l, hd + 1))
                    ve.reduce_max(small[:, 44:48], c, AX_X).then_inc(cs_x.sem, 1)
                    ve.wait_ge(*cs_x(l, hd + 1))
                    ve.tensor_tensor(c, c, per_tile(small[:, 44:48]), ALU.subtract).then_inc(cs_d.sem, 1)
                    ve.wait_ge(*cs_e(l, hd + 1))
                    ve.tensor_reduce(small[:, 48:52], c, AX_X, ALU.add).then_inc(cs_s.sem, 1)
                    ve.wait_ge(*cs_s(l, hd + 1))
                    ve.reciprocal(small[:, 52:56], small[:, 48:52]).then_inc(cs_r.sem, 1)
                    ve.wait_ge(*cs_r(l, hd + 1))
                    mul(small[:, 52:56], small[:, 52:56], C("validcmp")).then_inc(cs_v.sem, 1)
                    ve.wait_ge(*cs_v(l, hd + 1))
                    mul(small[:, 52:56], small[:, 52:56], m2["gate"][:, :, 3 * hd]).then_inc(cs_g.sem, 1)
                    ve.wait_ge(*cs_g(l, hd + 1))
                    mul(c, c, per_tile(small[:, 52:56])).then_inc(cs_p.sem, 1)

                for u in range(17):
                    if u >= 1:
                        w = u - 1
                        scale(at2, l, w, m2["gate"][:, :, 3 * (w // 2) + 1 + w % 2])
                    if u < 16:
                        maxima(at2, l, u)

                with ve.Fori(0, 4) as it:
                    for r in range(6):
                        j, b = r // 3, r % 3
                        ve.wait_ge(mg_s.sem, l * 24 + it * 6 + (mg_s.start + r + 1))
                        ve.wait_ge(br_mm.sem, l * 24 + it * 6 + (r + 1))
                        m = m2["m"][:, bass.ds(it * 2 + j, 1), :].rearrange("p a t -> p (a t)")
                        out = (m, ropec, ropes)[b]
                        mul(out, m2["sig"][:, r, :], bank[3 + r % 3][:, :]).then_inc(br_m.sem, 1)
                        ve.wait_ge(br_m.sem, l * 24 + it * 6 + (br_m.start + r + 1))
                        if b == 2:
                            ve.wait_ge(br_a.sem, l * 16 + it * 4 + (2 * j + 1))
                        if b > 0:
                            add(m, m, out).then_inc(br_a.sem, 1)
                        if b == 2:
                            ve.wait_ge(br_a.sem, l * 16 + it * 4 + (2 * j + 2))
                w_out(l + LAYERS)

            ve.sem_inc(act_ready.sem, act_ready.start)
            ve.sem_inc(br_m.sem, br_m.start)
            ve.sem_inc(h_ready.sem, h_ready.start)
            ve.wait_ge(s_x0, 16)
            for j in range(ND):
                ve.tensor_copy(x[:, j, :], arena[:, j * T:(j + 1) * T]).then_inc(x_ready.sem, 1)
            ve.memset(qsl[:, :, :], 0.0).then_inc(s_init, 1)
            ve.memset(ksl[:, :, :], 0.0).then_inc(s_init, 1)
            ve.wait_ge(s_init, 2)
            R1 = slice(64, 96)
            ang, turns, pf = m1["sin"][R1, :], m1["cos"][R1, :], m1["tb"][R1, :]
            ve.wait_ge(s_const, 16)
            ve.wait_ge(s_pos, 16)
            k = [0]

            def step(i):
                k[0] += 1
                i.then_inc(s_rope, 1)
                ve.wait_ge(s_rope, k[0])

            step(ve.tensor_copy(pf, m1["ta"][R1, :].bitcast(I32)))
            step(ve.tensor_scalar(ang, pf, C("invfreq", R1), None, ALU.mult))
            step(ve.tensor_scalar(turns, ang, 1 / (2 * math.pi), 12582912.0, ALU.mult, ALU.add))
            step(ve.tensor_scalar(turns, turns, 12582912.0, None, ALU.subtract))
            for part in TWO_PI_PARTS:
                step(ve.scalar_tensor_tensor(ang, turns, -part, ang, ALU.mult, ALU.add))
            step(ve.tensor_scalar(ang, ang, 3.1415925, -3.1415925, ALU.min, ALU.max))
            a, b = C("lb")[:, 0:4], C("lb")[:, 4:8]
            ve.tensor_tensor(lbt[:, 8:12], a, b, ALU.max).then_inc(lb_s, 1)
            ve.wait_ge(lb_s, 1)
            ve.tensor_tensor(lbt[:, 0:4], a, lbt[:, 8:12], ALU.subtract).then_inc(lb_s, 1)
            ve.tensor_tensor(lbt[:, 4:8], b, lbt[:, 8:12], ALU.subtract).then_inc(lb_s, 1)
            ve.wait_ge(lb_e, 1)
            n = [3]

            def lb_step(i):
                n[0] += 1
                i.then_inc(lb_s, 1)
                ve.wait_ge(lb_s, n[0])

            lb_step(add(lbt[:, 8:12], lbt[:, 0:4], lbt[:, 4:8]))
            lb_step(ve.reciprocal(lbt[:, 12:16], lbt[:, 8:12]))
            lb_step(mul(lbt[:, 0:4], lbt[:, 0:4], lbt[:, 12:16]))
            lb_step(mul(lbt[:, 4:8], lbt[:, 4:8], lbt[:, 12:16]))
            lb_step(add(lbt[:, 8:12], lbt[:, 0:4], lbt[:, 4:8]))
            lb_step(ve.tensor_tensor(lbt[:, 16:20], lbt[:, 0:4], lbt[:, 0:4], ALU.subtract))
            lb_step(ve.tensor_tensor(lbt[:, 20:24], lbt[:, 8:12], lbt[:, 0:4], ALU.subtract))
            lb_step(ve.tensor_scalar(lbt[:, 24:32], lbt[:, 16:24], -1.0, 1.0, ALU.mult, ALU.add))
            ve.wait_ge(s_ropea, 2)
            step(mul(turns, turns, turns))
            step(ve.tensor_scalar(turns, turns, -2.0, 1.0, ALU.mult, ALU.add))
            with ve.Fori(0, LAYERS) as l:
                norm(2 * l, l, par[:, PAR1["g_in"]])
                mixer1(l)
                norm(2 * l + 1, None, par[:, PAR1["g_ffn"]])
                ffn(l)
            with ve.Fori(0, LAYERS) as l:
                norm(2 * l + 4, l + LAYERS, par[:, PAR2["g_in"]])
                mixer2(l)
                norm(2 * l + 5, None, par[:, PAR2["g_ffn"]])
                ffn(l + LAYERS)
            norm(8, None, C("gfinal"))


def parts_of_two_pi():
    out, rest = [], 2 * math.pi
    for _ in range(4):
        e = math.floor(math.log2(rest))
        q = 2.0 ** (e - 7)
        out.append(math.floor(rest / q) * q)
        rest -= out[-1]
    return out


TWO_PI_PARTS = parts_of_two_pi()


def constants(hg_lb, final_norm_g):
    c = np.zeros((P, NCONST), np.float32)
    i = np.arange(P)
    c[:, CONST["ident"]] = np.eye(P)
    c[:, CONST["ones"]] = 1
    c[:, CONST["negdiag"]] = np.where(i[None] > i[:, None], NEG, 0)
    c[:, CONST["causalT"]] = i[None] >= i[:, None]
    rot = np.zeros((P, P))
    for m in range(P):
        if m % 64 < 8:
            rot[m + 8, m] = -1
        elif m % 64 < 16:
            rot[m - 8, m] = 1
    c[:, CONST["rot2"]] = rot
    rot = np.zeros((P, QK1))
    for m in range(32):
        rot[64 + (m + 16) % 32, 64 + m] = -1 if m < 16 else 1
    c[:, CONST["rot1"]] = rot
    levels = [np.eye(P)]
    for m in LEVELS:
        same = i[:, None] // (2 * m) == i[None] // (2 * m)
        levels.append(same & (i[:, None] // m % 2 == 0) & (i[None] // m % 2 == 1))
    c[:, CONST["levels"]] = np.concatenate(levels, 1)
    t = np.arange(T)
    inv = np.float32(500000.0) ** (-np.arange(0, 16, 2, dtype=np.float32) / np.float32(16))
    ang = t.astype(np.float32)[None] * inv.astype(np.float32)[:, None]
    cos, sin = np.ones((P, T)), np.zeros((P, T))
    for m in range(P):
        if m % 64 < 16:
            cos[m], sin[m] = np.cos(ang[m % 8]), np.sin(ang[m % 8])
    c[:, CONST["cos2"]], c[:, CONST["sin2"]] = cos, sin
    ends = np.arange(NCMP) * 16 + 31
    neg = np.where(ends[None] <= t[:, None], 0, NEG).reshape(NT, P, NCMP)
    c[:, CONST["negcmp"]] = neg.transpose(1, 0, 2).reshape(P, -1)
    c[:, CONST["validcmp"]] = (t >= 31).reshape(NT, P).T
    wins = np.array([2, 4, 8, 16]).reshape(2, 2).repeat(64, 1)
    c[:, CONST["invwin"]] = 1 / wins.T
    count = np.minimum(np.arange(1, 17)[None, None], wins[:, :, None])
    c[:, CONST["invcount"]] = (1 / count).transpose(1, 0, 2).reshape(P, 32)
    f = np.float32(1) / (np.float32(10000.0) ** (np.arange(16, dtype=np.float32) / np.float32(16)))
    c[64:96, CONST["invfreq"]] = np.tile(f, 2)[:, None]
    c[:, CONST["eps"]] = EPS
    c[:, CONST["eps96"]] = EPS * QK1
    c[:, CONST["lb"]] = hg_lb.reshape(LAYERS, 4, P).transpose(2, 0, 1).reshape(P, 8)
    c[:, CONST["gfinal"]] = final_norm_g.reshape(ND, P).T
    return c


def column_tiles(w):
    k, n = w.shape
    nb = -(-n // P)
    full = np.zeros((k, nb * P), np.float32)
    full[:, :n] = w
    a = full.reshape(k // P, P, nb, P).transpose(2, 1, 0, 3).reshape(nb, P, k // P * P)
    return pad_tiles(a)


def pad_tiles(a):
    out = np.zeros((a.shape[0], P, TILE), np.float32)
    out[:, :, :a.shape[2]] = a
    return out


def ffn_tiles(gate, up, down):
    g, u = column_tiles(gate), column_tiles(up)
    return [np.stack([g, u], 1).reshape(2 * FB, P, TILE), down.reshape(FB, P, D)]


def stream1(w_in, w_q_up, w_kv_up, w_out, gate, up, down):
    rope = np.zeros((D, P), np.float32)
    rope[:, 64:96] = w_in[:, 384:416]
    q_up = w_q_up.reshape(2, P, 384).transpose(1, 0, 2).reshape(1, P, 768)
    kv = w_kv_up.reshape(P, HEADS1, 192)
    kv = np.concatenate([kv[:, :, :64].reshape(P, 256), kv[:, :, 64:].reshape(P, 512)], 1)[None]
    return np.concatenate([
        column_tiles(w_in[:, :384]), column_tiles(rope), column_tiles(w_in[:, 672:928]),
        column_tiles(w_in[:, 416:672]), column_tiles(w_in[:, 928:1184]), pad_tiles(q_up), pad_tiles(kv),
        column_tiles(w_out), np.zeros((1, P, TILE), np.float32), *ffn_tiles(gate, up, down)])


def stream2(w_in, w1_k, w1_v, branches, w_out, gate, up, down):
    sizes = dict(hq=512, hf=512, hi=512, hog=512, gq=256, gk=256, gv=512, glr=16, gog=512, nq=512, nkc=128,
                 nvc=128, nks=128, nvs=128, nkw=128, nvw=128, ngate=24, mgate=3072)
    s, at = {}, 0
    for name, n in sizes.items():
        s[name] = w_in[:, at:at + n]
        at += n
    out = [column_tiles(s["hf"]), column_tiles(np.concatenate([s["glr"], s["ngate"]], 1))]
    out += [column_tiles(s[n]) for n in ("hq", "hog", "gog", "hi", "gk", "gq", "gv", "nq", "nkc", "nks", "nkw",
                                         "nvc", "nvs", "nvw")]
    out += [w.reshape(2, 8, P, P).transpose(0, 2, 1, 3).reshape(2, P, TILE) for w in (w1_k, w1_v)]
    mg = column_tiles(s["mgate"]).reshape(3, ND, P, TILE)
    br = np.stack([w.reshape(4, P, ND, P).transpose(2, 1, 0, 3).reshape(ND, P, 512) for w in branches], 1)
    for i in range(0, ND, 2):
        out.append(mg[:, i:i + 2].transpose(1, 0, 2, 3).reshape(6, P, TILE))
        out.append(br[i:i + 2].reshape(3, 2, P, 512).transpose(0, 2, 1, 3).reshape(3, P, TILE))
    return np.concatenate(out + [column_tiles(w_out), *ffn_tiles(gate, up, down)])


def by_block(g):
    return g.reshape(-1, P).T


def params_of(layout, parts):
    out = np.zeros((P, NPAR), np.float32)
    for name, value in parts.items():
        sl = layout[name]
        out[:value.shape[0], sl] = value
    return out


def diagonal_blocks(w):
    out = np.zeros((P, 2, P), np.float32)
    for g in range(4):
        o = 64 * (g % 2)
        out[o:o + 64, g // 2, o:o + 64] = w[g]
    return out.reshape(P, 2 * P)


def kernel(**inputs):
    import concourse.bacc as bacc
    from concourse.bass_utils import run_bass_kernel_spmd

    a = {k: np.asarray(v) for k, v in inputs.items()}
    tiles, params = [], []
    for l in range(LAYERS):
        tiles.append(stream1(a["w_in"][l], a["w_q_up"][l], a["w_kv_up"][l], a["w_out"][l], a["w_gate"][l],
                             a["w_up"][l], a["w_down"][l]))
        b = a["b_spatial"][l].reshape(2, 2, 1, 1, P)
        params.append(params_of(PAR1, {
            "g_in": by_block(a["g_mix_norm"][l]), "g_q": by_block(a["g_q_lat"][l]),
            "g_kv": by_block(a["g_kv_lat"][l]), "g_qh": a["g_q_head"][l][:, None],
            "g_kh": a["g_k_head"][l][:, None], "pool_scale": by_block(a["pool_scale"][l]),
            "g_out": np.concatenate([by_block(a[n][l]) for n in ("g_out_mla", "g_out_sgu", "g_out_pool")], 1),
            "g_ffn": by_block(a["g_ffn_norm"][l]), "g_sgu": np.broadcast_to(a["g_sgu_v"][l], (P, 256)),
            "w_sp": a["w_spatial"][l].transpose(2, 0, 1).reshape(P, 4 * P),
            "b_sp": np.broadcast_to(b, (2, 2, 64, NT, P)).transpose(1, 2, 0, 3, 4).reshape(P, 2 * T),
            "w_pool": diagonal_blocks(a["w_pool"][l])}))
    for l in range(LAYERS):
        p = {k[:-2]: v[l] for k, v in a.items() if k.endswith("_2") and k != "final_norm_g_2"}
        tiles.append(stream2(p["w_in"], p["cmp_w1_k"], p["cmp_w1_v"],
                             (p["w_br_hg"], p["w_br_gla"], p["w_br_nsa"]), p["w_out"], p["w_ffn_gate"],
                             p["w_ffn_up"], p["w_ffn_down"]))
        params.append(params_of(PAR2, {
            "g_in": by_block(p["norm1_g"]), "g_hg": by_block(p["hg_norm_g"]), "gla_b": by_block(p["gla_b"]),
            "g_gla": by_block(p["gla_norm_g"]), "g_ffn": by_block(p["norm2_g"]), "w_gla": p["gla_w2"],
            "pos_k": p["cmp_pos_k"].reshape(16, P).T, "pos_v": p["cmp_pos_v"].reshape(16, P).T,
            "w2_k": np.concatenate([p["cmp_w2_k"]] * 2, 1), "w2_v": p["cmp_w2_v"]}))
    arrays = {
        "xT": a["x"][0].T.reshape(ND, P, T).transpose(1, 0, 2).reshape(P, ND * T),
        "pos": np.broadcast_to(a["positions"].astype(np.int32), (P, T)),
        "wstream": np.concatenate(tiles), "params": np.stack(params),
        "const": constants(a["hg_lb_2"], a["final_norm_g_2"])}
    arrays = {k: np.ascontiguousarray(v) for k, v in arrays.items()}
    assert arrays["wstream"].shape[0] == ALL_TILES
    nc = bacc.Bacc("TRN2", target_bir_lowering=False, num_devices=1)
    args = [nc.dram_tensor(k, v.shape, mybir.dt.from_np(v.dtype), kind="ExternalInput").ap()
            for k, v in arrays.items()]
    out = nc.dram_tensor("outT", (P, ND * T), F32, kind="ExternalOutput").ap()
    build(nc, *args, out)
    r = run_bass_kernel_spmd(nc, [arrays], core_ids=[0])
    y = r.results[0]["outT"]
    return y.reshape(P, ND, T).transpose(1, 0, 2).reshape(D, T).T.reshape(1, T, D)
```

```python
import math
from contextlib import ExitStack

import numpy as np
import concourse.bass as bass
from concourse import mybir

F32 = mybir.dt.float32
F32R = mybir.dt.float32r
I32 = mybir.dt.int32
U32 = mybir.dt.uint32
ACT = mybir.ActivationFunctionType
ALU = mybir.AluOpType
AX_X = mybir.AxisListType.X

P = 128
T = 512
NT = T // P
D = 1024
ND = D // P
LAYERS = 2
EPS = 1e-6
NEG = -1e30
TILE = 1024
RING = 3
FB = 22

MIX1_TILES = 21
MIX2_TILES = 87
FFN_TILES = 3 * FB
PER1 = MIX1_TILES + FFN_TILES
PER2 = MIX2_TILES + FFN_TILES
BASE2 = LAYERS * PER1
ALL_TILES = LAYERS * (PER1 + PER2)

NCMP = T // 16 - 1
LEVELS = [1, 2, 4, 8, 16, 32, 64]

HEADS1, QK1, NOPE1 = 4, 96, 64

def columns(spec):
    out, at = {}, 0
    for name, n in spec:
        out[name] = slice(at, at + n)
        at += n
    return out, at

CONST, NCONST = columns([
    ("ident", P), ("ones", P), ("negdiag", P), ("rot2", P), ("rot1", QK1), ("causalT", P),
    ("levels", 8 * P), ("cos2", T), ("sin2", T), ("negcmp", NT * NCMP), ("invcount", 32), ("invwin", 2),
    ("invfreq", 1), ("eps", 1), ("eps96", 1), ("validcmp", NT), ("lb", 8), ("gfinal", ND)])
PAR1, NPAR1 = columns([
    ("g_in", ND), ("g_q", 2), ("g_kv", 1), ("g_qh", 1), ("g_kh", 1), ("pool_scale", 2), ("g_out", ND),
    ("g_ffn", ND), ("g_sgu", 256), ("w_sp", 4 * P), ("b_sp", 2 * P), ("w_pool", 256)])
PAR2, NPAR2 = columns([
    ("g_in", ND), ("g_hg", 4), ("gla_b", 2), ("g_gla", 4), ("g_ffn", ND), ("w_gla", 256),
    ("pos_k", 16), ("pos_v", 16), ("w2_k", P), ("w2_v", 64)])
NPAR = max(NPAR1, NPAR2)


class Signal:

    def __init__(self, sem, per, start=0):
        self.sem, self.per, self.start = sem, per, start

    def __call__(self, n, k):
        return self.sem, n * self.per + (self.start + k)


def build(nc, xT, pos, wstream, params, const, outT):
    ctx = ExitStack()
    with ctx:
        def sb(name, shape, dt=F32):
            return ctx.enter_context(nc.sbuf_tensor(name, shape, dt))

        def signal(name, per, start=0):
            return Signal(ctx.enter_context(nc.semaphore(name)), per, start)

        x = sb("x", [P, ND, T])
        ring = sb("ring", [P, RING, TILE])
        cst = sb("cst", [P, NCONST])
        par = sb("par", [P, NPAR])
        rstd = sb("rstd", [P, 2, T])
        small = sb("small", [P, 64])
        lbt = sb("lbt", [P, 40])
        rope2 = sb("rope2", [P, 2, T])
        rope1 = sb("rope1", [P, 2, T])
        MIX = 26032
        ARENA = MIX + ND * T + 4 * TILE
        with nc.sbuf_tensor("h", [P, ND, T], F32) as h, nc.sbuf_tensor("arena", [P, ARENA], F32) as arena:
            pass
        h_hi = sb("h_hi", [P, ND, T], F32R)
        act_hi = sb("act_hi", [P, FB, T], F32R)
        act_lo = sb("act_lo", [P, FB, T], F32R)
        sil = sb("sil", [P, 3, T])
        sb("arena_gap", [P, MIX - (2 * FB + 3) * T])
        h_lo = sb("h_lo", [P, ND, T], F32R)
        w_hi = sb("w_hi", [P, 2, TILE], F32R)
        w_lo = sb("w_lo", [P, 2, TILE], F32R)
        bank = [ctx.enter_context(nc.psum_tensor(f"bank{i}", [P, T], F32)) for i in range(8)]

        def C(name, rows=slice(0, P)):
            return cst[rows, CONST[name]]

        def view(off, *dims):
            n = int(np.prod(dims))
            assert off + n <= MIX, (off, dims)
            a = arena[:, off:off + n]
            if len(dims) == 1:
                return a
            if len(dims) == 2:
                return a.rearrange("p (a b) -> p a b", a=dims[0])
            return a.rearrange("p (a b c) -> p a b c", a=dims[0], b=dims[1])

        W0 = 18848
        prob = view(W0, 2, 1280)
        probT = view(W0 + 2560, 2, 1280)
        ST = [view(W0 + 2048 * i, 4, T) for i in range(2)]
        PS0 = [0, P, 3 * P, 6 * P]
        PT0 = [0, 4 * P, 7 * P, 9 * P]
        sq = view(W0 + 5120, 2, T)
        m1, m1_at = {}, {}
        at = 0
        for name, dims in [("qlat", (2, T)), ("kvlat", (T,)), ("krope", (T,)), ("u", (2, T)), ("v", (NT, 256)),
                           ("pin", (2, T + 16)), ("win_a", (T + 16,)), ("win_b", (T + 16,)), ("qh", (4, T)),
                           ("kh", (4, T)), ("V", (NT, T)), ("mix", (ND, T)), ("win_m", (2, T))]:
            m1[name] = view(at, *dims)
            m1_at[name] = at
            at += int(np.prod(dims))
        assert at <= W0, at
        m1["cos"], m1["sin"] = rope1[:, 0, :], rope1[:, 1, :]
        at = W0
        for name, dims in [("sqlat", (3, T)), ("ta", (T,)), ("tb", (T,)), ("sqkr", (T,))]:
            m1[name] = view(at, *dims)
            m1_at[name] = at
            at += int(np.prod(dims))
        m2 = {}
        at = 0
        for name, dims in [("hq", (4, T)), ("hk", (4, T)), ("hlf", (4, T)), ("hv", (NT, T)), ("hy", (4, T)),
                           ("gq", (2, T)), ("gk", (2, T)), ("glf", (2, T)), ("gv", (NT, T)), ("gy", (4, T)),
                           ("nv", (NT, 256)), ("gate", (NT, 24)), ("hid", (124,)), ("kc", (62,)), ("vc", (128,)),
                           ]:
            m2[name] = view(at, *dims)
            at += int(np.prod(dims))
        assert at <= W0, at
        at = 0
        for name, dims in [("nq", (4, T)), ("ck", (2, T)), ("cv", (2, T)), ("ks", (2, T)), ("kw", (2, T))]:
            m2[name] = view(at, *dims)
            at += int(np.prod(dims))
        cm = [view(W0 + 5120 + 256 * i, 2, NT * NCMP) for i in range(2)]
        cm_max, cm_sum, cm_rec = (view(W0 + 6144 + 8 * i, 2, NT) for i in range(3))
        m2["ob"] = view(W0 + 6144, 2, T)
        m2["X"] = rope1[:, 0, :]
        m2["Eq"], m2["Ek"] = rope1[:, 1, 0:256], rope1[:, 1, 256:T]
        ropec, ropes = rope2[:, 0, :], rope2[:, 1, :]
        ksl = rope2
        qsl = view(W0 + 4096, 2, T)
        m2["cmpT"] = view(10240, 8, T)
        m2["m"] = view(10240, ND, T)
        m2["sig"] = view(W0, 6, T)

        sgt = view(m1_at["ta"], NT, 256)

        h_tmp = [act_hi[:, j, :] for j in range(ND)]
        mix_hi = [act_hi[:, 12 + j, :] for j in range(ND)]
        m_hi = [act_hi[:, 8 + j, :] for j in range(ND)]
        m_lo = [h_lo[:, j, :] for j in range(ND)]
        ZS = 28

        slot = [ctx.enter_context(nc.semaphore(f"weights_in_slot{r}")) for r in range(RING)]
        s_const = ctx.enter_context(nc.semaphore("constants_loaded"))
        s_x0 = [ctx.enter_context(nc.semaphore(f"x_loaded{i}")) for i in range(ND // 2)]
        s_pos = ctx.enter_context(nc.semaphore("positions_loaded"))
        s_par = signal("params_loaded", 16)
        s_init = ctx.enter_context(nc.semaphore("vector_setup"))
        s_rope = ctx.enter_context(nc.semaphore("rope_angles"))
        s_ropea = ctx.enter_context(nc.semaphore("rope_sines"))
        s_out = ctx.enter_context(nc.semaphore("output_stored"))
        x_ready = signal("residual_block_ready", ND)
        n_sq = signal("norm_squares", ND)
        n_ss = signal("norm_sum", 1)
        n_ln = signal("norm_log", 1)
        n_rs = signal("norm_rstd", 1)
        h_ready = signal("h_block_ready", ND, 1)
        gu_mm = signal("gate_up_product", 2 * FB)
        silu = signal("gate_silu", FB, 3)
        act_ready = signal("ffn_hidden_ready", FB, 3)
        down_mm = signal("down_tile_done", FB)
        act_v = signal("ffn_hidden_value", FB)
        act_h = signal("ffn_hidden_high", FB)
        h_v = signal("ffn_input_value", ND)
        h_h = signal("ffn_input_high", ND)
        w_h = signal("weight_tile_high", FFN_TILES)
        w_split = signal("weight_tile_split", FFN_TILES, RING)
        w1_h = signal("mixer1_tile_high", ND)
        w1_split = signal("mixer1_tile_split", ND)
        w2_h = signal("mixer2_tile_high", ZS + 24 + ND)
        w2_split = signal("mixer2_tile_split", ZS + 24 + ND)
        hh_t = signal("h_high_made", ND)
        hh_l = signal("h_low_ready", ND)
        hh_r = signal("h_high_ready", ND)
        wo_h = signal("w_out_input_high", ND)
        wo_r = signal("w_out_input_ready", ND)
        z_mm = signal("z1_product", 22)
        z_out = signal("z1_copied", 22)
        z_sq = signal("z1_squares", 3)
        lat_ss = signal("latent_sum", 2)
        lat_ln = signal("latent_log", 2)
        lat_rs = signal("latent_rstd", 2)
        lat_n = signal("latent_normed", 3)
        hd_sq = signal("head_squares", 9)
        hd_raw = signal("head_raw", 8)
        hd_ss = signal("head_sum", 8)
        hd_ln = signal("head_log", 8)
        hd_rs = signal("head_rstd", 8)
        hd_n = signal("head_normed", 8)
        hd_rot = signal("head_rotated", 8)
        hd_t = signal("head_rope_parts", 16)
        hd_r = signal("head_roped", 8)
        sg_q = signal("sgu_squares", 1)
        sg_ss = signal("sgu_sumsq", 1)
        sg_ln = signal("sgu_log", 1)
        sg_rs = signal("sgu_rstd", 1)
        sg_w = signal("sgu_weights_masked", 4)
        sg_v = signal("sgu_values_normed", NT)
        sg_mm = signal("sgu_mixed", 2)
        sg_z = signal("sgu_biased", 2)
        sg_g = signal("sgu_gated", 2)
        pw = signal("pool_step", 13)
        pl_m = signal("pool_means", 2)
        pl_mm = signal("pool_product", 2)
        pl_o = signal("pool_out", 2)
        mx_sq = signal("mix_squares", ND)
        mx_ss = signal("mix_sum", 3)
        mx_ln = signal("mix_log", 3)
        mx_rs = signal("mix_rstd", 3)
        mx_n = signal("mix_normed", ND)
        wo_mm = signal("w_out_product", ND)
        def attention_signals(tag, units):
            return {k: signal(f"{tag}_{k}", n * units) for k, n in
                    [("scores", 4), ("maxed", 4), ("exped", 4), ("recip", 1), ("gated", 1), ("scaled", 4),
                     ("turned", 4), ("turned_out", 4), ("pv", 1)]}
        at1 = attention_signals("mla", HEADS1)
        at2 = attention_signals("nsa", 16)
        o1_out = signal("mla_out_copied", HEADS1)
        y_mm = signal("z2_product", 42)
        y_out = signal("z2_copied", 42)
        lb_s = ctx.enter_context(nc.semaphore("lower_bounds"))
        lb_e = ctx.enter_context(nc.semaphore("lower_bound_exps"))
        lb_l = signal("lower_bound_of_layer", 2)
        og_s = signal("output_gate_silu", 2)
        hf_s = signal("forget_sigmoid", 4)
        hf_k = signal("forget_key", 4)
        hf_m = signal("forget_mixed", 4)
        hf_f = signal("forget_gate", 4)
        hf_l = signal("forget_log", 4)
        gl_a = signal("gla_abs", 2)
        gl_e = signal("gla_exp", 2)
        gl_l = signal("gla_ln", 2)
        gl_d = signal("gla_logsig", 2)
        gl_f = signal("gla_log_decay", 2)
        ln_x0 = signal("lin_suffix_zeroed", 6)
        ln_e = signal("lin_prefix_exp", 54)
        ln_f = signal("lin_suffix_exp", 48)
        ln_q = signal("lin_scaled_q", 54)
        ln_k = signal("lin_scaled_k", 48)
        ln_x = signal("lin_suffix", 48)
        ln_p = signal("lin_prefix", 48)
        ln_mm = signal("lin_scores", 80)
        ln_st = signal("lin_scores_placed", 80)
        ln_pv = signal("lin_pv", 8)
        lo_sq = signal("lin_out_squares", 8)
        lo_o = signal("lin_out_copied", 8)
        lo_ss = signal("lin_out_sum", 8)
        lo_ln = signal("lin_out_log", 8)
        lo_rs = signal("lin_out_rstd", 8)
        lo_n = signal("lin_out_normed", 8)
        lo_y = signal("lin_out_gated", 8)
        rp_mm = signal("nsa_rotated", 7)
        rp_u = signal("nsa_rope_sin", 7)
        rp_t = signal("nsa_rope_cos", 7)
        rp_o = signal("nsa_roped", 16)
        cv_o = signal("cmp_values_laid", 3)
        ch_mm = signal("cmp_hidden", 4)
        ch_b = signal("cmp_bias", 2)
        ch_g = signal("cmp_gelu", 2)
        cc_mm = signal("cmp_projected", 2)
        cc_o = signal("cmp_kv_copied", 2)
        cs_mm = signal("cmp_scores", 8)
        cs_m = signal("cmp_masked", 8)
        cs_x = signal("cmp_max", 4)
        cs_d = signal("cmp_shifted", 4)
        cs_e = signal("cmp_exp", 4)
        cs_s = signal("cmp_sum", 4)
        cs_r = signal("cmp_recip", 4)
        cs_v = signal("cmp_valid", 4)
        cs_g = signal("cmp_gate", 4)
        cs_p = signal("cmp_probs", 4)
        cs_t = signal("cmp_turned", 8)
        cs_o = signal("cmp_turned_out", 8)
        no_y = signal("nsa_out_copied", 4)
        mg_mm = signal("merge_gate_product", 24)
        mg_s = signal("merge_gate_sigmoid", 24, 3)
        br_mm = signal("branch_product", 24)
        br_m = signal("branch_merged", 24, 6)
        br_a = signal("branch_added", 16)

        block = ctx.enter_context(nc.Block())

        MIX_ORDER = (4, 5, 6, 7, 0, 1, 2, 3)
        LIN = [(u, m2["hq"][:, u, :], m2["hk"][:, u, :], m2["hlf"][:, u, :], [(u, 0, P)]) for u in range(4)] + \
              [(4 + b, m2["gq"][:, b, :], m2["gk"][:, b, :], m2["glf"][:, b, :],
                [(4 + 2 * b, 0, 64), (5 + 2 * b, 64, P)]) for b in range(2)]

        LIN_PLACED = {hd: 10 * (hd + 1) for hd in range(4)} | {4: 59, 5: 60, 6: 79, 7: 80}

        def raw_block(i):
            return m2["nq"][:, i - 1, :] if 1 <= i < 5 else m2[{0: "ck", 5: "ks", 6: "kw"}[i]][:, 0, :]

        def lin_value(head, s):
            v = m2["hv"] if head < 4 else m2["gv"]
            return v[:, s, (head % 4) * P:(head % 4 + 1) * P]

        def lin_gate(head):
            return (m2["hy"] if head < 4 else m2["gy"])[:, head % 4, :]

        def halves(a, m, which):
            return a.rearrange("p (g two m) -> p g two m", two=2, m=m)[:, :, which, :]

        def ends(a, m, which):
            v = a.rearrange("p (g two m) -> p g two m", two=2, m=m)[:, :, which, m - 1:m]
            return v.broadcast_to([P, T // (2 * m), m])

        def compact(a, m):
            return a.rearrange("p (g m) -> p g m", m=m)

        def diagonal(s):
            flat = ST[s].rearrange("p a b -> p (a b)")
            return [flat[:, 640 * i:640 * i + P] for i in range(NT)]

        def diag4(s):
            off = W0 + 2048 * s
            return arena[:, off:off + 2560].rearrange("p (a b) -> p a b", b=640)[:, :, 0:P]

        Y = {}
        order = [("hi", 4, 0), ("gv", 4, 4), ("nv", 2, 8), ("glr", 1, 10), ("ngate", 1, 10), ("hf", 4, 11),
                 ("gdec", 2, None), ("hq", 4, 15), ("hog", 4, 19), ("gk", 2, 23), ("gq", 2, 25), ("gog", 4, 27),
                 ("nq", 4, 31), ("nkc", 1, 35), ("nks", 1, 36), ("nkw", 1, 37), ("nvc", 1, 38)]
        WHOLE, BEFORE = 12, 22
        for name, n, tile in order:
            for i in range(n):
                Y[name, i] = (len(Y), tile)
        YKEYS = list(Y)
        YN = 42
        FILL = {}
        for u in range(6):
            levels = (1, 3, 5, 6, 7, 8) if u < 4 else range(1, 9)
            first = BEFORE + (3 * u if u < 4 else 12 + 4 * (u - 4))
            FILL |= {(u, v): (YKEYS[first + n // 2], n % 2) for n, v in enumerate(levels)}

        def y_bank(g):
            return bank[g % 3]

        def tile_in(l, base, per, t):
            return slot[t % RING], l * (16 * per // RING) + 16 * ((base + t) // RING + 1)

        FREE1 = [(z_mm, k) for k in (1, 2, 3, 4, 5, 6, 7, 8, 9, 10, 14, 22)] + \
                [(w1_split, j + 1) for j in range(ND)] + ["pad"]
        FREE2 = [(y_mm, k) for k in (*range(1, 11), 12)] + [(w2_split, k + 1) for k in range(ZS)] + \
                [(ch_mm, 1), (ch_mm, 2), (ch_mm, 3), (ch_mm, 4)]
        for i in range(4):
            FREE2 += [(w2_split, ZS + 6 * i + k) for k in range(1, 7)] + \
                     [(br_mm, 6 * i + k) for k in (2, 4, 6)]
        FREE2 += [(w2_split, ZS + 24 + j + 1) for j in range(ND)]
        assert len(FREE1) == MIX1_TILES and len(FREE2) == MIX2_TILES, (len(FREE1), len(FREE2))

        @block.sync
        def _(sp):
            def load(t, r):
                sp.dma_start(ring[:, r, :],
                             wstream[bass.ds(t, 1)].rearrange("a p n -> p (a n)")).then_inc(slot[r], 16)

            def layer(l, nf, base, per, free):
                mix = len(free)
                sp.wait_ge(*h_ready(2 * nf, 0))
                sp.dma_start(par[:, :], params[bass.ds(nf, 1)].rearrange("a p n -> p (a n)")).then_inc(s_par.sem, 16)

                def wait_product(t):
                    if t < 0:
                        sp.wait_ge(*w_split(nf, t + 1))
                    elif t < mix:
                        if free[t] == "pad":
                            sp.wait_ge(*tile_in(l, base, per, t))
                        else:
                            sem, k = free[t]
                            sp.wait_ge(*sem(l, k))
                    else:
                        sp.wait_ge(*w_split(nf, t - mix + 1))

                for t in range(mix + 2 * RING):
                    wait_product(t - RING)
                    load(l * per + (base + t), t % RING)
                with sp.Fori(1, 11) as it:
                    for r in range(6):
                        sp.wait_ge(w_split.sem, nf * FFN_TILES + it * 6 + (w_split.start + r - RING + 1))
                        load(l * per + it * 6 + (base + mix + r), r % RING)

            for j in range(0, ND, 2):
                sp.dma_start(x[:, j:j + 2, :].rearrange("p a t -> p (a t)"), xT[:, j * T:(j + 2) * T])\
                    .then_inc(s_x0[j // 2], 16)
            sp.dma_start(cst[:, :], const).then_inc(s_const, 16)
            sp.dma_start(m1["ta"].bitcast(I32), pos).then_inc(s_pos, 16)
            with sp.Fori(0, LAYERS) as l:
                layer(l, l, 0, PER1, FREE1)
            with sp.Fori(0, LAYERS) as l:
                layer(l, l + LAYERS, BASE2, PER2, FREE2)
            sp.wait_ge(*h_ready(8, ND))
            sp.dma_start(outT, h[:, :, :].rearrange("p a t -> p (a t)")).then_inc(s_out, 16)
            sp.wait_ge(s_out, 16)

        @block.tensor
        def _(pe):
            def product(out, lhsT, rhs, start=True, stop=True):
                return pe.matmul(out, lhsT, rhs, start=start, stop=stop)

            def norm(n):
                for j in range(ND):
                    pe.wait_ge(*n_sq(n, j + 1))
                    last = product(bank[0][:, :], C("ones"), h[:, j, :], j == 0, j == ND - 1)
                last.then_inc(n_ss.sem, 1)

            def wide(out, r, rhs, n=ND, cols=P, coming=None):
                for k in range(n):
                    if coming is not None:
                        pe.wait_ge(*h_ready(coming, k + 1))
                    last = product(out, ring[:, r, k * P:k * P + cols], rhs[:, k, :], k == 0, k == n - 1)
                return last

            def token_major(out, r, first=0, cols=P, coming=None):
                for m in range(NT):
                    for k in range(ND):
                        if coming is not None and m == 0:
                            pe.wait_ge(*h_ready(coming, k + 1))
                        last = product(out[:, m * cols:(m + 1) * cols], h[:, k, m * P:m * P + P],
                                       ring[:, r, k * P + first:k * P + first + cols], k == 0, k == ND - 1)
                return last

            def halves_product(out, w, k, hi, lo, start, stop):
                ks = slice(k * P, k * P + P)
                product(out, w_hi[:, w, ks], hi, start, False)
                product(out, w_hi[:, w, ks], lo, False, False)
                return product(out, w_lo[:, w, ks], hi, False, stop)

            def w_out(nf, l, split, hi, lo, order):
                for j in range(ND):
                    pe.wait_ge(*split(l, j + 1))
                    for n, k in enumerate(order):
                        if j == 0:
                            pe.wait_ge(*wo_r(nf, n + 1))
                        last = halves_product(bank[j][:, :], j % 2, k, hi[k], lo[k], n == 0, n == ND - 1)
                    last.then_inc(wo_mm.sem, 1)

            def ffn(nf, norm_pass):
                def gate_up(g, r, it):
                    for w, (banks, used) in enumerate(((bank[0:3], silu), (bank[3:6], act_ready))):
                        pe.wait_ge(w_split.sem, nf * FFN_TILES + it * 6 + (w_split.start + 2 * g + w + 1))
                        pe.wait_ge(used.sem, nf * FB + it * RING + (used.start + g - 2))
                        for k in range(ND):
                            if r == 0 and w == 0:
                                pe.wait_ge(*h_ready(norm_pass, k + 1))
                            last = halves_product(banks[r][:, :], w, k, h_hi[:, k, :], h_lo[:, k, :],
                                                  k == 0, k == ND - 1)
                        last.then_inc(gu_mm.sem, 1)

                with pe.Fori(0, 7) as it:
                    for r in range(3):
                        gate_up(r, r, it)
                gate_up(FB - 1, 0, 0)

                def down(d, it, first=False, last=False):
                    pe.wait_ge(w_split.sem, nf * FFN_TILES + it * 6 + (w_split.start + 2 * FB + d + 1))
                    if isinstance(it, int):
                        hi, lo = act_hi[:, d, :], act_lo[:, d, :]
                    else:
                        hi, lo = (a[:, bass.ds(it * 6 + d, 1), :].rearrange("p a t -> p (a t)")
                                  for a in (act_hi, act_lo))
                    for j in range(ND):
                        i = halves_product(bank[j][:, :], d % 2, j, hi, lo, first, last)
                    i.then_inc(down_mm.sem, 1)

                pe.wait_ge(*act_ready(nf, FB))
                down(0, 0, first=True)
                with pe.Fori(0, 3) as it:
                    for d in range(1, 7):
                        down(d, it)
                for d in range(19, FB):
                    down(d, 0, last=d == FB - 1)

            def scores(s, l, u, q, k):
                for t in range(NT):
                    if u > 0:
                        pe.wait_ge(*s["exped"](l, NT * (u - 1) + t + 1))
                    b = bank[3 + t]
                    product(b[:, 0:(t + 1) * P], q[:, t * P:t * P + P], k[:, 0:(t + 1) * P], True, False)
                    product(b[:, t * P:(t + 1) * P], C("ident"), C("negdiag"), False, True)\
                        .then_inc(s["scores"].sem, 1)

            def turn_and_pv(s, l, u, v, out, bank_free, first, more):
                pe.wait_ge(*s["scaled"](l, NT * (u + 1)))
                for st in range(NT):
                    c = NT * u + st
                    if c >= 2:
                        pe.wait_ge(*s["turned_out"](l, c - 1))
                    b = bank[(7, 2)[c % 2]]
                    for t in range(st, NT):
                        off = PS0[t] + st * P
                        last = pe.transpose(b[:, (t - st) * P:(t - st + 1) * P],
                                            prob[:, u % 2, off:off + P], C("ident"))
                    last.then_inc(s["turned"].sem, 1)
                if bank_free is not None:
                    pe.wait_ge(*bank_free)
                for st in range(NT):
                    pe.wait_ge(*s["turned_out"](l, NT * u + st + 1))
                    last = product(out[:, st * P:T], v(st), probT[:, u % 2, PT0[st]:PT0[st] + (NT - st) * P],
                                   first and st == 0, (not more) and st == NT - 1)
                return last

            def mixer1(l):
                def z_wait(g, tile=None):
                    if tile is not None:
                        pe.wait_ge(*tile_in(l, 0, PER1, tile))
                    if g >= 3:
                        pe.wait_ge(*z_out(l, g - 2))

                def lat_sum(i):
                    blocks = ((0, 1), (2,))[i]
                    for c in blocks:
                        pe.wait_ge(*z_sq(l, c + 1))
                        last = product(bank[3 + i][:, :], C("ones"), m1["sqlat"][:, c, :],
                                       c == blocks[0], c == blocks[-1])
                    last.then_inc(lat_ss.sem, 1)

                for g in range(4):
                    z_wait(g, g)
                    wide(bank[g % 3][:, :], g % RING, h, coming=2 * l if g == 0 else None).then_inc(z_mm.sem, 1)
                for c in range(2):
                    z_wait(4 + c, 4 + c)
                    token_major(bank[(4 + c) % 3], (4 + c) % RING).then_inc(z_mm.sem, 1)
                    lat_sum(c)
                for g in range(6, 10):
                    z_wait(g, g)
                    wide(bank[g % 3][:, :], g % RING, h).then_inc(z_mm.sem, 1)

                def head(i):
                    g = 10 + i
                    z_wait(g, 10 if i < 4 else 11)
                    b = bank[g % 3]
                    if i < 4:
                        pe.wait_ge(*lat_n(l, 2))
                        for c in range(2):
                            at = c * 384 + i * QK1
                            last = product(b[0:QK1, :], ring[:, 10 % RING, at:at + QK1], m1["qlat"][:, c, :],
                                           c == 0, c == 1)
                    else:
                        pe.wait_ge(*lat_n(l, 3))
                        at = (i - 4) * NOPE1
                        last = product(b[0:NOPE1, :], ring[:, 11 % RING, at:at + NOPE1], m1["kvlat"])
                    last.then_inc(z_mm.sem, 1)

                def head_sum(i):
                    pe.wait_ge(*hd_sq(l, i + 2))
                    if i >= 2:
                        pe.wait_ge(*hd_ln(l, i - 1))
                    else:
                        pe.wait_ge(*lat_ln(l, i + 1))
                    b = bank[3 + i % 2]
                    if i < 4:
                        last = product(b[0:QK1, :], C("ones", slice(0, QK1))[:, 0:QK1], sq[0:QK1, i % 2, :])
                    else:
                        product(b[0:QK1, :], C("ones", slice(0, 64))[:, 0:QK1], sq[0:64, i % 2, :], True, False)
                        last = product(b[0:QK1, :], C("ones", slice(64, 96))[:, 0:QK1], m1["sqkr"][64:96, :],
                                       False, True)
                    last.then_inc(hd_ss.sem, 1)

                def rotate(i):
                    pe.wait_ge(*hd_n(l, i + 1))
                    if i >= 2:
                        pe.wait_ge(*hd_t(l, 2 * (i - 2) + 1))
                    hv = (m1["qh"] if i < 4 else m1["kh"])[0:QK1, i % 4, :]
                    product(bank[5 + i % 2][0:QK1, :], C("rot1", slice(0, QK1)), hv).then_inc(hd_rot.sem, 1)

                for i in range(8):
                    head(i)
                    if i >= 1:
                        head_sum(i - 1)
                    if i >= 2:
                        rotate(i - 2)
                head_sum(7)
                rotate(6)
                for m in range(NT):
                    z_wait(18 + m)
                    product(bank[(18 + m) % 3][:, :], m1["kvlat"][:, m * P:m * P + P],
                            ring[:, 11 % RING, 256:768]).then_inc(z_mm.sem, 1)
                rotate(7)

                pe.wait_ge(*sg_v(l, NT))
                pe.wait_ge(*sg_w(l, 4))
                pe.wait_ge(*hd_ln(l, 8))
                for b in range(2):
                    for hh in range(2):
                        hd = 2 * b + hh
                        for m in range(NT):
                            last = product(bank[3 + b][64 * hh:64 * hh + 64, m * P:m * P + P],
                                           m1["v"][:, m, hd * 64:hd * 64 + 64],
                                           par[:, PAR1["w_sp"]][:, hd * P:hd * P + P])
                    last.then_inc(sg_mm.sem, 1)
                pe.wait_ge(*hd_t(l, 16))
                for b in range(2):
                    pe.wait_ge(*pl_m(l, b + 1))
                    product(bank[5 + b][:, :], par[:, PAR1["w_pool"]][:, b * P:b * P + P],
                            m1["win_m"][:, b, :]).then_inc(pl_mm.sem, 1)

                def mix_sum(i):
                    pe.wait_ge(*mx_sq(l, (2, 4, 8)[i]))
                    blocks = ((4, 5), (6, 7), (0, 1, 2, 3))[i]
                    for c in blocks:
                        last = product(bank[(3, 4, 3)[i]][:, :], C("ones"), h[:, c, :],
                                       c == blocks[0], c == blocks[-1])
                    last.then_inc(mx_ss.sem, 1)

                pe.wait_ge(*sg_z(l, 2))
                mix_sum(0)
                mix_sum(1)
                pe.wait_ge(*hd_r(l, 8))
                pe.wait_ge(*z_out(l, 22))
                pe.wait_ge(*mx_ln(l, 2))
                pe.wait_ge(*pl_o(l, 2))
                for u in range(HEADS1 + 1):
                    if u < HEADS1:
                        scores(at1, l, u, m1["qh"][0:QK1, u, :], m1["kh"][0:QK1, u, :])
                    if u >= 1:
                        w = u - 1
                        turn_and_pv(at1, l, w, lambda st, w=w: m1["V"][:, st, w * P:w * P + P], bank[w % 2][:, :],
                                    o1_out(l, w - 1) if w >= 2 else None, True, False)\
                            .then_inc(at1["pv"].sem, 1)
                mix_sum(2)
                w_out(l, l, w1_split, mix_hi, [h_lo[:, k, :] for k in range(ND)], MIX_ORDER)

            def mixer2(l):
                def project(key, part=None):
                    name, i = key
                    g, tile = Y[key]
                    b = y_bank(g)
                    if g >= 3 and part != 1:
                        pe.wait_ge(*y_out(l, g - 2))
                    if name == "gdec":
                        pe.wait_ge(*y_out(l, Y["glr", 0][0] + 1))
                        last = product(b[:, :], par[0:16, PAR2["w_gla"]][:, i * P:i * P + P], ropec[0:16, :])
                    elif name == "glr":
                        pe.wait_ge(*tile_in(l, BASE2, PER2, tile))
                        last = wide(b[0:16, :], tile % RING, h, cols=16)
                    elif name == "ngate":
                        last = token_major(b, tile % RING, 16, 24)
                    elif name in ("hi", "gv", "nv"):
                        pe.wait_ge(*tile_in(l, BASE2, PER2, tile + i))
                        last = token_major(b, (tile + i) % RING, coming=4 + 2 * l if g == 0 else None)
                    else:
                        s = tile + i - 11
                        if part != 1:
                            pe.wait_ge(*w2_split(l, s + 1))
                        if s == 0:
                            pe.wait_ge(*hh_l(l, ND))
                        for k in range(ND) if part is None else range(4 * part, 4 * part + 4):
                            if s == 0:
                                pe.wait_ge(*hh_r(l, k + 1))
                            last = halves_product(b[:, :], s % 2, k, h_hi[:, k, :], h_lo[:, k, :],
                                                  k == 0, k == ND - 1)
                    if part != 0:
                        last.then_inc(y_mm.sem, 1)

                for key in YKEYS[:BEFORE]:
                    project(key)

                group = 0
                for u, q, k, lf, heads in LIN:
                    if u >= 4:
                        for head, _, _ in LIN[u - 1][4]:
                            lin_pv(l, head)
                            lin_sum(l, head)
                    for v in range(10):
                        for head, lo, hi in heads:
                            rows = slice(lo, hi)
                            if v == 0:
                                pe.wait_ge(*(y_out(l, Y["hq", u][0] + 1) if u < 4 else
                                             y_out(l, Y["gq", u - 4][0] + 1)))
                                if u < 4:
                                    pe.wait_ge(*hf_k(l, u + 1))
                            else:
                                pe.wait_ge(*ln_q(l, 9 * u + v))
                                if v >= 2:
                                    pe.wait_ge(*ln_k(l, 8 * u + v - 1))
                            if group >= 4:
                                pe.wait_ge(*ln_st(l, group - 3))
                            b = bank[3 + group % 4]
                            qv = q if v == 0 else qsl[:, v % 2, :]
                            kv = k if v < 2 else ksl[:, v % 2, :]
                            if v < 8:
                                for t in range(NT):
                                    c = slice(t * P, t * P + P)
                                    last = product(b[:, c], kv[rows, c], qv[rows, c])
                            else:
                                for n, (ks_, q0, q1) in enumerate((((0, 1, 2), (2, 3, 4)) if v == 8 else
                                                                   ((0, 2, 4), (1, 2, 4)))):
                                    w = (q1 - q0) * P
                                    last = product(b[:, n * w:(n + 1) * w], kv[rows, ks_ * P:ks_ * P + P],
                                                   qv[rows, q0 * P:q1 * P])
                            last.then_inc(ln_mm.sem, 1)
                            group += 1
                        if (u, v) in FILL:
                            project(*FILL[u, v])
                        if 0 < u < 4 and v == 2:
                            lin_pv(l, u - 1)
                        if 0 < u < 4 and v == 4:
                            lin_sum(l, u - 1)
                for head, _, _ in LIN[-1][4]:
                    lin_pv(l, head)
                    lin_sum(l, head)

                def rotation(i):
                    if i >= 2:
                        pe.wait_ge(*rp_u(l, i - 1))
                    product(bank[i % 2][:, :], C("rot2"), raw_block(i)).then_inc(rp_mm.sem, 1)

                def hidden(n):
                    data, done, posn, b1, b2 = ((m2["cv"], cv_o(l, 3), "pos_v", 6, 3),
                                                (m2["ck"], rp_o(l, 4), "pos_k", 4, 5))[n // 2]
                    if n % 2 == 0:
                        pe.wait_ge(*done)
                    t = 39 + n
                    pe.wait_ge(*tile_in(l, BASE2, PER2, t))
                    for p in range(8 * (n % 2), 8 * (n % 2) + 8):
                        w = ring[:, t % RING, (p % 8) * P:(p % 8) * P + P]
                        product(bank[b1][:, 0:2 * NCMP], w, data[:, :, 2 * p:2 * p + 16 * (NCMP - 1) + 1:16],
                                p == 0, p == 15)
                        last = product(bank[b2][:, 0:1], w, par[:, PAR2[posn]][:, p:p + 1], p == 0, p == 15)
                    last.then_inc(ch_mm.sem, 1)

                pe.wait_ge(*y_out(l, YN))
                rotation(0)
                rotation(1)
                pe.wait_ge(*ln_st(l, 80))
                for n in range(4):
                    hidden(n)
                    rotation(n + 2)
                rotation(6)
                pe.wait_ge(*rp_u(l, 7))
                pe.wait_ge(*ch_g(l, 1))
                for g in range(2):
                    last = product(bank[1][0:NCMP, g * 64:g * 64 + 64], m2["hid"][:, 62 + g * 31:93 + g * 31],
                                   par[:, PAR2["w2_v"]])
                last.then_inc(cc_mm.sem, 1)
                pe.wait_ge(*ch_g(l, 2))
                product(bank[0][:, 0:62], par[:, PAR2["w2_k"]], m2["hid"][:, 0:62]).then_inc(cc_mm.sem, 1)

                def cmp_scores(hd):
                    if hd >= 2:
                        pe.wait_ge(*cs_m(l, hd - 1))
                    rows, g = slice(64 * (hd % 2), 64 * (hd % 2) + 64), hd // 4
                    for t in range(NT):
                        last = product(bank[2 + hd % 2][:, t * NCMP:(t + 1) * NCMP],
                                       m2["nq"][rows, hd // 2, t * P:t * P + P],
                                       m2["kc"][rows, g * NCMP:(g + 1) * NCMP])
                    last.then_inc(cs_mm.sem, 1)

                pe.wait_ge(*cc_o(l, 2))
                pe.wait_ge(*rp_o(l, 16))
                cmp_scores(0)
                cmp_scores(1)
                for hd in range(8):
                    if hd % 2 == 0:
                        if hd + 2 < 8:
                            cmp_scores(hd + 2)
                            cmp_scores(hd + 3)
                        pe.wait_ge(*cs_p(l, hd // 2 + 1))
                    if hd >= 2:
                        pe.wait_ge(*cs_o(l, hd - 1))
                    for t in range(NT):
                        last = pe.transpose(bank[4 + hd % 2][0:NCMP, t * P:t * P + P],
                                            cm[hd // 2 % 2][:, hd % 2, t * NCMP:(t + 1) * NCMP], C("ident"))
                    last.then_inc(cs_t.sem, 1)
                pe.wait_ge(*cs_o(l, 8))
                for u in range(17):
                    if u < 16:
                        hd = u // 2
                        rows = slice(64 * (hd % 2), 64 * (hd % 2) + 64)
                        keys = (m2["ks"], m2["kw"])[u % 2][rows, hd // 4, :]
                        scores(at2, l, u, m2["nq"][rows, hd // 2, :], keys)
                    if u >= 1:
                        w = u - 1
                        hd, win = w // 2, w % 2
                        out = bank[(hd // 2) % 2][64 * (hd % 2):64 * (hd % 2) + 64, :]
                        at = 128 * win + 64 * (hd // 4)
                        last = turn_and_pv(at2, l, w, lambda st, at=at: m2["nv"][:, st, at:at + 64], out,
                                           no_y(l, hd // 2 - 1) if hd % 2 == 0 and win == 0 and hd >= 4 else None,
                                           win == 0, True)
                        if win:
                            last = product(out, m2["vc"][0:NCMP, (hd // 4) * 64:(hd // 4) * 64 + 64],
                                           m2["cmpT"][0:NCMP, hd, :], False, True)
                        last.then_inc(at2["pv"].sem, 1)

                with pe.Fori(0, 4) as it:
                    for r in range(6):
                        if r == 0:
                            pe.wait_ge(*lo_y(l, 8))
                            pe.wait_ge(*no_y(l, 4))
                        pe.wait_ge(w2_split.sem, l * w2_split.per + it * 6 + (ZS + r + 1))
                        pe.wait_ge(mg_s.sem, l * 24 + it * 6 + (mg_s.start + r - 2))
                        for k in range(ND):
                            last = halves_product(bank[r % 3][:, :], r % 2, k, h_hi[:, k, :], h_lo[:, k, :],
                                                  k == 0, k == ND - 1)
                        last.then_inc(mg_mm.sem, 1)
                    for r in range(6):
                        sem, v = tile_in(l, BASE2, PER2, 49 + r // 2)
                        pe.wait_ge(sem, v + it * 48)
                        pe.wait_ge(br_m.sem, l * 24 + it * 6 + (br_m.start + r - 2))
                        y = (m2["hy"], m2["gy"], m2["nq"])[r % 3]
                        for c in range(4):
                            at = (r % 2) * 512 + c * P
                            last = product(bank[3 + r % 3][:, :], ring[:, (49 + r // 2) % RING, at:at + P],
                                           y[:, c, :], c == 0, c == 3)
                        last.then_inc(br_mm.sem, 1)
                w_out(l + LAYERS, l, lambda l, k: w2_split(l, ZS + 24 + k), m_hi, m_lo, range(ND))

            def lin_pv(l, head):
                pe.wait_ge(*ln_st(l, LIN_PLACED[head]))
                if head > 0:
                    pe.wait_ge(*lo_ln(l, head))
                else:
                    pe.wait_ge(*y_out(l, Y["hi", 3][0] + 1))
                if head >= 4:
                    pe.wait_ge(*y_out(l, Y["gv", 3][0] + 1))
                for st in range(NT):
                    last = product(bank[7][:, st * P:T], lin_value(head, st), ST[head % 2][:, st, st * P:T],
                                   st == 0, st == NT - 1)
                last.then_inc(ln_pv.sem, 1)

            def lin_sum(l, head):
                pe.wait_ge(*lo_o(l, head + 1))
                product(bank[7][:, :], C("ones"), sq[:, head % 2, :]).then_inc(lo_ss.sem, 1)

            pe.wait_ge(s_const, 16)
            with pe.Fori(0, LAYERS) as l:
                norm(2 * l)
                mixer1(l)
                norm(2 * l + 1)
                ffn(l, 2 * l + 1)
            with pe.Fori(0, LAYERS) as l:
                norm(2 * l + 4)
                mixer2(l)
                norm(2 * l + 5)
                ffn(l + LAYERS, 2 * l + 5)
            norm(8)

        @block.gpsimd
        def _(po):
            def times_one(out, a, n):
                return po.tensor_tensor(out, a, C("ones")[:, 0:1].broadcast_to([P, n]), ALU.mult)

            def halves(raw, w, high, count, done):
                times_one(w_hi[:, w, :], raw, TILE).then_inc(high.sem, 1)
                po.wait_ge(high.sem, count)
                po.tensor_tensor(w_lo[:, w, :], raw, w_hi[:, w, :].bitcast(F32), ALU.subtract)\
                    .then_inc(done.sem, 1)

            def mixer1(l):
                for s in range(ND):
                    po.wait_ge(*tile_in(l, 0, PER1, 12 + s))
                    if s < 2:
                        po.wait_ge(*h_ready(2 * l, 1))
                    else:
                        po.wait_ge(*wo_mm(l, s - 1))
                    halves(ring[:, (12 + s) % RING, :], s % 2, w1_h, l * ND + (s + 1), w1_split)

            def mixer2(l):
                def split(s, it=0):
                    if s < ZS:
                        t, dt = 11 + s, 6
                    elif s < ZS + 24:
                        t, dt = 43 + 9 * ((s - ZS) // 6) + (s - ZS) % 6, 9
                    else:
                        t, dt = 79 + s - ZS - 24, 0
                    sem, v = tile_in(l, BASE2, PER2, t)
                    po.wait_ge(sem, v + it * (16 * dt // RING))
                    if s < 2:
                        po.wait_ge(*h_ready(4 + 2 * l, 1))
                    elif s < 6:
                        po.wait_ge(*y_mm(l, WHOLE + s - 1))
                    elif s < ZS + 2:
                        po.wait_ge(y_mm.sem, l * y_mm.per + it * 6 + (WHOLE + s + 1))
                    elif s < ZS + 26:
                        po.wait_ge(mg_mm.sem, l * mg_mm.per + it * 6 + (s - ZS - 1))
                    else:
                        po.wait_ge(*wo_mm(l + LAYERS, s - ZS - 25))
                    halves(ring[:, t % RING, :], s % 2, w2_h, l * w2_h.per + it * 6 + (s + 1), w2_split)

                for s in range(6):
                    split(s)
                with po.Fori(0, 3) as it:
                    for s in range(6, 12):
                        split(s, it)
                for s in range(24, ZS):
                    split(s)
                split(ZS)
                split(ZS + 1)
                with po.Fori(0, 3) as it:
                    for s in range(ZS + 2, ZS + 8):
                        split(s, it)
                for s in range(ZS + 20, ZS + 24 + ND):
                    split(s)

            def ffn(l, nf, base, mix, per):
                def split(s, it=0):
                    raw, w = ring[:, (mix + s) % RING, :], s % 2
                    sem, v = tile_in(l, base, per, mix + s)
                    po.wait_ge(sem, v + it * 32)
                    if s < 2:
                        po.wait_ge(*wo_mm(nf, ND - 1 + s))
                    elif s < 2 * FB + 2:
                        po.wait_ge(gu_mm.sem, nf * gu_mm.per + it * 6 + (s - 1))
                    else:
                        po.wait_ge(down_mm.sem, nf * down_mm.per + it * 6 + (s - 2 * FB - 1))
                    halves(raw, w, w_h, nf * FFN_TILES + it * 6 + (s + 1), w_split)

                for s in range(2):
                    split(s)
                with po.Fori(0, 7) as it:
                    for s in range(2, 8):
                        split(s, it)
                for s in range(44, 46):
                    split(s)
                with po.Fori(0, 3) as it:
                    for s in range(46, 52):
                        split(s, it)
                for s in range(64, 66):
                    split(s)

            po.wait_ge(s_const, 16)
            po.sem_inc(w_split.sem, w_split.start)
            with po.Fori(0, LAYERS) as l:
                mixer1(l)
                ffn(l, l, 0, MIX1_TILES, PER1)
            with po.Fori(0, LAYERS) as l:
                mixer2(l)
                ffn(l, l + LAYERS, BASE2, MIX2_TILES, PER2)

        @block.scalar
        def _(sc):
            def eps(rows, name="eps"):
                return C(name, rows)

            def rsqrt(out_i, psum, rows, scale, eps_name, ln_sig, ln_at, rs_sig, rs_free):
                if rs_free is not None:
                    sc.wait_ge(*rs_free)
                sc.activation(rstd[rows, out_i, :], psum[rows, :], ACT.Ln, bias=eps(rows, eps_name), scale=scale)\
                    .then_inc(ln_sig.sem, 1)
                sc.wait_ge(*ln_sig(*ln_at))
                sc.activation(rstd[rows, out_i, :], rstd[rows, out_i, :], ACT.Exp, scale=-0.5)\
                    .then_inc(rs_sig.sem, 1)

            ALL = slice(0, P)

            def norm(n):
                for j in range(ND):
                    sc.wait_ge(*x_ready(n, j + 1))
                    sc.activation(h[:, j, :], x[:, j, :], ACT.Square).then_inc(n_sq.sem, 1)
                sc.wait_ge(*n_ss(n, 1))
                rsqrt(0, bank[0], ALL, 1.0 / D, "eps", n_ln, (n, 1), n_rs, None)

            def ffn(nf):
                for j in range(ND):
                    sc.wait_ge(*h_v(nf, j + 1))
                    sc.activation(h_hi[:, j, :], sil[:, j % 3, :], ACT.Copy).then_inc(h_h.sem, 1)

                def gate(g, r, it):
                    sc.wait_ge(gu_mm.sem, nf * gu_mm.per + it * 6 + (2 * g + 1))
                    sc.wait_ge(act_ready.sem, nf * FB + it * RING + (act_ready.start + g - 2))
                    sc.activation(sil[:, r, :], bank[r][:, :], ACT.Silu).then_inc(silu.sem, 1)

                with sc.Fori(0, 7) as it:
                    for r in range(3):
                        gate(r, r, it)
                gate(FB - 1, 0, 0)

            def exps(s, l, u):
                for t in range(NT):
                    sc.wait_ge(*s["maxed"](l, NT * u + t + 1))
                    if u >= 2 and t == 0:
                        sc.wait_ge(*s["turned"](l, NT * (u - 1)))
                    c = 4 * (u % 2) + t
                    sc.activation(prob[:, u % 2, PS0[t]:PS0[t] + (t + 1) * P], bank[3 + t][:, 0:(t + 1) * P], ACT.Exp,
                                  bias=small[:, 16 + c:17 + c], accum_out=small[:, 24 + c:25 + c])\
                        .then_inc(s["exped"].sem, 1)

            def turned_copies(s, l, u):
                if u >= 2:
                    sc.wait_ge(*s["pv"](l, u - 1))
                for st in range(NT):
                    c = NT * u + st
                    sc.wait_ge(*s["turned"](l, c + 1))
                    sc.activation(probT[:, u % 2, PT0[st]:PT0[st] + (NT - st) * P],
                                  bank[(7, 2)[c % 2]][:, 0:(NT - st) * P], ACT.Copy).then_inc(s["turned_out"].sem, 1)

            def mixer1(l):
                def lat_rstd(i):
                    sc.wait_ge(*lat_ss(l, i + 1))
                    rsqrt(i, bank[3 + i], ALL, (1 / 256, 1 / 128)[i], "eps", lat_ln, (l, i + 1), lat_rs, None)

                for g in range(3):
                    sc.wait_ge(*z_mm(l, g + 1))
                    dst = m1["qlat"][:, g, :] if g < 2 else m1["kvlat"]
                    sc.activation(m1["sqlat"][:, g, :], bank[g][:, :], ACT.Square).then_inc(z_sq.sem, 1)
                    sc.activation(dst, bank[g][:, :], ACT.Copy).then_inc(z_out.sem, 1)
                sc.wait_ge(*z_mm(l, 4))
                sc.activation(m1["sqkr"][64:96, :], bank[0][64:96, :], ACT.Square).then_inc(hd_sq.sem, 1)
                sc.activation(m1["krope"][64:96, :], bank[0][64:96, :], ACT.Copy).then_inc(z_out.sem, 1)
                for c in range(2):
                    sc.wait_ge(*z_mm(l, 5 + c))
                    sc.activation(m1["v"][:, :, c * P:c * P + P],
                                  bank[(4 + c) % 3][:, :].rearrange("p (m n) -> p m n", m=NT), ACT.Copy)\
                        .then_inc(z_out.sem, 1)
                    lat_rstd(c)
                for g in range(6, 10):
                    sc.wait_ge(*z_mm(l, g + 1))
                    dst = m1["u"][:, g - 6, :] if g < 8 else m1["pin"][:, g - 8, 16:16 + T]
                    sc.activation(dst, bank[g % 3][:, :], ACT.Copy).then_inc(z_out.sem, 1)
                sc.wait_ge(*sg_ss(l, 1))
                sc.activation(small[:, 4:8], small[:, 0:4], ACT.Ln, bias=eps(ALL), scale=1 / 256).then_inc(sg_ln.sem, 1)
                sc.wait_ge(*sg_ln(l, 1))
                sc.activation(small[:, 8:12], small[:, 4:8], ACT.Exp, scale=-0.5).then_inc(sg_rs.sem, 1)

                def head_rstd(i):
                    sc.wait_ge(*hd_ss(l, i + 1))
                    rsqrt(i % 2, bank[3 + i % 2], slice(0, QK1), 1.0 if i < 4 else 1 / QK1,
                          "eps96" if i < 4 else "eps", hd_ln, (l, i + 1), hd_rs,
                          hd_n(l, i - 1) if i >= 2 else lat_n(l, 3))

                for i in range(8):
                    g = 10 + i
                    rows = slice(0, QK1) if i < 4 else slice(0, NOPE1)
                    sc.wait_ge(*z_mm(l, g + 1))
                    if i >= 2:
                        sc.wait_ge(*hd_ss(l, i - 1))
                    sc.activation(sq[rows, i % 2, :], bank[g % 3][rows, :], ACT.Square).then_inc(hd_sq.sem, 1)
                    sc.activation((m1["qh"] if i < 4 else m1["kh"])[rows, i % 4, :], bank[g % 3][rows, :], ACT.Copy)\
                        .then_inc(z_out.sem, 1)
                    if i >= 1:
                        head_rstd(i - 1)
                head_rstd(7)
                for m in range(NT):
                    sc.wait_ge(*z_mm(l, 19 + m))
                    sc.activation(m1["V"][:, m, :], bank[(18 + m) % 3][:, :], ACT.Copy).then_inc(z_out.sem, 1)
                for b in range(2):
                    sc.wait_ge(*sg_g(l, b + 1))
                    sc.activation(h[:, 4 + b, :], m1["mix"][:, 4 + b, :], ACT.Square).then_inc(mx_sq.sem, 1)
                for b in range(2):
                    col = par[:, PAR1["pool_scale"]][:, b:b + 1]
                    sc.wait_ge(*pl_mm(l, b + 1))
                    sc.activation(h[:, 6 + b, :], bank[5 + b][:, :], ACT.Square, scale=col).then_inc(mx_sq.sem, 1)
                    sc.activation(m1["mix"][:, 6 + b, :], bank[5 + b][:, :], ACT.Copy, scale=col)\
                        .then_inc(pl_o.sem, 1)

                def mix_rstd(i):
                    sc.wait_ge(*mx_ss(l, i + 1))
                    rsqrt(i % 2, bank[(3, 4, 3)[i]], ALL, (1 / 256, 1 / 256, 1 / 512)[i], "eps", mx_ln, (l, i + 1),
                          mx_rs, hd_n(l, 8) if i < 2 else mx_n(l, 2))

                mix_rstd(0)
                mix_rstd(1)
                for u in range(HEADS1 + 1):
                    if u < HEADS1:
                        exps(at1, l, u)
                    if u >= 1:
                        w = u - 1
                        turned_copies(at1, l, w)
                        sc.wait_ge(*at1["pv"](l, w + 1))
                        sc.activation(h[:, w, :], bank[w % 2][:, :], ACT.Square).then_inc(mx_sq.sem, 1)
                        sc.activation(m1["mix"][:, w, :], bank[w % 2][:, :], ACT.Copy).then_inc(o1_out.sem, 1)
                for n, c in enumerate(MIX_ORDER):
                    if n == 4:
                        mix_rstd(2)
                    sc.wait_ge(*mx_n(l, n + 1))
                    sc.activation(mix_hi[c], m1["mix"][:, c, :], ACT.Copy).then_inc(wo_h.sem, 1)

            def mixer2(l):
                def copy_out(key):
                    name, i = key
                    g = Y[key][0]
                    b = y_bank(g)
                    sc.wait_ge(*y_mm(l, g + 1))
                    tok = b[:, :].rearrange("p (m n) -> p m n", m=NT)
                    cols = slice(i * P, i * P + P)
                    if name == "hf":
                        sc.activation(m2["hk"][:, i, :], b[:, :], ACT.Sigmoid, scale=-1.0).then_inc(hf_s.sem, 1)
                        last = sc.activation(m2["hlf"][:, i, :], b[:, :], ACT.Sigmoid)
                    elif name == "glr":
                        last = sc.activation(ropec[0:16, :], b[0:16, :], ACT.Copy)
                    elif name == "ngate":
                        last = sc.activation(m2["gate"].rearrange("p m n -> p (m n)"), b[:, 0:NT * 24], ACT.Sigmoid)
                    elif name == "gdec":
                        col = par[:, PAR2["gla_b"]][:, i:i + 1]
                        sc.activation(m2["gk"][:, i, :], b[:, :], ACT.Abs, bias=col).then_inc(gl_a.sem, 1)
                        last = sc.activation(m2["glf"][:, i, :], b[:, :], ACT.Identity, bias=col)
                    elif name == "hq":
                        last = sc.activation(m2["hq"][:, i, :], b[:, :], ACT.Silu)
                    elif name in ("hi", "gv", "nv"):
                        last = sc.activation(m2[{"hi": "hv"}.get(name, name)][:, :, cols], tok, ACT.Copy)
                    elif name in ("gq", "nq"):
                        last = sc.activation(m2[name][:, i, :], b[:, :], ACT.Copy, scale=0.125)
                    else:
                        if name == "gk":
                            sc.wait_ge(*gl_d(l, i + 1))
                        dst = {"hog": "hy", "gog": "gy", "gk": "gk", "nkc": "ck", "nks": "ks", "nkw": "kw", "nvc": "cv"}[name]
                        last = sc.activation(m2[dst][:, i, :], b[:, :], ACT.Copy)
                    last.then_inc(y_out.sem, 1)

                for j in range(ND):
                    sc.wait_ge(*h_ready(4 + 2 * l, j + 1))
                    sc.activation(h_tmp[j], h[:, j, :], ACT.Copy).then_inc(hh_t.sem, 1)
                for key in YKEYS[:WHOLE]:
                    copy_out(key)
                sc.wait_ge(*hh_l(l, ND))
                for j in range(ND):
                    sc.activation(h_hi[:, j, :], h_tmp[j].bitcast(F32), ACT.Copy).then_inc(hh_r.sem, 1)
                for key in YKEYS[WHOLE:BEFORE - 4]:
                    copy_out(key)
                for i in range(2):
                    sc.wait_ge(*gl_a(l, i + 1))
                    sc.activation(m2["gk"][:, i, :], m2["gk"][:, i, :], ACT.Exp, scale=-1.0).then_inc(gl_e.sem, 1)
                for i in range(4):
                    sc.wait_ge(*hf_f(l, i + 1))
                    sc.activation(m2["hlf"][:, i, :], m2["hlf"][:, i, :], ACT.Ln).then_inc(hf_l.sem, 1)
                for i in range(2):
                    sc.wait_ge(*gl_e(l, i + 1))
                    sc.activation(m2["gk"][:, i, :], m2["gk"][:, i, :], ACT.Ln, bias=1.0).then_inc(gl_l.sem, 1)

                for key in YKEYS[BEFORE - 4:BEFORE]:
                    copy_out(key)

                def out_copy(hd):
                    if hd >= 2:
                        sc.wait_ge(*lo_ss(l, hd - 1))
                        sc.wait_ge(*lo_y(l, hd - 1))
                    sc.wait_ge(*ln_pv(l, hd + 1))
                    sc.activation(sq[:, hd % 2, :], bank[7][:, :], ACT.Square).then_inc(lo_sq.sem, 1)
                    sc.activation(m2["ob"][:, hd % 2, :], bank[7][:, :], ACT.Copy).then_inc(lo_o.sem, 1)

                def out_rstd(hd):
                    sc.wait_ge(*lo_ss(l, hd + 1))
                    rsqrt(hd % 2, bank[7], ALL, 1 / P, "eps", lo_ln, (l, hd + 1), lo_rs,
                          lo_n(l, hd - 1) if hd >= 2 else None)

                for u, q, k, lf, heads in LIN:
                    if u >= 4:
                        for head, _, _ in LIN[u - 1][4]:
                            out_copy(head)
                            out_rstd(head)
                    for v in range(10):
                        m = (1 << v) >> 1
                        if v >= 1:
                            if v == 1:
                                sc.wait_ge(*(hf_l(l, u + 1) if u < 4 else gl_f(l, u - 3)))
                                if u > 0:
                                    sc.wait_ge(*ln_q(l, 9 * u))
                            else:
                                sc.wait_ge(*ln_p(l, 8 * u + v - 1))
                                sc.wait_ge(*ln_q(l, 9 * u + v - 1))
                            sc.activation(compact(m2["Eq"], m), halves(lf, m, 1), ACT.Exp).then_inc(ln_e.sem, 1)
                        if v >= 2:
                            sc.wait_ge(*ln_x(l, 8 * u + v - 1))
                            if 8 * u + v - 2 > 0:
                                sc.wait_ge(*ln_k(l, 8 * u + v - 2))
                            sc.activation(compact(m2["Ek"], m), halves(m2["X"], m, 0), ACT.Exp).then_inc(ln_f.sem, 1)
                        if (u, v) in FILL and FILL[u, v][1] == 1:
                            copy_out(FILL[u, v][0])
                        if (u, v) in ((1, 4), (4, 8)):
                            gates = m2["hy" if u == 1 else "gy"].rearrange("p a b -> p (a b)")
                            sc.wait_ge(*y_out(l, Y["hog" if u == 1 else "gog", 3][0] + 1))
                            sc.activation(gates, gates, ACT.Silu).then_inc(og_s.sem, 1)
                        if 0 < u < 4 and v == 3:
                            out_copy(u - 1)
                        if 0 < u < 4 and v == 5:
                            out_rstd(u - 1)
                for head, _, _ in LIN[-1][4]:
                    out_copy(head)
                    out_rstd(head)

                for kv, (b1, b2) in enumerate(((6, 3), (4, 5))):
                    sc.wait_ge(*ch_mm(l, 2 * kv + 2))
                    sc.activation(small[:, 40 + kv:41 + kv], bank[b2][:, 0:1], ACT.Copy).then_inc(ch_b.sem, 1)
                    sc.wait_ge(*ch_b(l, kv + 1))
                    sc.activation(m2["hid"][:, 62 * (1 - kv):62 * (1 - kv) + 62], bank[b1][:, 0:62], ACT.Gelu_apprx_tanh,
                                  bias=small[:, 40 + kv:41 + kv]).then_inc(ch_g.sem, 1)
                sc.wait_ge(*cc_mm(l, 1))
                sc.activation(m2["vc"][0:NCMP, :], bank[1][0:NCMP, 0:P], ACT.Copy).then_inc(cc_o.sem, 1)
                sc.wait_ge(*cc_mm(l, 2))
                sc.activation(m2["kc"], bank[0][:, 0:62], ACT.Copy).then_inc(cc_o.sem, 1)
                for p in range(5):
                    if p < 4:
                        sc.wait_ge(*cs_d(l, p + 1))
                        sc.activation(cm[p % 2], cm[p % 2], ACT.Exp).then_inc(cs_e.sem, 1)
                    for hd in range(2 * p - 2, 2 * p) if p else ():
                        sc.wait_ge(*cs_t(l, hd + 1))
                        sc.activation(m2["cmpT"][0:NCMP, hd, :], bank[4 + hd % 2][0:NCMP, :], ACT.Copy)\
                            .then_inc(cs_o.sem, 1)
                for u in range(17):
                    if u < 16:
                        exps(at2, l, u)
                    if u >= 1:
                        w = u - 1
                        turned_copies(at2, l, w)
                        if w % 4 == 3:
                            sc.wait_ge(*at2["pv"](l, w + 1))
                            sc.activation(m2["nq"][:, w // 4, :], bank[(w // 4) % 2][:, :], ACT.Copy)\
                                .then_inc(no_y.sem, 1)
                with sc.Fori(0, 4) as it:
                    for r in range(6):
                        sc.wait_ge(mg_mm.sem, l * 24 + it * 6 + (r + 1))
                        sc.wait_ge(br_m.sem, l * 24 + it * 6 + (br_m.start + r - 5))
                        sc.activation(m2["sig"][:, r, :], bank[r % 3][:, :], ACT.Sigmoid).then_inc(mg_s.sem, 1)
                sc.wait_ge(*br_a(l, 16))
                for j in range(ND):
                    sc.activation(m_hi[j], m2["m"][:, j, :], ACT.Copy).then_inc(wo_h.sem, 1)

            sc.wait_ge(s_const, 16)
            sc.sem_inc(silu.sem, silu.start)
            sc.sem_inc(mg_s.sem, mg_s.start)
            R1 = slice(64, 96)
            sc.wait_ge(s_rope, 9)
            sc.activation(m1["cos"][R1, :], m1["sin"][R1, :], ACT.Sin, scale=0.5).then_inc(s_ropea, 1)
            sc.wait_ge(s_ropea, 1)
            sc.activation(m1["sin"][R1, :], m1["sin"][R1, :], ACT.Sin).then_inc(s_ropea, 1)
            sc.wait_ge(lb_s, 3)
            sc.activation(lbt[:, 0:8], lbt[:, 0:8], ACT.Exp).then_inc(lb_e, 1)
            with sc.Fori(0, LAYERS) as l:
                norm(2 * l)
                mixer1(l)
                norm(2 * l + 1)
                ffn(l)
            with sc.Fori(0, LAYERS) as l:
                norm(2 * l + 4)
                mixer2(l)
                norm(2 * l + 5)
                ffn(l + LAYERS)
            norm(8)

        @block.vector
        def _(ve):
            def mul(out, a, b):
                return ve.tensor_tensor(out, a, b, ALU.mult)

            def add(out, a, b):
                return ve.tensor_tensor(out, a, b, ALU.add)

            def norm(n, nf, gains):
                ve.wait_ge(*n_rs(n, 1))
                if nf is not None:
                    ve.wait_ge(*s_par(nf, 16))
                for j in range(ND):
                    ve.scalar_tensor_tensor(h[:, j, :], x[:, j, :], gains[:, j:j + 1], rstd[:, 0, :],
                                            ALU.mult, ALU.mult).then_inc(h_ready.sem, 1)

            def ffn_norm(n, nf, gains):
                ve.wait_ge(*n_rs(n, 1))

                def low(j):
                    ve.wait_ge(*h_h(nf, j + 1))
                    ve.tensor_tensor(h_lo[:, j, :], sil[:, j % 3, :], h_hi[:, j, :].bitcast(F32),
                                     ALU.subtract).then_inc(h_ready.sem, 1)

                for j in range(ND):
                    if j >= 3:
                        ve.wait_ge(*h_ready(n, j - 2))
                    ve.scalar_tensor_tensor(sil[:, j % 3, :], x[:, j, :], gains[:, j:j + 1], rstd[:, 0, :],
                                            ALU.mult, ALU.mult).then_inc(h_v.sem, 1)
                    if j >= 1:
                        low(j - 1)
                low(ND - 1)

            def ffn(nf):
                def hidden(g, r, it):
                    ve.wait_ge(silu.sem, nf * FB + it * RING + (silu.start + g + 1))
                    ve.wait_ge(gu_mm.sem, nf * gu_mm.per + it * 6 + (2 * g + 2))
                    if isinstance(it, int):
                        hi, lo = act_hi[:, g, :], act_lo[:, g, :]
                    else:
                        hi, lo = (a[:, bass.ds(it * 3 + g, 1), :].rearrange("p a t -> p (a t)")
                                  for a in (act_hi, act_lo))
                    mul(sil[:, r, :], sil[:, r, :], bank[3 + r][:, :]).then_inc(act_v.sem, 1)
                    ve.wait_ge(act_v.sem, nf * FB + it * 3 + (g + 1))
                    ve.tensor_scalar(hi, sil[:, r, :], 1.0, None, ALU.mult).then_inc(act_h.sem, 1)
                    ve.wait_ge(act_h.sem, nf * FB + it * 3 + (g + 1))
                    ve.tensor_tensor(lo, sil[:, r, :], hi.bitcast(F32), ALU.subtract).then_inc(act_ready.sem, 1)

                with ve.Fori(0, 7) as it:
                    for r in range(3):
                        hidden(r, r, it)
                hidden(FB - 1, 0, 0)
                ve.wait_ge(*down_mm(nf, FB))
                for j in range(ND):
                    add(x[:, j, :], x[:, j, :], bank[j][:, :]).then_inc(x_ready.sem, 1)

            def w_out(nf):
                for j in range(ND):
                    ve.wait_ge(*wo_mm(nf, j + 1))
                    add(x[:, j, :], x[:, j, :], bank[j][:, :]).then_inc(x_ready.sem, 1)

            def maxima(s, l, u):
                for t in range(NT):
                    ve.wait_ge(*s["scores"](l, NT * u + t + 1))
                    c = 4 * (u % 2) + t
                    ve.reduce_max(small[:, 16 + c:17 + c], bank[3 + t][:, 0:(t + 1) * P], AX_X, negate=True)\
                        .then_inc(s["maxed"].sem, 1)

            def scale(s, l, u, gates):
                ve.wait_ge(*s["exped"](l, NT * (u + 1)))
                c = 4 * (u % 2)
                inv = small[:, 32 + c:36 + c]
                ve.reciprocal(inv, small[:, 24 + c:28 + c]).then_inc(s["recip"].sem, 1)
                ve.wait_ge(*s["recip"](l, u + 1))
                if gates is not None:
                    mul(inv, inv, gates).then_inc(s["gated"].sem, 1)
                    ve.wait_ge(*s["gated"](l, u + 1))
                for t in range(NT):
                    v = prob[:, u % 2, PS0[t]:PS0[t] + (t + 1) * P]
                    ve.tensor_scalar(v, v, small[:, 32 + c + t:33 + c + t], None, ALU.mult)\
                        .then_inc(s["scaled"].sem, 1)

            def mixer1(l):
                def gain(name, j, rows=slice(0, P)):
                    return par[rows, PAR1[name]][:, j:j + 1]

                def normed(out, src, g, rs, sig=None):
                    i = ve.scalar_tensor_tensor(out, src, g, rs, ALU.mult, ALU.mult)
                    if sig is not None:
                        i.then_inc(sig.sem, 1)
                    return i

                ve.wait_ge(*lat_rs(l, 1))
                for c in range(2):
                    if c == 0:
                        ve.wait_ge(*z_out(l, 2))
                    normed(m1["qlat"][:, c, :], m1["qlat"][:, c, :], gain("g_q", c), rstd[:, 0, :], lat_n)
                ve.wait_ge(*lat_rs(l, 2))
                normed(m1["kvlat"], m1["kvlat"], gain("g_kv", 0), rstd[:, 1, :], lat_n)
                ve.wait_ge(*z_out(l, 6))
                mul(sgt, m1["v"], m1["v"]).then_inc(sg_q.sem, 1)
                ve.wait_ge(*sg_q(l, 1))
                ve.tensor_reduce(small[:, 0:4], sgt, AX_X, ALU.add).then_inc(sg_ss.sem, 1)
                for hd in range(4):
                    w = par[:, PAR1["w_sp"]][:, hd * P:hd * P + P]
                    mul(w, w, C("causalT")).then_inc(sg_w.sem, 1)

                def head_norm(i):
                    ve.wait_ge(*hd_rs(l, i + 1))
                    ve.wait_ge(*z_out(l, 11 + i))
                    if i < 4:
                        v = m1["qh"][0:QK1, i, :]
                        normed(v, v, gain("g_qh", 0, slice(0, QK1)), rstd[0:QK1, i % 2, :], hd_n)
                    else:
                        v = m1["kh"][0:64, i - 4, :]
                        normed(v, v, gain("g_kh", 0, slice(0, 64)), rstd[0:64, i % 2, :])
                        normed(m1["kh"][64:96, i - 4, :], m1["krope"][64:96, :], gain("g_kh", 0, slice(64, 96)),
                               rstd[64:96, i % 2, :], hd_n)

                def head_rope(i):
                    ve.wait_ge(*hd_rot(l, i + 1))
                    r1 = slice(64, 96)
                    if i > 0:
                        ve.wait_ge(*hd_r(l, i))
                    v = (m1["qh"] if i < 4 else m1["kh"])[r1, i % 4, :]
                    mul(m1["tb"][r1, :], bank[5 + i % 2][r1, :], m1["sin"][r1, :]).then_inc(hd_t.sem, 1)
                    mul(v, v, m1["cos"][r1, :]).then_inc(hd_t.sem, 1)
                    ve.wait_ge(*hd_t(l, 2 * i + 2))
                    add(v, v, m1["tb"][r1, :]).then_inc(hd_r.sem, 1)

                for i in range(8):
                    head_norm(i)
                    if i >= 1:
                        head_rope(i - 1)
                head_rope(7)

                ve.wait_ge(*sg_rs(l, 1))
                for m in range(NT):
                    ve.scalar_tensor_tensor(m1["v"][:, m, :], m1["v"][:, m, :], small[:, 8 + m:9 + m],
                                            par[:, PAR1["g_sgu"]], ALU.mult, ALU.mult).then_inc(sg_v.sem, 1)

                steps = [0]

                def step(i):
                    steps[0] += 1
                    i.then_inc(pw.sem, 1)
                    ve.wait_ge(*pw(l, steps[0]))

                A, B = m1["win_a"], m1["win_b"]
                W = T + 16
                low, high = slice(0, 64), slice(64, P)
                step(ve.memset(m1["pin"][:, :, 0:16], 0.0))
                ve.wait_ge(*z_out(l, 10))
                for b in range(2):
                    p_ = m1["pin"][:, b, :]
                    if b > 0:
                        ve.wait_ge(*pl_m(l, b))
                    step(add(A[:, 1:W], p_[:, 1:W], p_[:, 0:W - 1]))
                    if b == 0:
                        step(add(B[high, 3:W], A[high, 3:W], A[high, 1:W - 2]))
                    else:
                        step(add(B[:, 3:W], A[:, 3:W], A[:, 1:W - 2]))
                        step(add(A[:, 7:W], B[:, 7:W], B[:, 3:W - 4]))
                        step(add(B[high, 15:W], A[high, 15:W], A[high, 7:W - 8]))
                    step(ve.tensor_copy(B[low, 16:W], A[low, 16:W]))
                    step(ve.scalar_tensor_tensor(m1["win_m"][:, b, :], B[:, 16:W], C("invwin")[:, b:b + 1],
                                                 p_[:, 16:W], ALU.mult, ALU.subtract))
                    step(mul(A[:, 0:16], B[:, 16:32], C("invcount")[:, 16 * b:16 * b + 16]))
                    ve.tensor_tensor(m1["win_m"][:, b, 0:16], A[:, 0:16], p_[:, 16:32], ALU.subtract)\
                        .then_inc(pl_m.sem, 1)
                assert steps[0] == pw.per, steps[0]

                for b in range(2):
                    ve.wait_ge(*sg_mm(l, b + 1))
                    v = m1["mix"][:, 4 + b, :]
                    bias = par[:, PAR1["b_sp"]][:, b * P:b * P + P].unsqueeze(1).broadcast_to([P, NT, P])
                    add(v.rearrange("p (a b) -> p a b", a=NT), bank[3 + b][:, :].rearrange("p (a b) -> p a b", a=NT),
                        bias).then_inc(sg_z.sem, 1)
                    ve.wait_ge(*sg_z(l, b + 1))
                    mul(v, v, m1["u"][:, b, :]).then_inc(sg_g.sem, 1)

                def mix_norm(i):
                    ve.wait_ge(*mx_rs(l, i + 1))
                    if i == 1:
                        ve.wait_ge(*pl_o(l, 2))
                    for c in ((4, 5), (6, 7), (0, 1, 2, 3))[i]:
                        v = m1["mix"][:, c, :]
                        normed(v, v, gain("g_out", c), rstd[:, i % 2, :], mx_n)

                mix_norm(0)
                mix_norm(1)
                for u in range(HEADS1 + 1):
                    if u >= 1:
                        scale(at1, l, u - 1, None)
                    if u < HEADS1:
                        maxima(at1, l, u)
                ve.wait_ge(*o1_out(l, HEADS1))

                def low(n):
                    c = MIX_ORDER[n]
                    ve.wait_ge(*wo_h(l, n + 1))
                    ve.tensor_tensor(h_lo[:, c, :], m1["mix"][:, c, :], mix_hi[c].bitcast(F32),
                                     ALU.subtract).then_inc(wo_r.sem, 1)

                for n in range(4):
                    low(n)
                mix_norm(2)
                for n in range(4, ND):
                    low(n)
                w_out(l)

            def mixer2(l):
                for j in range(ND):
                    ve.wait_ge(*hh_t(l, j + 1))
                    ve.tensor_tensor(h_lo[:, j, :], h[:, j, :], h_tmp[j].bitcast(F32), ALU.subtract)\
                        .then_inc(hh_l.sem, 1)
                for n in range(2):
                    ve.tensor_copy(lbt[:, 32 + 4 * n:36 + 4 * n], lbt[:, bass.ds(l * 4 + (16 + 8 * n), 4)])\
                        .then_inc(lb_l.sem, 1)
                ve.wait_ge(*lb_l(l, 2))
                for i in range(4):
                    lb, om = lbt[:, 32 + i:33 + i], lbt[:, 36 + i:37 + i]
                    kk, f = m2["hk"][:, i, :], m2["hlf"][:, i, :]
                    ve.wait_ge(*y_out(l, Y["hf", i][0] + 1))
                    ve.tensor_scalar(kk, kk, om, None, ALU.mult).then_inc(hf_k.sem, 1)
                    ve.tensor_scalar(f, f, om, lb, ALU.mult, ALU.add).then_inc(hf_m.sem, 1)
                    ve.wait_ge(*hf_m(l, i + 1))
                    ve.tensor_scalar(f, f, 1e-19, None, ALU.max).then_inc(hf_f.sem, 1)
                for i in range(2):
                    f = m2["glf"][:, i, :]
                    ve.wait_ge(*gl_l(l, i + 1))
                    ve.scalar_tensor_tensor(f, f, 0.0, m2["gk"][:, i, :], ALU.min, ALU.subtract)\
                        .then_inc(gl_d.sem, 1)
                    ve.wait_ge(*gl_d(l, i + 1))
                    ve.tensor_scalar(f, f, 1 / 16, None, ALU.mult).then_inc(gl_f.sem, 1)

                def place(v, group0, heads):
                    for n, (hd, _, _) in enumerate(heads):
                        g = group0 + v * len(heads) + n
                        b = bank[3 + g % 4]
                        s = ST[hd % 2]
                        if v == 0 and hd >= 2:
                            ve.wait_ge(*ln_pv(l, hd - 1))
                        ve.wait_ge(*ln_mm(l, g + 1))
                        if g > 0:
                            ve.wait_ge(*ln_st(l, g))
                        if v < 8:
                            mask = C("levels")[:, v * P:v * P + P].unsqueeze(1).broadcast_to([P, NT, P])
                            src = b[:, :].rearrange("p (a b) -> p a b", a=NT)
                            if v == 0:
                                last = mul(diag4(hd % 2), src, mask)
                            else:
                                ve.memset(small[:, 60:61], 0.0)
                                last = ve.copy_predicated(diag4(hd % 2), mask.bitcast(U32), src)
                        elif v == 8:
                            ve.tensor_copy(s[:, 0, P:2 * P], b[:, 0:P])
                            last = ve.tensor_copy(s[:, 2, 3 * P:T], b[:, P:2 * P])
                        else:
                            last = ve.tensor_copy(s[:, 0:2, 2 * P:T],
                                                  b[:, :].rearrange("p (a b) -> p a b", a=2))
                        last.then_inc(ln_st.sem, 1)

                def lin_out(hd):
                    ve.wait_ge(*lo_rs(l, hd + 1))
                    ve.wait_ge(*lo_o(l, hd + 1))
                    o = m2["ob"][:, hd % 2, :]
                    g = par[:, PAR2["g_hg" if hd < 4 else "g_gla"]][:, hd % 4:hd % 4 + 1]
                    ve.scalar_tensor_tensor(o, o, g, rstd[:, hd % 2, :], ALU.mult, ALU.mult).then_inc(lo_n.sem, 1)
                    ve.wait_ge(*lo_n(l, hd + 1))
                    y = lin_gate(hd)
                    ve.wait_ge(*og_s(l, 1 if hd < 4 else 2))
                    mul(y, y, o).then_inc(lo_y.sem, 1)

                group0 = 0
                for u, q, k, lf, heads in LIN:
                    X = m2["X"]
                    if u >= 4:
                        for hd, _, _ in LIN[u - 1][4]:
                            lin_out(hd)
                    if u == 0:
                        ve.memset(qsl[:, :, :], 0.0)
                    ve.memset(X, 0.0).then_inc(ln_x0.sem, 1)
                    for v in range(1, 10):
                        m = 1 << (v - 1)
                        qo, ko = qsl[:, v % 2, :], ksl[:, v % 2, :]
                        if v == 1:
                            ve.wait_ge(*ln_x0(l, u + 1))
                        ve.wait_ge(*ln_e(l, 9 * u + v))
                        if v == 1 and u >= 4:
                            ve.wait_ge(*y_out(l, Y["gq", u - 4][0] + 1))
                        elif v == 1:
                            ve.wait_ge(*y_out(l, Y["hq", u][0] + 1))
                        mul(halves(qo, m, 1), halves(q, m, 1), compact(m2["Eq"], m)).then_inc(ln_q.sem, 1)
                        if v >= 2:
                            ve.wait_ge(*ln_f(l, 8 * u + v - 1))
                            mul(halves(ko, m, 0), halves(k, m, 0), compact(m2["Ek"], m)).then_inc(ln_k.sem, 1)
                        if v <= 8:
                            if v > 1:
                                ve.wait_ge(*ln_p(l, 8 * u + v - 1))
                            add(halves(X, m, 0), halves(X, m, 0), ends(lf, m, 1)).then_inc(ln_x.sem, 1)
                            ve.wait_ge(*ln_x(l, 8 * u + v))
                            add(halves(lf, m, 1), halves(lf, m, 1), ends(lf, m, 0)).then_inc(ln_p.sem, 1)
                        place(v - 1, group0, heads)
                        if 0 < u < 4 and v == 6:
                            lin_out(u - 1)
                    place(9, group0, heads)
                    group0 += 10 * len(heads)
                for hd, _, _ in LIN[-1][4]:
                    lin_out(hd)

                ve.wait_ge(*y_out(l, YN))
                cv = m2["cv"]
                ve.tensor_copy(cv[0:64, 1, :], cv[64:P, 0, :]).then_inc(cv_o.sem, 1)
                ve.wait_ge(*cv_o(l, 1))
                ve.tensor_copy(cv[64:P, 0, 0:T - 1], cv[0:64, 0, 1:T]).then_inc(cv_o.sem, 1)
                ve.tensor_copy(cv[64:P, 1, 0:T - 1], cv[0:64, 1, 1:T]).then_inc(cv_o.sem, 1)

                for i in range(7):
                    ve.wait_ge(*rp_mm(l, i + 1))
                    if i > 0:
                        ve.wait_ge(*rp_o(l, (4, 5, 6, 7, 8, 12)[i - 1]))
                    mul(ropes, bank[i % 2][:, :], C("sin2")).then_inc(rp_u.sem, 1)
                    mul(ropec, raw_block(i), C("cos2")).then_inc(rp_t.sem, 1)
                    ve.wait_ge(*rp_u(l, i + 1))
                    ve.wait_ge(*rp_t(l, i + 1))
                    if 1 <= i < 5:
                        add(m2["nq"][:, i - 1, :], ropec, ropes).then_inc(rp_o.sem, 1)
                        continue
                    dst = m2[{0: "ck", 5: "ks", 6: "kw"}[i]]
                    for g in range(2):
                        src = slice(64 * g, 64 * g + 64)
                        add(dst[0:64, g, :], ropec[src, :], ropes[src, :]).then_inc(rp_o.sem, 1)
                        d = 1 if i == 0 else 0
                        add(dst[64:P, g, 0:T - d], ropec[src, d:T], ropes[src, d:T]).then_inc(rp_o.sem, 1)

                def per_tile(a):
                    return a.rearrange("p h a -> p (h a)").unsqueeze(2).broadcast_to([P, 2 * NT, NCMP])

                gates = m2["gate"].rearrange("p m (h b) -> p h m b", b=3)
                for p in range(4):
                    c = cm[p % 2].rearrange("p h (a b) -> p (h a) b", a=NT)
                    for hd in (2 * p, 2 * p + 1):
                        if p >= 2:
                            ve.wait_ge(*cs_t(l, 2 * p - 2))
                        ve.wait_ge(*cs_mm(l, hd + 1))
                        add(cm[p % 2][:, hd % 2, :], bank[2 + hd % 2][:, 0:NT * NCMP], C("negcmp"))\
                            .then_inc(cs_m.sem, 1)
                    ve.wait_ge(*cs_m(l, 2 * p + 2))
                    ve.reduce_max(cm_max.rearrange("p h a -> p (h a)"), c, AX_X).then_inc(cs_x.sem, 1)
                    ve.wait_ge(*cs_x(l, p + 1))
                    ve.tensor_tensor(c, c, per_tile(cm_max), ALU.subtract).then_inc(cs_d.sem, 1)
                    ve.wait_ge(*cs_e(l, p + 1))
                    ve.tensor_reduce(cm_sum.rearrange("p h a -> p (h a)"), c, AX_X, ALU.add).then_inc(cs_s.sem, 1)
                    ve.wait_ge(*cs_s(l, p + 1))
                    ve.reciprocal(cm_rec, cm_sum).then_inc(cs_r.sem, 1)
                    ve.wait_ge(*cs_r(l, p + 1))
                    mul(cm_rec, cm_rec, C("validcmp").unsqueeze(1).broadcast_to([P, 2, NT])).then_inc(cs_v.sem, 1)
                    ve.wait_ge(*cs_v(l, p + 1))
                    mul(cm_rec, cm_rec, gates[:, 2 * p:2 * p + 2, :, 0]).then_inc(cs_g.sem, 1)
                    ve.wait_ge(*cs_g(l, p + 1))
                    mul(c, c, per_tile(cm_rec)).then_inc(cs_p.sem, 1)

                for u in range(17):
                    if u >= 1:
                        w = u - 1
                        scale(at2, l, w, m2["gate"][:, :, 3 * (w // 2) + 1 + w % 2])
                    if u < 16:
                        maxima(at2, l, u)

                with ve.Fori(0, 4) as it:
                    for r in range(6):
                        j, b = r // 3, r % 3
                        ve.wait_ge(mg_s.sem, l * 24 + it * 6 + (mg_s.start + r + 1))
                        ve.wait_ge(br_mm.sem, l * 24 + it * 6 + (r + 1))
                        m = m2["m"][:, bass.ds(it * 2 + j, 1), :].rearrange("p a t -> p (a t)")
                        out = (m, ropec, ropes)[b]
                        mul(out, m2["sig"][:, r, :], bank[3 + r % 3][:, :]).then_inc(br_m.sem, 1)
                        ve.wait_ge(br_m.sem, l * 24 + it * 6 + (br_m.start + r + 1))
                        if b == 2:
                            ve.wait_ge(br_a.sem, l * 16 + it * 4 + (2 * j + 1))
                        if b > 0:
                            add(m, m, out).then_inc(br_a.sem, 1)
                        if b == 2:
                            ve.wait_ge(br_a.sem, l * 16 + it * 4 + (2 * j + 2))
                for j in range(ND):
                    ve.wait_ge(*wo_h(l + LAYERS, j + 1))
                    ve.tensor_tensor(m_lo[j], m2["m"][:, j, :], m_hi[j].bitcast(F32), ALU.subtract)\
                        .then_inc(wo_r.sem, 1)
                w_out(l + LAYERS)

            ve.sem_inc(act_ready.sem, act_ready.start)
            ve.sem_inc(br_m.sem, br_m.start)
            ve.sem_inc(h_ready.sem, h_ready.start)
            for j in range(0, ND, 2):
                ve.wait_ge(s_x0[j // 2], 16)
                ve.sem_inc(x_ready.sem, 2)
            ve.memset(ksl[:, :, :], 0.0).then_inc(s_init, 1)
            R1 = slice(64, 96)
            ang, turns, pf = m1["sin"][R1, :], m1["cos"][R1, :], m1["tb"][R1, :]
            ve.wait_ge(s_const, 16)
            ve.wait_ge(s_pos, 16)
            k = [0]

            def step(i):
                k[0] += 1
                i.then_inc(s_rope, 1)
                ve.wait_ge(s_rope, k[0])

            step(ve.tensor_copy(pf, m1["ta"][R1, :].bitcast(I32)))
            step(ve.tensor_scalar(ang, pf, C("invfreq", R1), None, ALU.mult))
            step(ve.tensor_scalar(turns, ang, 1 / (2 * math.pi), 12582912.0, ALU.mult, ALU.add))
            step(ve.tensor_scalar(turns, turns, 12582912.0, None, ALU.subtract))
            for part in TWO_PI_PARTS:
                step(ve.scalar_tensor_tensor(ang, turns, -part, ang, ALU.mult, ALU.add))
            step(ve.tensor_scalar(ang, ang, 3.1415925, -3.1415925, ALU.min, ALU.max))
            a, b = C("lb")[:, 0:4], C("lb")[:, 4:8]
            ve.tensor_tensor(lbt[:, 8:12], a, b, ALU.max).then_inc(lb_s, 1)
            ve.wait_ge(lb_s, 1)
            ve.tensor_tensor(lbt[:, 0:4], a, lbt[:, 8:12], ALU.subtract).then_inc(lb_s, 1)
            ve.tensor_tensor(lbt[:, 4:8], b, lbt[:, 8:12], ALU.subtract).then_inc(lb_s, 1)
            ve.wait_ge(lb_e, 1)
            n = [3]

            def lb_step(i):
                n[0] += 1
                i.then_inc(lb_s, 1)
                ve.wait_ge(lb_s, n[0])

            lb_step(add(lbt[:, 8:12], lbt[:, 0:4], lbt[:, 4:8]))
            lb_step(ve.reciprocal(lbt[:, 12:16], lbt[:, 8:12]))
            lb_step(mul(lbt[:, 0:4], lbt[:, 0:4], lbt[:, 12:16]))
            lb_step(mul(lbt[:, 4:8], lbt[:, 4:8], lbt[:, 12:16]))
            lb_step(add(lbt[:, 8:12], lbt[:, 0:4], lbt[:, 4:8]))
            lb_step(ve.tensor_tensor(lbt[:, 16:20], lbt[:, 0:4], lbt[:, 0:4], ALU.subtract))
            lb_step(ve.tensor_tensor(lbt[:, 20:24], lbt[:, 8:12], lbt[:, 0:4], ALU.subtract))
            lb_step(ve.tensor_scalar(lbt[:, 24:32], lbt[:, 16:24], -1.0, 1.0, ALU.mult, ALU.add))
            ve.wait_ge(s_ropea, 2)
            step(mul(turns, turns, turns))
            step(ve.tensor_scalar(turns, turns, -2.0, 1.0, ALU.mult, ALU.add))
            with ve.Fori(0, LAYERS) as l:
                norm(2 * l, l, par[:, PAR1["g_in"]])
                mixer1(l)
                ffn_norm(2 * l + 1, l, par[:, PAR1["g_ffn"]])
                ffn(l)
            with ve.Fori(0, LAYERS) as l:
                norm(2 * l + 4, l + LAYERS, par[:, PAR2["g_in"]])
                mixer2(l)
                ffn_norm(2 * l + 5, l + LAYERS, par[:, PAR2["g_ffn"]])
                ffn(l + LAYERS)
            norm(8, None, C("gfinal"))


def parts_of_two_pi():
    out, rest = [], 2 * math.pi
    for _ in range(4):
        e = math.floor(math.log2(rest))
        q = 2.0 ** (e - 7)
        out.append(math.floor(rest / q) * q)
        rest -= out[-1]
    return out


TWO_PI_PARTS = parts_of_two_pi()


def constants(hg_lb, final_norm_g):
    c = np.zeros((P, NCONST), np.float32)
    i = np.arange(P)
    c[:, CONST["ident"]] = np.eye(P)
    c[:, CONST["ones"]] = 1
    c[:, CONST["negdiag"]] = np.where(i[None] > i[:, None], NEG, 0)
    c[:, CONST["causalT"]] = i[None] >= i[:, None]
    rot = np.zeros((P, P))
    for m in range(P):
        if m % 64 < 8:
            rot[m + 8, m] = -1
        elif m % 64 < 16:
            rot[m - 8, m] = 1
    c[:, CONST["rot2"]] = rot
    rot = np.zeros((P, QK1))
    for m in range(32):
        rot[64 + (m + 16) % 32, 64 + m] = -1 if m < 16 else 1
    c[:, CONST["rot1"]] = rot
    levels = [np.eye(P)]
    for m in LEVELS:
        same = i[:, None] // (2 * m) == i[None] // (2 * m)
        levels.append(same & (i[:, None] // m % 2 == 0) & (i[None] // m % 2 == 1))
    c[:, CONST["levels"]] = np.concatenate(levels, 1)
    t = np.arange(T)
    inv = np.float32(500000.0) ** (-np.arange(0, 16, 2, dtype=np.float32) / np.float32(16))
    ang = t.astype(np.float32)[None] * inv.astype(np.float32)[:, None]
    cos, sin = np.ones((P, T)), np.zeros((P, T))
    for m in range(P):
        if m % 64 < 16:
            cos[m], sin[m] = np.cos(ang[m % 8]), np.sin(ang[m % 8])
    c[:, CONST["cos2"]], c[:, CONST["sin2"]] = cos, sin
    ends = np.arange(NCMP) * 16 + 31
    neg = np.where(ends[None] <= t[:, None], 0, NEG).reshape(NT, P, NCMP)
    c[:, CONST["negcmp"]] = neg.transpose(1, 0, 2).reshape(P, -1)
    c[:, CONST["validcmp"]] = (t >= 31).reshape(NT, P).T
    wins = np.array([2, 4, 8, 16]).reshape(2, 2).repeat(64, 1)
    c[:, CONST["invwin"]] = 1 / wins.T
    count = np.minimum(np.arange(1, 17)[None, None], wins[:, :, None])
    c[:, CONST["invcount"]] = (1 / count).transpose(1, 0, 2).reshape(P, 32)
    f = np.float32(1) / (np.float32(10000.0) ** (np.arange(16, dtype=np.float32) / np.float32(16)))
    c[64:96, CONST["invfreq"]] = np.tile(f, 2)[:, None]
    c[:, CONST["eps"]] = EPS
    c[:, CONST["eps96"]] = EPS * QK1
    c[:, CONST["lb"]] = hg_lb.reshape(LAYERS, 4, P).transpose(2, 0, 1).reshape(P, 8)
    c[:, CONST["gfinal"]] = final_norm_g.reshape(ND, P).T
    return c


def column_tiles(w):
    k, n = w.shape
    nb = -(-n // P)
    full = np.zeros((k, nb * P), np.float32)
    full[:, :n] = w
    a = full.reshape(k // P, P, nb, P).transpose(2, 1, 0, 3).reshape(nb, P, k // P * P)
    return pad_tiles(a)


def pad_tiles(a):
    out = np.zeros((a.shape[0], P, TILE), np.float32)
    out[:, :, :a.shape[2]] = a
    return out


def ffn_tiles(gate, up, down):
    g, u = column_tiles(gate), column_tiles(up)
    return [np.stack([g, u], 1).reshape(2 * FB, P, TILE), down.reshape(FB, P, D)]


def stream1(w_in, w_q_up, w_kv_up, w_out, gate, up, down):
    rope = np.zeros((D, P), np.float32)
    rope[:, 64:96] = w_in[:, 384:416]
    q_up = w_q_up.reshape(2, P, 384).transpose(1, 0, 2).reshape(1, P, 768)
    kv = w_kv_up.reshape(P, HEADS1, 192)
    kv = np.concatenate([kv[:, :, :64].reshape(P, 256), kv[:, :, 64:].reshape(P, 512)], 1)[None]
    return np.concatenate([
        column_tiles(w_in[:, :384]), column_tiles(rope), column_tiles(w_in[:, 672:928]),
        column_tiles(w_in[:, 416:672]), column_tiles(w_in[:, 928:1184]), pad_tiles(q_up), pad_tiles(kv),
        column_tiles(w_out), np.zeros((1, P, TILE), np.float32), *ffn_tiles(gate, up, down)])


def stream2(w_in, w1_k, w1_v, branches, w_out, gate, up, down):
    sizes = dict(hq=512, hf=512, hi=512, hog=512, gq=256, gk=256, gv=512, glr=16, gog=512, nq=512, nkc=128,
                 nvc=128, nks=128, nvs=128, nkw=128, nvw=128, ngate=24, mgate=3072)
    s, at = {}, 0
    for name, n in sizes.items():
        s[name] = w_in[:, at:at + n]
        at += n
    s["low_rank_and_gate"] = np.concatenate([s["glr"], s["ngate"]], 1)
    out = [column_tiles(s[n]) for n in ("hi", "gv", "nvs", "nvw", "low_rank_and_gate", "hf", "hq", "hog", "gk",
                                        "gq", "gog", "nq", "nkc", "nks", "nkw", "nvc")]
    out += [w.reshape(2, 8, P, P).transpose(0, 2, 1, 3).reshape(2, P, TILE) for w in (w1_v, w1_k)]
    mg = column_tiles(s["mgate"]).reshape(3, ND, P, TILE)
    br = np.stack([w.reshape(4, P, ND, P).transpose(2, 1, 0, 3).reshape(ND, P, 512) for w in branches], 1)
    for i in range(0, ND, 2):
        out.append(mg[:, i:i + 2].transpose(1, 0, 2, 3).reshape(6, P, TILE))
        out.append(br[i:i + 2].reshape(3, 2, P, 512).transpose(0, 2, 1, 3).reshape(3, P, TILE))
    return np.concatenate(out + [column_tiles(w_out), *ffn_tiles(gate, up, down)])


def by_block(g):
    return g.reshape(-1, P).T


def params_of(layout, parts):
    out = np.zeros((P, NPAR), np.float32)
    for name, value in parts.items():
        sl = layout[name]
        out[:value.shape[0], sl] = value
    return out


def diagonal_blocks(w):
    out = np.zeros((P, 2, P), np.float32)
    for g in range(4):
        o = 64 * (g % 2)
        out[o:o + 64, g // 2, o:o + 64] = w[g]
    return out.reshape(P, 2 * P)


def kernel(**inputs):
    import concourse.bacc as bacc
    from concourse.bass_utils import run_bass_kernel_spmd

    a = {k: np.asarray(v) for k, v in inputs.items()}
    tiles, params = [], []
    for l in range(LAYERS):
        tiles.append(stream1(a["w_in"][l], a["w_q_up"][l], a["w_kv_up"][l], a["w_out"][l], a["w_gate"][l],
                             a["w_up"][l], a["w_down"][l]))
        b = a["b_spatial"][l].reshape(2, 2, 1, P)
        params.append(params_of(PAR1, {
            "g_in": by_block(a["g_mix_norm"][l]), "g_q": by_block(a["g_q_lat"][l]),
            "g_kv": by_block(a["g_kv_lat"][l]), "g_qh": a["g_q_head"][l][:, None],
            "g_kh": a["g_k_head"][l][:, None], "pool_scale": by_block(a["pool_scale"][l]),
            "g_out": np.concatenate([by_block(a[n][l]) for n in ("g_out_mla", "g_out_sgu", "g_out_pool")], 1),
            "g_ffn": by_block(a["g_ffn_norm"][l]), "g_sgu": np.broadcast_to(a["g_sgu_v"][l], (P, 256)),
            "w_sp": a["w_spatial"][l].transpose(2, 0, 1).reshape(P, 4 * P),
            "b_sp": np.broadcast_to(b, (2, 2, 64, P)).transpose(1, 2, 0, 3).reshape(P, 2 * P),
            "w_pool": diagonal_blocks(a["w_pool"][l])}))
    for l in range(LAYERS):
        p = {k[:-2]: v[l] for k, v in a.items() if k.endswith("_2") and k != "final_norm_g_2"}
        tiles.append(stream2(p["w_in"], p["cmp_w1_k"], p["cmp_w1_v"],
                             (p["w_br_hg"], p["w_br_gla"], p["w_br_nsa"]), p["w_out"], p["w_ffn_gate"],
                             p["w_ffn_up"], p["w_ffn_down"]))
        params.append(params_of(PAR2, {
            "g_in": by_block(p["norm1_g"]), "g_hg": by_block(p["hg_norm_g"]), "gla_b": by_block(p["gla_b"]),
            "g_gla": by_block(p["gla_norm_g"]), "g_ffn": by_block(p["norm2_g"]), "w_gla": p["gla_w2"],
            "pos_k": p["cmp_pos_k"].reshape(16, P).T, "pos_v": p["cmp_pos_v"].reshape(16, P).T,
            "w2_k": np.concatenate([p["cmp_w2_k"]] * 2, 1), "w2_v": p["cmp_w2_v"]}))
    arrays = {
        "xT": a["x"][0].T.reshape(ND, P, T).transpose(1, 0, 2).reshape(P, ND * T),
        "pos": np.broadcast_to(a["positions"].astype(np.int32), (P, T)),
        "wstream": np.concatenate(tiles), "params": np.stack(params),
        "const": constants(a["hg_lb_2"], a["final_norm_g_2"])}
    arrays = {k: np.ascontiguousarray(v) for k, v in arrays.items()}
    assert arrays["wstream"].shape[0] == ALL_TILES
    nc = bacc.Bacc("TRN2", target_bir_lowering=False, num_devices=1)
    args = [nc.dram_tensor(k, v.shape, mybir.dt.from_np(v.dtype), kind="ExternalInput").ap()
            for k, v in arrays.items()]
    out = nc.dram_tensor("outT", (P, ND * T), F32, kind="ExternalOutput").ap()
    build(nc, *args, out)
    r = run_bass_kernel_spmd(nc, [arrays], core_ids=[0])
    y = r.results[0]["outT"]
    return y.reshape(P, ND, T).transpose(1, 0, 2).reshape(D, T).T.reshape(1, T, D)
```
